# Optimizing a Trainium2 kernel written in Bass

```python
import math
import jax
import jax.numpy as jnp
from jax import lax
import numpy as np
import jax, jax.numpy as jnp

D_MODEL = 1024
BATCH = 1
SEQ = 512
DEPTH = 1

HEAD_DIM = 64
A_Q_HEADS = 8
A_KV_HEADS = 2
A_WINDOW = 128
B_GROUPS = ((128, 1), (512, 4), (2048, 16))
B_HEADS_PER_GROUP = 8
A_WIDTH = A_Q_HEADS * HEAD_DIM
B_WIDTH = B_HEADS_PER_GROUP * HEAD_DIM
N_BRANCHES = 2
N_BUCKETS = 32
MAX_DISTANCE = 1024
REL_HEADS = A_Q_HEADS + len(B_GROUPS) * B_HEADS_PER_GROUP
PROJ_SIZES = (A_WIDTH, A_KV_HEADS * HEAD_DIM, A_KV_HEADS * HEAD_DIM,
              len(B_GROUPS) * B_WIDTH, len(B_GROUPS) * B_WIDTH, len(B_GROUPS) * B_WIDTH,
              A_WIDTH, B_WIDTH, N_BRANCHES * D_MODEL)
IN_WIDTH = sum(PROJ_SIZES)
EPS = 1e-6
NEG_INF = -1e30


def rms_norm(x, gain):
    xf = x.astype(jnp.float32)
    y = xf * lax.rsqrt(jnp.mean(xf * xf, axis=-1, keepdims=True) + EPS)
    return (y * gain.astype(jnp.float32)).astype(x.dtype)

def t5_bucket(rel):
    half = N_BUCKETS // 2
    max_exact = half // 2
    ret = (rel > 0).astype(jnp.int32) * half
    n = jnp.abs(rel)
    nf = jnp.maximum(n, max_exact).astype(jnp.float32)
    large = max_exact + (jnp.log(nf / max_exact) / math.log(MAX_DISTANCE / max_exact)
                         * (half - max_exact)).astype(jnp.int32)
    large = jnp.minimum(large, half - 1)
    return ret + jnp.where(n < max_exact, n, large)

def banded_attention(q, k, v, half_window, stride, bias_table, sink):
    bsz, L, H, dh = q.shape
    KV = k.shape[2]
    G = H // KV
    blk = half_window
    nb = -(-L // blk)
    Lp = nb * blk
    pad = Lp - L
    qb = jnp.pad(q, ((0, 0), (0, pad), (0, 0), (0, 0))).reshape(bsz, nb, blk, KV, G, dh)

    def windows(t):
        tp = jnp.pad(t, ((0, 0), (blk, blk + pad), (0, 0), (0, 0))).reshape(bsz, nb + 2, blk, KV, dh)
        return jnp.concatenate([tp[:, :-2], tp[:, 1:-1], tp[:, 2:]], axis=2)

    kw = windows(k)
    vw = windows(v)
    scores = jnp.einsum('bnqkgd,bnmkd->bkgnqm', qb, kw).astype(jnp.float32)

    qi = jnp.arange(blk)
    mi = jnp.arange(3 * blk)
    rel = mi[None, :] - blk - qi[:, None]
    bias = bias_table[t5_bucket(rel * stride)]
    bias = bias.transpose(2, 0, 1).reshape(KV, G, 1, blk, 3 * blk).astype(jnp.float32)
    blocks = jnp.arange(nb)[:, None, None] * blk
    qpos = blocks + qi[None, :, None]
    kpos = blocks - blk + mi[None, None, :]
    valid = (kpos >= 0) & (kpos < L) & (jnp.abs(kpos - qpos) <= half_window)

    logits = jnp.where(valid, scores + bias, NEG_INF)
    lse = jax.nn.logsumexp(logits, axis=-1)
    if sink is not None:
        lse = jnp.logaddexp(lse, sink.astype(jnp.float32).reshape(KV, G, 1, 1))
    probs = jnp.exp(logits - lse[..., None])
    out = jnp.einsum('bkgnqm,bnmkd->bnqkgd', probs.astype(v.dtype), vw)
    out = out.reshape(bsz, Lp, H, dh)[:, :L]
    lse = lse.transpose(0, 3, 4, 1, 2).reshape(bsz, Lp, H)[:, :L]
    return out, lse

def dilated_group(q, k, v, window, dilation, bias_table):
    bsz, S, H, dh = q.shape
    L = S // dilation

    def to_sub(t):
        return t.reshape(bsz, L, dilation, H, dh).transpose(0, 2, 1, 3, 4).reshape(bsz * dilation, L, H, dh)

    out, lse = banded_attention(to_sub(q), to_sub(k), to_sub(v), window // (2 * dilation),
                                dilation, bias_table, None)
    out = out.reshape(bsz, dilation, L, H, dh).transpose(0, 2, 1, 3, 4).reshape(bsz, S, H, dh)
    lse = lse.reshape(bsz, dilation, L, H).transpose(0, 2, 1, 3).reshape(bsz, S, H)
    return out, lse

def head_rms_norm(t, gain):
    return rms_norm(t, gain)

def first_inputs(seed: int = 0) -> dict:
    key = jax.random.key(seed)
    ks = jax.random.split(key, 16)
    f32 = jnp.float32
    x = jax.random.normal(ks[0], (BATCH, SEQ, D_MODEL), f32)
    norm_gain = 1.0 + 0.02 * jax.random.normal(ks[1], (DEPTH, D_MODEL), f32)
    w_in = jax.random.normal(ks[2], (DEPTH, D_MODEL, IN_WIDTH), f32) * D_MODEL ** -0.5
    q_norm_a = 1.0 + 0.02 * jax.random.normal(ks[3], (DEPTH, HEAD_DIM), f32)
    k_norm_a = 1.0 + 0.02 * jax.random.normal(ks[4], (DEPTH, HEAD_DIM), f32)
    q_norm_b = 1.0 + 0.02 * jax.random.normal(ks[5], (DEPTH, HEAD_DIM), f32)
    k_norm_b = 1.0 + 0.02 * jax.random.normal(ks[6], (DEPTH, HEAD_DIM), f32)
    sink_a = 0.5 * jax.random.normal(ks[7], (DEPTH, A_Q_HEADS), f32)
    rel_bias = 0.5 * jax.random.normal(ks[8], (N_BUCKETS, REL_HEADS), f32)
    w_branch_a = jax.random.normal(ks[9], (DEPTH, A_WIDTH, D_MODEL), f32) * A_WIDTH ** -0.5
    w_branch_b = jax.random.normal(ks[10], (DEPTH, B_WIDTH, D_MODEL), f32) * B_WIDTH ** -0.5
    b_merge = 0.1 * jax.random.normal(ks[11], (DEPTH, N_BRANCHES, D_MODEL), f32)
    w_out = jax.random.normal(ks[12], (DEPTH, D_MODEL, D_MODEL), f32) * D_MODEL ** -0.5
    return {"x": x, "norm_gain": norm_gain, "w_in": w_in, "q_norm_a": q_norm_a,
            "k_norm_a": k_norm_a, "q_norm_b": q_norm_b, "k_norm_b": k_norm_b,
            "sink_a": sink_a, "rel_bias": rel_bias, "w_branch_a": w_branch_a,
            "w_branch_b": w_branch_b, "b_merge": b_merge, "w_out": w_out}

def first_block(x, norm_gain, w_in, q_norm_a, k_norm_a, q_norm_b, k_norm_b, sink_a,
              rel_bias, w_branch_a, w_branch_b, b_merge, w_out):
    bsz, S, D = x.shape
    n_groups = len(B_GROUPS)
    scale = HEAD_DIM ** -0.5
    split_idx = [int(i) for i in np.cumsum(PROJ_SIZES)[:-1]]
    for layer in range(DEPTH):
        h = rms_norm(x, norm_gain[layer])
        proj = h @ w_in[layer]
        qa, ka, va, qb, kb, vb, ga, gb, mg = jnp.split(proj, split_idx, axis=-1)

        qa = head_rms_norm(qa.reshape(bsz, S, A_Q_HEADS, HEAD_DIM), q_norm_a[layer]) * scale
        ka = head_rms_norm(ka.reshape(bsz, S, A_KV_HEADS, HEAD_DIM), k_norm_a[layer])
        va = va.reshape(bsz, S, A_KV_HEADS, HEAD_DIM)
        ya, _ = banded_attention(qa, ka, va, A_WINDOW, 1, rel_bias[:, :A_Q_HEADS], sink_a[layer])
        ya = ya.reshape(bsz, S, A_WIDTH) * jax.nn.silu(ga)

        qb = head_rms_norm(qb.reshape(bsz, S, n_groups, B_HEADS_PER_GROUP, HEAD_DIM), q_norm_b[layer]) * scale
        kb = head_rms_norm(kb.reshape(bsz, S, n_groups, B_HEADS_PER_GROUP, HEAD_DIM), k_norm_b[layer])
        vb = vb.reshape(bsz, S, n_groups, B_HEADS_PER_GROUP, HEAD_DIM)
        outs = []
        lses = []
        for g, (window, dilation) in enumerate(B_GROUPS):
            c0 = A_Q_HEADS + g * B_HEADS_PER_GROUP
            o, l = dilated_group(qb[:, :, g], kb[:, :, g], vb[:, :, g], window, dilation,
                                 rel_bias[:, c0:c0 + B_HEADS_PER_GROUP])
            outs.append(o)
            lses.append(l)
        alpha = jax.nn.softmax(jnp.stack(lses, axis=0), axis=0)
        yb = jnp.sum(alpha[..., None].astype(x.dtype) * jnp.stack(outs, axis=0), axis=0)
        yb = yb.reshape(bsz, S, B_WIDTH) * jax.nn.silu(gb)

        br_a = ya @ w_branch_a[layer]
        br_b = yb @ w_branch_b[layer]
        gates = jax.nn.sigmoid(mg.reshape(bsz, S, N_BRANCHES, D).astype(jnp.float32)
                               + b_merge[layer].astype(jnp.float32)).astype(x.dtype)
        merged = gates[:, :, 0] * br_a + gates[:, :, 1] * br_b
        x = x + merged @ w_out[layer]
    return x


DEPTH_2 = 2

D_MIX = D_MODEL
A_HEADS = 4
A_WIDTH_2 = A_HEADS * HEAD_DIM
A_CHUNK = 128
B_HEADS = 8
B_DK = 64
B_DV = 64
B_WIDTH_2 = B_HEADS * B_DV
B_CONV = 4
B_CHUNK = 64
C_HEADS = 4
C_DK = 32
C_DV = 64
C_KEY = C_HEADS * C_DK
C_WIDTH = C_HEADS * C_DV
C_RANK = 16
C_TAU = 16.0
C_CHUNK = 64
D_FF = 2816
ALPHA = (2.0 * DEPTH_2) ** 0.25
BETA_INIT = (8.0 * DEPTH_2) ** -0.25
EPS_2 = 1e-5
SPLITS = (A_WIDTH_2, A_WIDTH_2,
          3 * B_WIDTH_2, B_WIDTH_2, B_HEADS, B_HEADS,
          C_KEY, C_KEY, C_WIDTH, C_WIDTH, C_RANK)
D_IN = sum(SPLITS)


def layer_norm(x, g, b):
    xf = x.astype(jnp.float32)
    mu = jnp.mean(xf, -1, keepdims=True)
    var = jnp.mean(jnp.square(xf - mu), -1, keepdims=True)
    return ((xf - mu) * lax.rsqrt(var + EPS_2) * g + b).astype(x.dtype)

def rms_norm_2(x, g):
    xf = x.astype(jnp.float32)
    return (xf * lax.rsqrt(jnp.mean(xf * xf, -1, keepdims=True) + EPS_2) * g).astype(x.dtype)

def l2_norm(x):
    xf = x.astype(jnp.float32)
    return (xf * lax.rsqrt(jnp.sum(xf * xf, -1, keepdims=True) + 1e-6)).astype(x.dtype)

def swiglu_half(x, w1, w3, w2):
    return 0.5 * ((jax.nn.silu(x @ w1) * (x @ w3)) @ w2)

def to_chunks(x, c):
    b_, t, h, d = x.shape
    return x.reshape(b_, t // c, c, h, d).transpose(0, 3, 1, 2, 4)

def gates_to_chunks(x, c):
    b_, t, h = x.shape
    return x.reshape(b_, t // c, c, h).transpose(0, 3, 1, 2)

def from_chunks(x):
    b_, h, n, c, d = x.shape
    return x.transpose(0, 2, 3, 1, 4).reshape(b_, n * c, h, d)

def causal_short_conv(x, w):
    k = w.shape[0]
    t = x.shape[1]
    xp = jnp.pad(x, ((0, 0), (k - 1, 0), (0, 0)))
    y = w[0] * xp[:, 0:t]
    for i in range(1, k):
        y = y + w[i] * xp[:, i:i + t]
    return y

def spatial_gating(u, v, ln_g, ln_b, w_s, b_s):
    b_, t, _ = v.shape
    n = t // A_CHUNK
    v = layer_norm(v, ln_g, ln_b).reshape(b_, n, A_CHUNK, A_HEADS, HEAD_DIM)
    mask = jnp.tril(jnp.ones((A_CHUNK, A_CHUNK), dtype=bool))
    w = jnp.where(mask, w_s, 0.0)
    z = jnp.einsum('hij,bnjhd->bnihd', w, v) + b_s.T[:, :, None]
    return u * z.reshape(b_, t, A_WIDTH_2)

def gated_delta_rule(q, k, v, log_g, beta):
    out_dtype = v.dtype
    q, k, v, log_g, beta = (t_.astype(jnp.float32) for t_ in (q, k, v, log_g, beta))
    c = q.shape[3]
    b_, h, _, _, dk = q.shape
    dv = v.shape[-1]
    incl = jnp.tril(jnp.ones((c, c), dtype=bool))
    strict = jnp.tril(jnp.ones((c, c), dtype=bool), -1)
    gam = jnp.cumsum(log_g, axis=-1)
    decay = jnp.exp(jnp.where(incl, gam[..., :, None] - gam[..., None, :], -jnp.inf))
    kk = jnp.einsum('bhnid,bhnjd->bhnij', k, k)
    lower = jnp.where(strict, beta[..., :, None] * kk * decay, 0.0)
    eye = jnp.eye(c, dtype=jnp.float32)
    rhs = jnp.concatenate([beta[..., None] * v, (beta * jnp.exp(gam))[..., None] * k], axis=-1)
    sol = lax.linalg.triangular_solve(eye + lower, rhs, left_side=True, lower=True, unit_diagonal=True)
    u_base, w_state = sol[..., :dv], sol[..., dv:]
    p_intra = jnp.einsum('bhnid,bhnjd->bhnij', q, k) * decay
    q_dec = q * jnp.exp(gam)[..., None]
    k_dec = k * jnp.exp(gam[..., -1:] - gam)[..., None]
    g_tot = jnp.exp(gam[..., -1])

    def step(s, inp):
        u_b, w_c, p_c, qd, kd, gt = inp
        u = u_b - jnp.einsum('bhck,bhkv->bhcv', w_c, s)
        o = jnp.einsum('bhck,bhkv->bhcv', qd, s) + jnp.einsum('bhij,bhjv->bhiv', p_c, u)
        s = gt[..., None, None] * s + jnp.einsum('bhck,bhcv->bhkv', kd, u)
        return s, o

    s0 = jnp.zeros((b_, h, dk, dv), jnp.float32)
    xs = tuple(jnp.moveaxis(t_, 2, 0) for t_ in (u_base, w_state, p_intra, q_dec, k_dec, g_tot))
    _, o = lax.scan(step, s0, xs)
    return jnp.moveaxis(o, 0, 2).astype(out_dtype)

def gated_deltanet(qkv, z, beta_logit, decay_logit, conv_w, a_log, dt_bias, norm_g):
    b_, t, _ = qkv.shape
    qkv = jax.nn.silu(causal_short_conv(qkv, conv_w))
    q, k, v = jnp.split(qkv, 3, axis=-1)
    q = l2_norm(q.reshape(b_, t, B_HEADS, B_DK)) * (B_DK ** -0.5)
    k = l2_norm(k.reshape(b_, t, B_HEADS, B_DK))
    v = v.reshape(b_, t, B_HEADS, B_DV)
    beta = jax.nn.sigmoid(beta_logit.astype(jnp.float32))
    log_g = -jnp.exp(a_log) * jax.nn.softplus(decay_logit.astype(jnp.float32) + dt_bias)
    o = gated_delta_rule(to_chunks(q, B_CHUNK), to_chunks(k, B_CHUNK), to_chunks(v, B_CHUNK),
                         gates_to_chunks(log_g, B_CHUNK), gates_to_chunks(beta, B_CHUNK))
    o = from_chunks(o)
    o = rms_norm_2(o, norm_g) * jax.nn.silu(z.reshape(b_, t, B_HEADS, B_DV))
    return o.reshape(b_, t, B_WIDTH_2)

def gla_chunked(q, k, v, log_a):
    out_dtype = v.dtype
    q, k, v, log_a = (t_.astype(jnp.float32) for t_ in (q, k, v, log_a))
    c = q.shape[3]
    b_, h, _, _, dk = q.shape
    dv = v.shape[-1]
    incl = jnp.tril(jnp.ones((c, c), dtype=bool))
    bcum = jnp.cumsum(log_a, axis=3)
    q_dec = q * jnp.exp(bcum)
    p_intra = jnp.where(incl, jnp.einsum('bhnid,bhnjd->bhnij', q_dec, k * jnp.exp(-bcum)), 0.0)
    o_intra = jnp.einsum('bhnij,bhnjv->bhniv', p_intra, v)
    k_dec = k * jnp.exp(bcum[..., -1:, :] - bcum)
    g_tot = jnp.exp(bcum[..., -1, :])

    def step(s, inp):
        o_i, qd, kd, vc, gt = inp
        o = o_i + jnp.einsum('bhck,bhkv->bhcv', qd, s)
        s = gt[..., :, None] * s + jnp.einsum('bhck,bhcv->bhkv', kd, vc)
        return s, o

    s0 = jnp.zeros((b_, h, dk, dv), jnp.float32)
    xs = tuple(jnp.moveaxis(t_, 2, 0) for t_ in (o_intra, q_dec, k_dec, v, g_tot))
    _, o = lax.scan(step, s0, xs)
    return jnp.moveaxis(o, 0, 2).astype(out_dtype)

def gla(q, k, v, r, g_low, gate_up, gate_b, norm_g):
    b_, t, _ = q.shape
    log_a = jax.nn.log_sigmoid((g_low @ gate_up + gate_b).astype(jnp.float32)) / C_TAU
    q = q.reshape(b_, t, C_HEADS, C_DK) * (C_DK ** -0.5)
    k = k.reshape(b_, t, C_HEADS, C_DK)
    v = v.reshape(b_, t, C_HEADS, C_DV)
    log_a = log_a.reshape(b_, t, C_HEADS, C_DK)
    o = gla_chunked(to_chunks(q, C_CHUNK), to_chunks(k, C_CHUNK), to_chunks(v, C_CHUNK),
                    to_chunks(log_a, C_CHUNK))
    o = rms_norm_2(from_chunks(o), norm_g) * jax.nn.silu(r.reshape(b_, t, C_HEADS, C_DV))
    return o.reshape(b_, t, C_WIDTH)

def second_inputs(seed: int = 0) -> dict:
    key = jax.random.key(seed)
    ks = jax.random.split(key, 40)
    L = DEPTH_2
    f32 = jnp.float32

    def nrm(i, shape, scale):
        return jax.random.normal(ks[i], shape, f32) * scale

    def gain(i, shape):
        return 1.0 + 0.1 * jax.random.normal(ks[i], shape, f32)

    a_val = jax.random.uniform(ks[17], (L, B_HEADS), f32, 1.0, 16.0)
    dt = jnp.exp(jax.random.uniform(ks[18], (L, B_HEADS), f32, np.log(1e-3), np.log(1e-1)))
    return {
        "x": jax.random.normal(ks[0], (BATCH, SEQ, D_MODEL), f32),
        "ffn1_w1": nrm(1, (L, D_MODEL, D_FF), D_MODEL ** -0.5),
        "ffn1_w3": nrm(2, (L, D_MODEL, D_FF), D_MODEL ** -0.5),
        "ffn1_w2": nrm(3, (L, D_FF, D_MODEL), BETA_INIT * D_FF ** -0.5),
        "ln1_g": gain(4, (L, D_MODEL)),
        "ln1_b": nrm(5, (L, D_MODEL), 0.02),
        "w_in": nrm(6, (L, D_MODEL, D_IN), D_MODEL ** -0.5),
        "sgu_ln_g": gain(7, (L, A_WIDTH_2)),
        "sgu_ln_b": nrm(8, (L, A_WIDTH_2), 0.02),
        "sgu_w": nrm(9, (L, A_HEADS, A_CHUNK, A_CHUNK), 0.5 * A_CHUNK ** -0.5),
        "sgu_b": gain(10, (L, A_HEADS, A_CHUNK)),
        "gdn_conv_w": nrm(11, (L, B_CONV, 3 * B_WIDTH_2), 0.5),
        "gdn_a_log": jnp.log(a_val),
        "gdn_dt_bias": dt + jnp.log(-jnp.expm1(-dt)),
        "gdn_norm_g": gain(12, (L, B_DV)),
        "gla_gate_up": nrm(13, (L, C_RANK, C_KEY), C_RANK ** -0.5),
        "gla_gate_b": nrm(14, (L, C_KEY), 0.1),
        "gla_norm_g": gain(15, (L, C_DV)),
        "w_out": nrm(16, (L, D_MIX, D_MODEL), BETA_INIT * D_MIX ** -0.5),
        "ln2_g": gain(19, (L, D_MODEL)),
        "ln2_b": nrm(20, (L, D_MODEL), 0.02),
        "ffn2_w1": nrm(21, (L, D_MODEL, D_FF), D_MODEL ** -0.5),
        "ffn2_w3": nrm(22, (L, D_MODEL, D_FF), D_MODEL ** -0.5),
        "ffn2_w2": nrm(23, (L, D_FF, D_MODEL), BETA_INIT * D_FF ** -0.5),
        "ln3_g": gain(24, (L, D_MODEL)),
        "ln3_b": nrm(25, (L, D_MODEL), 0.02),
    }

def second_block(x, ffn1_w1, ffn1_w3, ffn1_w2, ln1_g, ln1_b, w_in, sgu_ln_g, sgu_ln_b, sgu_w, sgu_b,
              gdn_conv_w, gdn_a_log, gdn_dt_bias, gdn_norm_g, gla_gate_up, gla_gate_b, gla_norm_g,
              w_out, ln2_g, ln2_b, ffn2_w1, ffn2_w3, ffn2_w2, ln3_g, ln3_b):
    split_at = [int(s) for s in np.cumsum(SPLITS)[:-1]]
    for l in range(DEPTH_2):
        x = layer_norm(ALPHA * x + swiglu_half(x, ffn1_w1[l], ffn1_w3[l], ffn1_w2[l]), ln1_g[l], ln1_b[l])
        h = x @ w_in[l]
        (a_u, a_v, b_qkv, b_z, b_beta, b_decay,
         c_q, c_k, c_v, c_r, c_g) = jnp.split(h, split_at, axis=-1)
        out_a = spatial_gating(jax.nn.gelu(a_u), jax.nn.gelu(a_v), sgu_ln_g[l], sgu_ln_b[l], sgu_w[l], sgu_b[l])
        out_b = gated_deltanet(b_qkv, b_z, b_beta, b_decay, gdn_conv_w[l], gdn_a_log[l], gdn_dt_bias[l], gdn_norm_g[l])
        out_c = gla(c_q, c_k, c_v, c_r, c_g, gla_gate_up[l], gla_gate_b[l], gla_norm_g[l])
        mix = jnp.concatenate([out_a, out_b, out_c], axis=-1) @ w_out[l]
        x = layer_norm(ALPHA * x + mix, ln2_g[l], ln2_b[l])
        x = layer_norm(ALPHA * x + swiglu_half(x, ffn2_w1[l], ffn2_w3[l], ffn2_w2[l]), ln3_g[l], ln3_b[l])
    return x


def setup_inputs(seed=0):
    out = dict(first_inputs(seed))
    for name, value in second_inputs(seed + 1).items():
        if name != "x":
            out[name + "_2"] = value
    return out


def reference(
    x, norm_gain, w_in, q_norm_a, k_norm_a, q_norm_b, k_norm_b, sink_a, rel_bias, w_branch_a,
    w_branch_b, b_merge, w_out, ffn1_w1_2, ffn1_w3_2, ffn1_w2_2, ln1_g_2, ln1_b_2, w_in_2,
    sgu_ln_g_2, sgu_ln_b_2, sgu_w_2, sgu_b_2, gdn_conv_w_2, gdn_a_log_2, gdn_dt_bias_2,
    gdn_norm_g_2, gla_gate_up_2, gla_gate_b_2, gla_norm_g_2, w_out_2, ln2_g_2, ln2_b_2,
    ffn2_w1_2, ffn2_w3_2, ffn2_w2_2, ln3_g_2, ln3_b_2,
):
    x = first_block(
        x, norm_gain, w_in, q_norm_a, k_norm_a, q_norm_b, k_norm_b, sink_a, rel_bias,
        w_branch_a, w_branch_b, b_merge, w_out,
    )
    return second_block(
        x, ffn1_w1_2, ffn1_w3_2, ffn1_w2_2, ln1_g_2, ln1_b_2, w_in_2, sgu_ln_g_2, sgu_ln_b_2,
        sgu_w_2, sgu_b_2, gdn_conv_w_2, gdn_a_log_2, gdn_dt_bias_2, gdn_norm_g_2, gla_gate_up_2,
        gla_gate_b_2, gla_norm_g_2, w_out_2, ln2_g_2, ln2_b_2, ffn2_w1_2, ffn2_w3_2, ffn2_w2_2,
        ln3_g_2, ln3_b_2,
    )


_drawn_inputs = setup_inputs


def setup_inputs(seed=0):
    import zlib

    import numpy as np

    out = dict(_drawn_inputs(seed))
    spreads = {}
    factors = {'norm_gain': 8.0,
     'q_norm_a': 8.0,
     'k_norm_a': 8.0,
     'q_norm_b': 8.0,
     'k_norm_b': 8.0,
     'sink_a': 8.0,
     'b_merge': 8.0,
     'sgu_ln_g_2': 8.0,
     'sgu_ln_b_2': 58.326,
     'sgu_b_2': 3.52,
     'gdn_norm_g_2': 2.719,
     'gla_gate_up_2': 3.661,
     'gla_gate_b_2': 8.0,
     'gla_norm_g_2': 5.053}
    for name, (base, spread) in spreads.items():
        noise = np.random.default_rng([zlib.crc32(name.encode()), seed]).standard_normal(out[name].shape)
        drawn = base * np.exp(spread * noise) if base else spread * noise
        out[name] = jnp.asarray(drawn.astype(out[name].dtype))
    for name, factor in factors.items():
        out[name] = (out[name] * factor).astype(out[name].dtype)
    return out
```

```python
from contextlib import ExitStack

import numpy as np
import concourse.bass as bass
from concourse import mybir

F32 = mybir.dt.float32
F32R = mybir.dt.float32r
ALU = mybir.AluOpType
ACT = mybir.ActivationFunctionType
AXX = mybir.AxisListType.X

P = 128
TOK = 512
D = 1024
KT = D // P
DFF = 2816
FT = DFF // P
LAYERS = 2
ALPHA = (2.0 * LAYERS) ** 0.25
EPS2 = 1e-5
EPS_L2 = 1e-6
CH = 64
NCH = TOK // CH
PAIRS = 4

UP = 2 * FT // 2
DOWN = 2 * KT
INP = 14
OUTP = KT // 2
PER = 2 * UP + 2 * DOWN + INP + OUTP
OFF_UP1, OFF_DN1 = 0, UP
OFF_IN = UP + DOWN
OFF_OUT = OFF_IN + INP
OFF_UP2 = OFF_OUT + OUTP
OFF_DN2 = OFF_UP2 + UP

K1 = 1024

VIEW = (1, 1, 4, 4)
HALF = (128, 64, 64, 64)
WIDE = (True, True, False, False)
ORDER = (0, 2, 1, 3)
KINDS = {0: ("q0", "q1", "k0", "v0")} | {g: ("q0", "q1", "k0", "k1", "v0", "v1") for g in (1, 2, 3)}
VW = (128, 256, 256, 256)
BASE = 4 + 18 + 4 + 12 + 4
P1_QN, P1_SINK, P1_BM = 8, 12, 16


def buckets(rel):
    half, exact, far = 16, 8, 1024
    n = np.abs(rel)
    nf = np.maximum(n, exact).astype(np.float32)
    large = exact + (np.log(nf / np.float32(exact)) / np.float32(np.log(far / exact)) * np.float32(half - exact)).astype(np.int32)
    return (rel > 0) * half + np.where(n < exact, n, np.minimum(large, half - 1))


def bias_constants():
    out = np.zeros((P, 1024 + 2048), np.float32)
    r = np.arange(512)
    for t, (stride, mid) in enumerate(((1, 255), (4, 127))):
        out[buckets((r - mid) * stride), 512 * t + r] = 1
    for g, (mid, step) in enumerate(((255, 1), (255, 1), (127, 1), (127, 4))):
        near = ((r - mid) % step == 0) & (np.abs(r - mid) <= HALF[g] * step)
        out[0:8, 1024 + 512 * g:1536 + 512 * g] = np.where(near, 0.0, 1e30)
    return out


def const_columns():
    at, parts = {}, []
    n = 0

    def put(name, a):
        nonlocal n
        a = np.asarray(a, np.float32).reshape(P, -1)
        at[name] = (n, a.shape[1])
        parts.append(a)
        n += a.shape[1]

    r = np.arange(P)
    put("ident", np.eye(P))
    put("head_mean", (r[:, None] // 64 == r[None, :] // 64) / 64.0)
    put("feat_mean", np.full((P, P), 1.0 / D))
    i, j = r[:, None] % CH, np.arange(CH)[None, :]
    put("eye64", i == j)
    put("upper64", i <= j)
    put("strict64", i < j)
    put("low1", (i == j + 1) & (j % 2 == 0))
    put("upT1", (j == i + 1) & (i % 2 == 0))
    for s in (2, 4, 8, 16, 32):
        put(f"upT{s}", ((i // s) % 2 == 0) & (j // s == i // s + 1))
    put("upper128", r[:, None] <= r[None, :])
    put("keep", np.tile((np.arange(TOK) % CH != 0)[None, :], (P, 1)))
    sel = np.zeros((P, PAIRS, P))
    for base in (0, 32):
        for h in range(8):
            sel[base + h, h // 2, 64 * (h % 2):64 * (h % 2) + 64] = 1
    put("sel", sel)
    seln = np.zeros((P, 2, PAIRS))
    for base in (0, 32):
        for h in range(8):
            seln[base + h, h % 2, h // 2] = 1
    put("seln", seln)
    return at, np.concatenate(parts, 1)


CONST_AT, CONSTS = const_columns()
NC = CONSTS.shape[1]
PK_LN, PK_CONV, PK_GN, PK_LAN, PK_ALOG, PK_DT, PK_GB, PK_UP = 0, 48, 96, 97, 98, 99, 100, 104
NPK = 232
SG_G, SG_B, SG_BS, SG_W = 0, 256, 512, 768
NSG = 1280


def at(l, per, n):
    return n if l is None else l * per + n


SIGNALS = """
apart_pe apart_dve apart_pool
c_in x_in xh0 par_in sgp_in eps hi_done lo_done used x_ready h_hi h_lo z_sum
ln_mean ln_zc ln_sq ln_var ln_std ln_rs ln_t ln_x ln_h conv_a conv_d conv_s
hn_sq hn_ps hn_std hn_rc hn_d ga_ps ga_ps2 ga_act ga_act2 ga_dve ga_pA ga_o gt_act gt_dve
sg_pool sg_ps sg_act sg_dve mixA mixB mixC mix_hi mix_lo tok_ps tok_sb col_ps col_sb
b_rel b_par b_far b_hh b_hl b_row b_scr b_bw b_b1 b_b2 b_x2 b_ms b_xs b_xr b_h b_c b_rp b_sq b_hm b_sd b_rc b_q
at_s at_l at_p at_t at_e at_v at_o st_ps st_a st_d st_e st_f y_w y_s y_h y_l y_ps y_d mg_h mg_l mg_a mg_d x1_h c2_in
dp_ps dp_dve dp_act dp_pool kv_act kv_dve lv_x lv_t lv_act lv_dve lv_pool wu_ps wu_sb
rc_st rc_u rc_un rc_ds rc_o rc_ov rc_sg tr_ps tr_sb stored
"""


def program(nc, stream, pk, sg, consts, consts2, rel, p1, x_in, out):
    base = BASE
    with ExitStack() as ctx:
        scr_t = nc.dram_tensor("bias_rows", (4, P, 8, 512), F32)
        scr = scr_t.ap()
        used_sems = {}

        def sem(name):
            used_sems[name] = ctx.enter_context(nc.semaphore(name))
            return used_sems[name]

        def sb(name, kb, shape, dt=F32):
            return nc.alloc_sbuf_tensor_at(name, shape, dt, offset=OFS + int(kb * K1))

        OFS = (nc.sbuf_base + 31) // 32 * 32
        raw = sb("raw", 0, [P, 2, 2048])
        wh = sb("wh", 16, [P, 2, 2048], F32R)
        wl = sb("wl", 32, [P, 2, 2048], F32R)
        x = sb("x", 48, [P, KT, TOK])
        xh = sb("xh", 64, [P, KT, TOK], F32R)
        xl = sb("xl", 80, [P, KT, TOK], F32R)
        hh = sb("hh", 96, [P, FT, TOK], F32R)
        hl = sb("hl", 140, [P, FT, TOK], F32R)
        sg_t = sb("sg_t", 184, [P, 2, TOK])
        hf = sb("hf", 188, [P, 2, TOK])
        zacc = sb("zacc", 184, [P, TOK])
        mean = sb("mean", 186, [P, TOK])
        sq = sb("sq", 188, [P, 2, TOK])
        rstd = sb("rstd", 192, [P, TOK])
        std = sb("std", 194, [P, TOK])
        cst = sb("cst", 196, [P, NC])
        pkt = sb("pkt", 196 + NC * 4 / K1 + 0.03125, [P, NPK])

        qkv = sb("qkv", 96, [P, 12, TOK])
        qT, kT, vT = qkv[:, 0:4, :], qkv[:, 4:8, :], qkv[:, 8:12, :]
        kN = sb("kN", 120, [P, PAIRS, NCH, CH])
        vN = sb("vN", 128, [P, PAIRS, NCH, CH])
        pT = sb("pT", 136, [P, PAIRS, NCH, CH])
        LT = sb("LT", 144, [P, PAIRS, NCH, CH])
        Tm = sb("Tm", 152, [P, PAIRS, NCH, CH])
        TT = sb("TT", 160, [P, PAIRS, NCH, CH])
        tmp = sb("tmp", 168, [P, 6, TOK])
        zs = sb("zs", 180, [P, PAIRS, TOK])
        rows = sb("rows", 188, [P, TOK])
        gam = sb("gam", 190, [P, TOK])
        gN = sb("gN", 192, [P, NCH, PAIRS])
        bN = sb("bN", 192.125, [P, NCH, PAIRS])
        bgN = sb("bgN", 192.25, [P, NCH, PAIRS])
        kdN = sb("kdN", 192.375, [P, NCH, PAIRS])
        glast = sb("glast", 192.5, [P, NCH, PAIRS])
        gtot = sb("gtot", 192.625, [P, NCH, PAIRS])
        egN = sb("egN", 192.75, [P, NCH, PAIRS])
        nega = sb("nega", 192.875, [P, 8])
        state = sb("state", 193, [P, 2, PAIRS, CH])
        unew = sb("unew", 195, [P, PAIRS, CH])
        au = sb("au", 144, [P, 2, TOK])
        av = sb("av", 148, [P, 4, 256])
        cqk = sb("cqk", 152, [P, 2, TOK])
        cr = sb("cr", 156, [P, 2, TOK])
        cv = sb("cv", 160, [P, 4, 256])
        sgp = sb("sgp", 136, [P, NSG])
        bcum = sb("bcum", 164, [P, TOK])
        la = sb("la", 166, [P, TOK])
        pA = sb("pA", 120, [P, 4, 4, CH])
        kdA = sb("kdA", 124, [P, 4, P])
        stA = sb("stA", 126, [P, NCH, CH])
        oA = sb("oA", 128, [P, 2, TOK])
        stat = sb("stat", 132, [P, 4, 6])
        mv = sb("mv", 132.125, [P, 4, 2])
        sgt = sb("sgt", 132.25, [P, 4])
        gtA = sb("gtA", 132.5, [P, NCH])
        cols = sb("cols", 206.25, [P, 8])
        ps = nc.alloc_psum_tensor("ps", [P, 8, TOK], F32)

        Xb = qkv[:, 8:12, :].rearrange("p a (c t) -> p a c t", t=CH)
        oT = qkv[:, 8:12, :]
        bk = qkv[:, 4:8, :].rearrange("p a (c t) -> p a c t", t=CH)
        nwT, ub = Tm, LT
        sgw = sgp[:, SG_W:SG_W + 512].rearrange("p (h i) -> p h i", i=P)
        qg = sb("qg", 96, [P, 4, TOK])
        kg = sb("kg", 104, [P, 4, TOK])
        vg = sb("vg", 112, [P, 4, TOK])
        btw = sb("btw", 120, [P, 8, 384])
        og = sb("og", 132, [P, 4, 4, TOK])
        lg = sb("lg", 164, [P, 2, 384])
        pb = sb("pb", 167, [P, 3, 384])
        pt = sb("pt", 171.5, [P, 2, 384])
        nmc = sb("nmc", 174.5, [P, 4, 32])
        lc = sb("lc", 175, [P, 4, 32])
        bsq = sb("bsq", 175.5, [P, 6, TOK])
        bt1 = sb("bt1", 187.5, [P, 8, P])
        bt2 = sb("bt2", 191.5, [P, 8, P])
        pk1 = sb("pk1", 206.5, [P, 32])
        c2 = sb("c2", 132, [P, 1024 + 2048])
        brow = sb("brow", 146, [P, 4, TOK])
        relb = sb("relb", 154, [P, 32])
        hb = sb("hb", 155, [P, 4, TOK])
        rw = sb("rw", 96, [P, 12, TOK])
        sgl = sb("sgl", 120, [P, 2, TOK])
        zg = sb("zg", 124, [P, 4, TOK])
        yh = sb("yh", 164, [P, 8, TOK], F32R)
        yl = sb("yl", 180, [P, 8, TOK], F32R)
        mt = sb("mt", 96, [P, 3, 2, TOK])
        mh = sb("mh", 132, [P, 8, TOK], F32R)
        ml = sb("ml", 148, [P, 8, TOK], F32R)

        def C(name, *shape):
            a, w = CONST_AT[name]
            v = cst[:, a:a + w]
            return v

        sel = C("sel").rearrange("p (a b) -> p a b", a=PAIRS)
        seln = C("seln").rearrange("p (a b) -> p a b", a=2)

        def bc(v, n=NCH):
            return v.unsqueeze(1).to_broadcast([P, n, v.shape[1]])

        def col(v):
            return v.unsqueeze(2).to_broadcast([P, v.shape[1], CH])

        def chunks(v):
            return v.rearrange("p (c t) -> p c t", t=CH)

        landed = [sem("landed0"), sem("landed1")]
        evac = [sem("evac0"), sem("evac1")]
        s = {name: sem(name) for name in SIGNALS.split()}
        block = ctx.enter_context(nc.Block())

        def n_evac(l, p, off):
            n = (min(off, OFF_DN1) + (max(off - OFF_IN, 0) if off <= OFF_DN2 else OFF_DN2 - OFF_IN)) // 2
            if p:
                n += max(min(off, OFF_IN) - OFF_DN1, 0) // 2 + max(off - OFF_DN2, 0) // 2
            return l * (E0_PER + p * 2 * KT) + BASE_E + n

        def c_no(l, off):
            return l * PER + base + off

        BASE_E = base // 2
        E0_PER = (OFF_DN1 + OFF_DN2 - OFF_IN) // 2
        N_CHUNKS = base + LAYERS * PER + 2

        def eps_col(name):
            k = ("eps_ln", "eps2", "eps_l2").index(name)
            return cols[:, k:k + 1]


        def in_products_pe(l, pe, chunk_t, chunk_n):
            for j in range(INP):
                pe.wait_ge(evac[j % 2], n_evac(l, j % 2, OFF_IN) + j // 2)
                if j in (1, 6):
                    chunk_n(l, OFF_IN, j, j % 2)
                else:
                    chunk_t(l, OFF_IN, j, j % 2, 128 if j == 7 else 256)

        def in_products_act(l, act, round_chunk):
            ac = nc.scalar
            into = {0: (au, ACT.Gelu_apprx_tanh), 1: (av, ACT.Gelu_apprx_tanh), 2: (zs[:, 0:2, :], ACT.Silu),
                    3: (zs[:, 2:4, :], ACT.Silu), 5: (cr, ACT.Silu)}
            for j in range(INP):
                p = j % 2
                n = c_no(l, OFF_IN) + j
                act.wait_ge(s["used"], n + 1)
                if j in into:
                    dst, fn = into[j]
                    if j == 1:
                        src = ps[:, 2:4, :].rearrange("p a (b c) -> p (a b) c", b=2)
                    else:
                        src = ps[:, 2 * p:2 * p + 2, :]
                    ac.activation(dst[:, :, :], src, fn).then_inc(evac[p], 1)
                if j >= 8:
                    q = j - 8
                    for k in range(2):
                        t = 2 * q + k
                        ac.activation(qkv[:, t, :], ps[:, 2 * p + k, :], ACT.Copy, scale=pkt[:, PK_CONV + 4 * t + 3:PK_CONV + 4 * t + 4]).then_inc(s["conv_a"], 1)
                round_chunk(n + 2, p)
                if j >= 9:
                    conv_silu(l, act, j - 9)
            conv_silu(l, act, 5)

        def conv_silu(l, act, q):
            act.wait_ge(evac[q % 2], n_evac(l, q % 2, OFF_IN) + (q + 8) // 2 + 1)
            nc.scalar.activation(qkv[:, 2 * q:2 * q + 2, :], qkv[:, 2 * q:2 * q + 2, :], ACT.Silu).then_inc(s["conv_s"], 1)

        def in_products_dve(l, dve, rest_chunk):
            ve = nc.vector
            for j in range(INP):
                p = j % 2
                n = c_no(l, OFF_IN) + j
                if j in (4, 6, 7):
                    dve.wait_ge(s["used"], n + 1)
                    if j == 4:
                        ve.tensor_copy(cqk[:, :, :], ps[:, 0:2, :]).then_inc(evac[p], 1)
                    if j == 6:
                        ve.tensor_copy(cv[:, :, :], ps[:, 0:2, :].rearrange("p a (b c) -> p (a b) c", b=2)).then_inc(evac[p], 1)
                    if j == 7:
                        ve.tensor_copy(rows[:, :], ps[:, 2, :]).then_inc(evac[p], 1)
                if j >= 8:
                    q = j - 8
                    m = 0
                    for tap in (2, 1, 0):
                        for k in range(2):
                            t = 2 * q + k
                            sh = 3 - tap
                            if tap == 2:
                                dve.wait_ge(s["conv_a"], l * 12 + 2 * q + k + 1)
                            else:
                                dve.wait_ge(s["conv_d"], l * 30 + 5 * q + m - 1)
                            y = qkv[:, t, sh:TOK]
                            m += 1
                            c = PK_CONV + 4 * t + tap
                            ve.scalar_tensor_tensor(out=y, in0=ps[:, 2 * p + k, 0:TOK - sh], scalar=pkt[:, c:c + 1], in1=y,
                                                    op0=ALU.mult, op1=ALU.add).then_inc(*((s["conv_d"], 1) if m < 6 else (evac[p], 1)))
                rest_chunk(n + 2, p)

        def heads_norm_act(act, tiles, n0, scale, eps, first=False):
            ac = nc.scalar
            for t in range(len(tiles) + 1):
                if t < len(tiles):
                    n = n0 + t
                    if t or not first:
                        act.wait_ge(s["hn_ps"], n - 1)
                    ac.activation(tmp[:, t % 2, :], tiles[t], ACT.Square).then_inc(s["hn_sq"], 1)
                if t:
                    n = n0 + t - 1
                    act.wait_ge(s["hn_ps"], n + 1)
                    if t > 1 or not first:
                        act.wait_ge(s["hn_rc"], n - 1)
                    ac.activation(tmp[:, 2 + (t - 1) % 2, :], ps[:, 6 + (t - 1) % 2, :], ACT.Sqrt, scale=scale, bias=eps).then_inc(s["hn_std"], 1)

        def heads_norm_pe(pe, n_tiles, n0, first=False):
            for t in range(n_tiles):
                n = n0 + t
                pe.wait_ge(s["hn_sq"], n + 1)
                if t or not first:
                    pe.wait_ge(s["hn_std"], n - 1)
                nc.tensor.matmul(ps[:, 6 + t % 2, :], C("head_mean"), tmp[:, t % 2, :], start=True, stop=True).then_inc(s["hn_ps"], 1)

        def heads_norm_dve(dve, tiles, factors, n0, then=None):
            for t in range(len(tiles)):
                n = n0 + t
                dve.wait_ge(s["hn_std"], n + 1)
                if t >= 2:
                    dve.wait_ge(s["hn_d"], n - 1)
                nc.vector.reciprocal(tmp[:, 4 + t % 2, :], tmp[:, 2 + t % 2, :]).then_inc(s["hn_rc"], 1)
                dve.wait_ge(s["hn_rc"], n + 1)
                nc.vector.scalar_tensor_tensor(out=tiles[t], in0=tiles[t], scalar=factors[t], in1=tmp[:, 4 + t % 2, :],
                                               op0=ALU.mult, op1=ALU.mult).then_inc(s["hn_d"], 1)
                if then:
                    dve.wait_ge(s["hn_d"], n + 1)
                    then(t)

        HN = 8 + 2 + 4 + 0

        def qk_tiles():
            return [qkv[:, t, :] for t in range(8)]

        def o_tiles():
            return [oT[:, pr, :] for pr in range(PAIRS)]

        def oA_tiles():
            return [oA[:, a, :] for a in range(2)]

        def mixer_pe(l, pe):
            te = nc.tensor
            hn = l * 14
            heads_norm_pe(pe, 8, hn, first=True)
            pe.wait_ge(evac[1], n_evac(l, 1, OFF_IN) + 4)
            te.matmul(ps[:, 4, :], pkt[64:80, PK_UP:PK_UP + P], rows[64:80, :], start=True, stop=True).then_inc(s["ga_ps"], 1)
            pe.wait_ge(s["sg_pool"], l * 3 + 3)
            for a in range(2):
                for t in range(4):
                    for b in range(2):
                        h = 2 * a + b
                        mm = te.matmul(ps[64 * b:64 * b + 64, 6 + a, t * P:(t + 1) * P], av[:, t, 64 * h:64 * h + 64],
                                       sgw[:, h, :], start=True, stop=True)
                mm.then_inc(s["sg_ps"], 1)
            pe.wait_ge(s["ga_dve"], l * 16 + 6)
            for c in range(NCH):
                for h in range(4):
                    mm = te.matmul(ps[64 * (c % 2):64 * (c % 2) + 64, h, (c // 2) * CH:(c // 2 + 1) * CH],
                                   tmp[32 * h:32 * h + 32, 1, c * CH:(c + 1) * CH],
                                   cqk[32 * h:32 * h + 32, 0, c * CH:(c + 1) * CH], start=True, stop=True)
            mm.then_inc(s["ga_ps2"], 1)
            pe.wait_ge(s["ga_dve"], l * 16 + 7)
            for t in range(4):
                mm = te.transpose(ps[:, 5, t * P:(t + 1) * P], cqk[:, 1, t * P:(t + 1) * P], C("ident"))
            mm.then_inc(s["ga_ps2"], 1)
            pe.wait_ge(s["ga_act2"], l * 1 + 1)
            pe.wait_ge(s["sg_dve"], l * 16 + 16)
            pe.sem_inc(s["apart_pe"], 1)
            for c in range(NCH):
                b, t = 64 * (c % 2), c // 2
                for h in range(4):
                    mm = te.matmul(ps[32 * h:32 * h + 32, 6 + c % 2, t * CH:(t + 1) * CH], kdA[b:b + 64, t, 32 * h:32 * h + 32],
                                   cv[b:b + 64, t, 64 * h:64 * h + 64], start=True, stop=True)
            mm.then_inc(s["ga_ps2"], 1)
            pe.wait_ge(s["ga_dve"], l * 16 + 16)
            for c in range(NCH):
                b, t = 64 * (c % 2), c // 2
                for h in range(4):
                    dst = ps[64 * (h % 2):64 * (h % 2) + 64, 2 * (h // 2) + c % 2, t * CH:(t + 1) * CH]
                    te.matmul(dst, stA[32 * h:32 * h + 32, c, :], cqk[32 * h:32 * h + 32, 0, c * CH:(c + 1) * CH], start=True, stop=False)
                    mm = te.matmul(dst, cv[b:b + 64, t, 64 * h:64 * h + 64], pA[b:b + 64, h, t, :], start=False, stop=True)
            mm.then_inc(s["ga_ps2"], 1)
            heads_norm_pe(pe, 2, hn + 8)

            pe.wait_ge(s["hn_std"], l * 14 + 10)
            pe.sem_inc(s["apart_pe"], 1)
            for src, b0 in ((kT, 0), (vT, 4)):
                for pr in range(PAIRS):
                    for c in range(NCH):
                        for b in (0, 64):
                            mm = te.matmul(ps[b:b + 64, b0 + pr, c * CH:(c + 1) * CH], src[b:b + 64, pr, c * CH:(c + 1) * CH],
                                           C("eye64")[b:b + 64, :], start=True, stop=True)
                mm.then_inc(s["tok_ps"], 1)
            pe.wait_ge(s["tok_sb"], l * 2 + 2)
            pe.wait_ge(s["gt_dve"], l * 4 + 4)
            pe.wait_ge(s["gt_act"], l * 5 + 5)
            for base_, bank in ((32, 4), (0, 5)):
                for c in range(NCH):
                    for b in range(2):
                        mm = te.matmul(ps[64 * b:64 * b + 64, bank, c * PAIRS:(c + 1) * PAIRS], gam[base_:base_ + 8, c * CH:(c + 1) * CH],
                                       seln[base_:base_ + 8, b, :], start=True, stop=True)
            mm.then_inc(s["col_ps"], 1)
            for pr in range(PAIRS):
                b4 = 4 * (pr % 2)
                if pr == 1:
                    pe.wait_ge(s["col_sb"], l * 2 + 2)
                if pr >= 2:
                    pe.wait_ge(s["dp_dve"], l * 44 + (pr - 2) * 11 + 11)
                te.matmul(ps[:, b4, :], sel[32:40, pr, :], gam[32:40, :], start=True, stop=True)
                te.matmul(ps[:, b4 + 1, :], sel[0:8, pr, :], gam[0:8, :], start=True, stop=True)
                for c in range(NCH):
                    for b in (0, 64):
                        te.matmul(ps[b:b + 64, b4 + 2, c * CH:(c + 1) * CH], kT[b:b + 64, pr, c * CH:(c + 1) * CH],
                                  kT[b:b + 64, pr, c * CH:(c + 1) * CH], start=True, stop=True)
                for c in range(NCH):
                    for b in (0, 64):
                        mm = te.matmul(ps[b:b + 64, b4 + 3, c * CH:(c + 1) * CH], kT[b:b + 64, pr, c * CH:(c + 1) * CH],
                                       qT[b:b + 64, pr, c * CH:(c + 1) * CH], start=True, stop=True)
                mm.then_inc(s["dp_ps"], 1)
            pe.wait_ge(s["dp_dve"], l * 44 + 44)
            pe.sem_inc(s["apart_pe"], 1)
            with pe.Fori(0, 5) as lev:
                for pr in range(PAIRS):
                    pe.wait_ge(s["lv_pool"], l * 20 + lev * 4 + pr + 1)
                    pe.wait_ge(s["lv_dve"], l * 40 + lev * 8)
                    pe.sem_inc(s["apart_pe"], 1)
                    for c in range(NCH):
                        for b in (0, 64):
                            mm = te.matmul(ps[b:b + 64, pr, c * CH:(c + 1) * CH], tmp[b:b + 64, pr, c * CH:(c + 1) * CH],
                                           Tm[b:b + 64, pr, c, :], start=True, stop=True)
                    mm.then_inc(s["lv_x"], 1)
                for pr in range(PAIRS):
                    pe.wait_ge(s["lv_act"], l * 20 + lev * 4 + pr + 1)
                    if pr >= 2:
                        pe.wait_ge(s["lv_dve"], l * 40 + lev * 8 + 2 * pr - 2)
                    else:
                        pe.wait_ge(s["lv_dve"], l * 40 + lev * 8)
                    pe.sem_inc(s["apart_pe"], 1)
                    for a, (lt, rt) in enumerate(((TT, Xb), (Xb, TT))):
                        for c in range(NCH):
                            for b in (0, 64):
                                mm = te.matmul(ps[b:b + 64, 4 + 2 * (pr % 2) + a, c * CH:(c + 1) * CH], lt[b:b + 64, pr, c, :],
                                               rt[b:b + 64, pr, c, :], start=True, stop=True)
                    mm.then_inc(s["lv_t"], 1)
            pe.wait_ge(s["lv_dve"], l * 40 + 40)
            pe.wait_ge(s["kv_dve"], l * 6 + 6)
            pe.sem_inc(s["apart_pe"], 1)
            for pr in range(PAIRS):
                for c in range(NCH):
                    for b in (0, 64):
                        mm = te.matmul(ps[b:b + 64, pr, c * CH:(c + 1) * CH], bk[b:b + 64, pr, c, :], TT[b:b + 64, pr, c, :], start=True, stop=True)
            mm.then_inc(s["wu_ps"], 1)
            for pr in range(PAIRS):
                for c in range(NCH):
                    for b in (0, 64):
                        mm = te.matmul(ps[b:b + 64, 4 + pr, c * CH:(c + 1) * CH], TT[b:b + 64, pr, c, :], vN[b:b + 64, pr, c, :], start=True, stop=True)
            mm.then_inc(s["wu_ps"], 1)
            pe.wait_ge(s["wu_sb"], l * 2 + 2)
            pe.sem_inc(s["apart_pe"], 1)
            HEADS = [(pr, b) for pr in range(PAIRS) for b in (0, 64)]
            for c in range(NCH):
                st = state[:, c % 2]
                pe.wait_ge(s["rc_st"], l * 9 + c + 1)
                pe.sem_inc(s["apart_pe"], 1)
                for pr, b in HEADS:
                    mm = te.matmul(ps[b:b + 64, 0, pr * CH:(pr + 1) * CH], nwT[b:b + 64, pr, c, :], st[b:b + 64, pr, :], start=True, stop=True)
                mm.then_inc(s["rc_u"], 1)
                pe.wait_ge(s["rc_un"], l * 8 + c + 1)
                pe.sem_inc(s["apart_pe"], 1)
                for pr, b in HEADS:
                    mm = te.matmul(ps[b:b + 64, 3, pr * CH:(pr + 1) * CH], kN[b:b + 64, pr, c, :], unew[b:b + 64, pr, :], start=True, stop=True)
                mm.then_inc(s["rc_ds"], 1)
                if c >= 2:
                    pe.wait_ge(s["rc_ov"], l * 8 + c - 1)
                    pe.sem_inc(s["apart_pe"], 1)
                for pr, b in HEADS:
                    dst = ps[b:b + 64, 1 + c % 2, pr * CH:(pr + 1) * CH]
                    te.matmul(dst, st[b:b + 64, pr, :], qT[b:b + 64, pr, c * CH:(c + 1) * CH], start=True, stop=False)
                    mm = te.matmul(dst, unew[b:b + 64, pr, :], pT[b:b + 64, pr, c, :], start=False, stop=True)
                mm.then_inc(s["rc_o"], 1)
            heads_norm_pe(pe, 4, hn + 10)
            pe.wait_ge(s["mix_lo"], l * 8 + 8)

        def mixer_act(l, act):
            ac = nc.scalar
            hn = l * 14
            heads_norm_act(act, qk_tiles(), hn, 64.0, eps_col("eps_l2"), first=True)
            act.wait_ge(s["sg_dve"], l * 16 + 8)
            ac.activation(sgt[:, :], mv[:, :, 1], ACT.Sqrt, bias=eps_col("eps2")).then_inc(s["sg_act"], 1)
            act.wait_ge(s["ga_ps"], l + 1)
            ac.activation(la[:, :], ps[:, 4, :], ACT.Abs, bias=pkt[:, PK_GB:PK_GB + 1]).then_inc(s["ga_act"], 1)
            act.wait_ge(evac[1], n_evac(l, 1, OFF_IN) + 4)
            ac.activation(tmp[32:40, 3, :], rows[32:40, :], ACT.Abs, bias=pkt[32:40, PK_DT:PK_DT + 1]).then_inc(s["gt_act"], 1)
            act.wait_ge(s["ga_act"], l * 7 + 1)
            ac.activation(la[:, :], la[:, :], ACT.Exp, scale=-1.0).then_inc(s["ga_act"], 1)
            act.wait_ge(s["gt_act"], l * 5 + 1)
            ac.activation(tmp[32:40, 3, :], tmp[32:40, 3, :], ACT.Exp, scale=-1.0).then_inc(s["gt_act"], 1)
            ac.activation(nega[32:40, 0:1], pkt[32:40, PK_ALOG:PK_ALOG + 1], ACT.Exp).then_inc(s["gt_act"], 1)
            act.wait_ge(s["ga_act"], l * 7 + 2)
            ac.activation(la[:, :], la[:, :], ACT.Ln, bias=1.0).then_inc(s["ga_act"], 1)
            act.wait_ge(s["gt_act"], l * 5 + 2)
            ac.activation(tmp[32:40, 3, :], tmp[32:40, 3, :], ACT.Ln, bias=1.0).then_inc(s["gt_act"], 1)
            act.wait_ge(s["ga_dve"], l * 16 + 3)
            ac.activation(tmp[:, 0, :], bcum[:, :], ACT.Exp, scale=1 / 16).then_inc(s["ga_act"], 1)
            ac.activation(tmp[:, 1, :], bcum[:, :], ACT.Exp, scale=-1 / 16).then_inc(s["ga_act"], 1)
            ac.activation(gtA[:, :], chunks(bcum[:, :])[:, :, 63], ACT.Exp, scale=1 / 16).then_inc(s["ga_act"], 1)
            act.wait_ge(s["ga_dve"], l * 16 + 4)
            ac.activation(tmp[:, 2, :], tmp[:, 2, :], ACT.Exp, scale=1 / 16).then_inc(s["ga_act"], 1)
            act.wait_ge(s["ga_ps2"], l * 4 + 2)
            ac.activation(kdA[:, :, :].rearrange("p a b -> p (a b)"), ps[:, 5, :], ACT.Copy).then_inc(s["ga_act2"], 1)
            act.wait_ge(s["ga_ps2"], l * 4 + 4)
            for a in range(2):
                for b in range(2):
                    ac.activation(oA[:, a, :].rearrange("p (t b i) -> p b t i", b=2, i=CH)[:, b], ps[:, 2 * a + b, 0:256].rearrange("p (t i) -> p t i", i=CH),
                                  ACT.Copy).then_inc(s["ga_o"], 1)
            act.wait_ge(s["ga_o"], l * 4 + 4)
            heads_norm_act(act, oA_tiles(), hn + 8, 1.0, eps_col("eps2"))
            ac.activation(gam[0:8, :], rows[0:8, :], ACT.Sigmoid).then_inc(s["gt_act"], 1)
            mix_hi(l, act, ((0, au[:, 0, :], "mixA", 1), (1, au[:, 1, :], "mixA", 2), (6, cr[:, 0, :], "mixC", 1), (7, cr[:, 1, :], "mixC", 2)), 0)

            act.wait_ge(s["tok_ps"], l * 2 + 1)
            ac.activation(kN[:, :, :, :], ps[:, 0:4, :].rearrange("p a (c t) -> p a c t", t=CH), ACT.Copy).then_inc(s["tok_sb"], 1)
            for pr in range(PAIRS):
                b4, d0 = 4 * (pr % 2), l * 44 + pr * 11
                act.wait_ge(s["dp_dve"], d0 + 2)
                ac.activation(tmp[:, 1, :], ps[:, b4, :], ACT.Exp).then_inc(s["dp_act"], 1)
                act.wait_ge(s["dp_dve"], d0 + 3)
                ac.activation(tmp[:, 2, :], tmp[:, 2, :], ACT.Exp).then_inc(s["dp_act"], 1)
                act.wait_ge(s["dp_dve"], d0 + 4)
                ac.activation(tmp[:, 0, :], tmp[:, 0, :], ACT.Exp, scale=-1.0).then_inc(s["dp_act"], 1)
            act.wait_ge(s["dp_dve"], l * 44 + 44)
            ac.activation(gtot[:, :, :], glast[:, :, :], ACT.Exp).then_inc(s["kv_act"], 1)
            ac.activation(egN[:, :, :], gN[:, :, :], ACT.Exp).then_inc(s["kv_act"], 1)
            act.wait_ge(s["kv_dve"], l * 6 + 1)
            ac.activation(kdN[:, :, :], kdN[:, :, :], ACT.Exp).then_inc(s["kv_act"], 1)
            with act.Fori(0, 5) as lev:
                for pr in range(PAIRS):
                    act.wait_ge(s["lv_x"], l * 20 + lev * 4 + pr + 1)
                    act.wait_ge(s["lv_t"], l * 20 + lev * 4)
                    ac.activation(Xb[:, pr, :, :], chunks(ps[:, pr, :]), ACT.Copy).then_inc(s["lv_act"], 1)
            act.wait_ge(s["wu_ps"], l * 2 + 1)
            ac.activation(nwT[:, :, :, :], ps[:, 0:4, :].rearrange("p a (c t) -> p a c t", t=CH), ACT.Copy, scale=-1.0).then_inc(s["wu_sb"], 1)
            for c in range(NCH):
                act.wait_ge(s["rc_o"], l * 8 + c + 1)
                ac.activation(oT[:, :, c * CH:(c + 1) * CH], ps[:, 1 + c % 2, 0:256].rearrange("p (a t) -> p a t", t=CH), ACT.Copy).then_inc(s["rc_ov"], 1)
            act.wait_ge(s["rc_ov"], l * 8 + 8)
            act.wait_ge(s["rc_st"], l * 9 + 9)
            heads_norm_act(act, o_tiles(), hn + 10, 1.0, eps_col("eps2"))
            mix_hi(l, act, [(2 + pr, oT[:, pr, :], "mixB", pr + 1) for pr in range(PAIRS)], 4)

        def mix_hi(l, act, tiles, n0):
            for m, (k, src, name, n) in enumerate(tiles):
                act.wait_ge(s[name], l * {"mixA": 2, "mixB": 4, "mixC": 2}[name] + n)
                nc.scalar.activation(xh[:, k, :], src, ACT.Copy).then_inc(s["mix_hi"], 1)

        def mix_rest(l, pool, tiles, n0):
            for m, (k, src) in enumerate(tiles):
                pool.wait_ge(s["mix_hi"], l * 8 + n0 + m + 1)
                nc.gpsimd.tensor_tensor(xl[:, k, :], src, xh[:, k, :].bitcast(F32), ALU.subtract).then_inc(s["mix_lo"], 1)

        def mixer_pool(l, pool):
            gp = nc.gpsimd
            pool.wait_ge(s["sgp_in"], l * 16 + 16)
            gp.tensor_tensor(sgw, sgw, C("upper128").unsqueeze(1).to_broadcast([P, 4, P]), ALU.mult).then_inc(s["sg_pool"], 1)
            pool.wait_ge(s["sg_dve"], l * 16 + 13)
            gp.tensor_tensor(av[:, :, :], av[:, :, :], sgp[:, SG_G:SG_G + 256].unsqueeze(1).to_broadcast([P, 4, 256]), ALU.mult).then_inc(s["sg_pool"], 1)
            pool.wait_ge(s["sg_pool"], l * 3 + 2)
            gp.tensor_tensor(av[:, :, :], av[:, :, :], sgp[:, SG_B:SG_B + 256].unsqueeze(1).to_broadcast([P, 4, 256]), ALU.add).then_inc(s["sg_pool"], 1)
            mix_rest(l, pool, ((0, au[:, 0, :]), (1, au[:, 1, :]), (6, cr[:, 0, :]), (7, cr[:, 1, :])), 0)
            for pr in range(PAIRS):
                d0 = l * 44 + pr * 11
                p0 = l * 24 + pr * 6
                pool.wait_ge(s["dp_dve"], d0 + 6)
                gp.tensor_tensor(pT[:, pr], pT[:, pr], bc(C("upper64")), ALU.mult).then_inc(s["dp_pool"], 1)
                pool.wait_ge(s["dp_act"], l * 12 + pr * 3 + 2)
                pool.wait_ge(s["dp_pool"], p0)
                gp.tensor_tensor(chunks(tmp[:, 3, :]), chunks(tmp[:, 2, :]), bc(C("strict64")), ALU.mult).then_inc(s["dp_pool"], 1)
                pool.wait_ge(s["dp_dve"], d0 + 8)
                gp.tensor_tensor(chunks(tmp[:, 5, :]), LT[:, pr], bc(C("upT1")), ALU.mult).then_inc(s["dp_pool"], 1)
                pool.wait_ge(s["dp_pool"], p0 + 3)
                gp.tensor_tensor(TT[:, pr], bc(C("eye64")), chunks(tmp[:, 5, :]), ALU.subtract).then_inc(s["dp_pool"], 1)
                pool.wait_ge(s["dp_dve"], d0 + 10)
                gp.tensor_tensor(chunks(tmp[:, 4, :]), chunks(tmp[:, 4, :]), bc(C("low1")), ALU.mult).then_inc(s["dp_pool"], 1)
                pool.wait_ge(s["dp_pool"], p0 + 5)
                gp.tensor_tensor(Tm[:, pr], bc(C("eye64")), chunks(tmp[:, 4, :]), ALU.subtract).then_inc(s["dp_pool"], 1)
            a0 = CONST_AT["upT2"][0]
            with pool.Fori(0, 5) as lev:
                for pr in range(PAIRS):
                    pool.wait_ge(s["lv_x"], l * 20 + lev * 4)
                    pool.sem_inc(s["apart_pool"], 1)
                    gp.tensor_tensor(chunks(tmp[:, pr, :]), LT[:, pr], bc(cst[:, bass.ds(lev * 64 + a0, 64)]), ALU.mult).then_inc(s["lv_pool"], 1)
            mix_rest(l, pool, [(2 + pr, oT[:, pr, :]) for pr in range(PAIRS)], 4)

        def mixer_dve(l, dve):
            ve = nc.vector
            hn = l * 14
            g0 = l * 16
            dve.wait_ge(s["conv_s"], l * 6 + 6)
            heads_norm_dve(dve, qk_tiles(), [0.125] * 4 + [1.0] * 4, hn)
            dve.wait_ge(evac[1], n_evac(l, 1, OFF_IN) + 1)
            for t in range(4):
                ve.bn_stats(stat[:, t, :], av[:, t, :]).then_inc(s["sg_dve"], 1)
            for t in range(4):
                dve.wait_ge(s["sg_dve"], g0 + t + 1)
                dve.sem_inc(s["apart_dve"], 1)
                ve.bn_aggr(mv[:, t, :], stat[:, t, :]).then_inc(s["sg_dve"], 1)
            dve.wait_ge(s["sg_act"], l + 1)
            ve.reciprocal(sgt[:, :], sgt[:, :]).then_inc(s["sg_dve"], 1)
            dve.wait_ge(s["sg_dve"], g0 + 9)
            for t in range(4):
                ve.tensor_scalar(av[:, t, :], av[:, t, :], mv[:, t, 0:1], sgt[:, t:t + 1], ALU.subtract, ALU.mult).then_inc(s["sg_dve"], 1)
            a0 = l * 16
            dve.wait_ge(s["ga_act"], l * 7 + 3)
            ve.tensor_scalar(bcum[:, :], ps[:, 4, :], pkt[:, PK_GB:PK_GB + 1], 0.0, ALU.add, ALU.min).then_inc(s["ga_dve"], 1)
            dve.wait_ge(s["ga_dve"], a0 + 1)
            ve.tensor_tensor(la[:, :], bcum[:, :], la[:, :], ALU.subtract).then_inc(s["ga_dve"], 1)
            dve.wait_ge(s["ga_dve"], a0 + 2)
            ve.tensor_tensor_scan(bcum[:, :], C("keep"), la[:, :], 0.0, ALU.mult, ALU.add).then_inc(s["ga_dve"], 1)
            dve.wait_ge(s["ga_dve"], a0 + 3)
            ve.tensor_tensor(chunks(tmp[:, 2, :]), chunks(bcum[:, :])[:, :, 63].unsqueeze(2).to_broadcast([P, NCH, CH]), chunks(bcum[:, :]),
                             ALU.subtract).then_inc(s["ga_dve"], 1)
            dve.wait_ge(s["ga_act"], l * 7 + 5)
            ve.scalar_tensor_tensor(out=cqk[:, 0, :], in0=cqk[:, 0, :], scalar=32.0 ** -0.5, in1=tmp[:, 0, :], op0=ALU.mult, op1=ALU.mult).then_inc(s["ga_dve"], 1)
            ve.tensor_tensor(tmp[:, 1, :], tmp[:, 1, :], cqk[:, 1, :], ALU.mult).then_inc(s["ga_dve"], 1)
            dve.wait_ge(s["ga_act"], l * 7 + 7)
            dve.wait_ge(s["ga_dve"], a0 + 6)
            ve.tensor_tensor(cqk[:, 1, :], cqk[:, 1, :], tmp[:, 2, :], ALU.mult).then_inc(s["ga_dve"], 1)
            dve.wait_ge(s["gt_act"], l * 5 + 4)
            ve.tensor_scalar(rows[32:40, :], rows[32:40, :], pkt[32:40, PK_DT:PK_DT + 1], 0.0, ALU.add, ALU.max).then_inc(s["gt_dve"], 1)
            dve.wait_ge(s["gt_dve"], l * 4 + 1)
            ve.tensor_tensor(rows[32:40, :], rows[32:40, :], tmp[32:40, 3, :], ALU.add).then_inc(s["gt_dve"], 1)
            dve.wait_ge(s["gt_dve"], l * 4 + 2)
            ve.tensor_scalar(rows[32:40, :], rows[32:40, :], nega[32:40, 0:1], -1.0, ALU.mult, ALU.mult).then_inc(s["gt_dve"], 1)
            dve.wait_ge(s["gt_dve"], l * 4 + 3)
            ve.tensor_tensor_scan(gam[32:40, :], C("keep")[32:40, :], rows[32:40, :], 0.0, ALU.mult, ALU.add).then_inc(s["gt_dve"], 1)
            for a in range(2):
                dve.wait_ge(s["sg_ps"], l * 2 + a + 1)
                z4 = ps[:, 6 + a, :].rearrange("p (t i) -> p t i", i=P)
                bs = sgp[:, SG_BS + a * P:SG_BS + (a + 1) * P].unsqueeze(1).to_broadcast([P, 4, P])
                ve.tensor_tensor(z4, z4, bs, ALU.add).then_inc(s["sg_dve"], 1)
                dve.wait_ge(s["sg_dve"], g0 + 14 + a)
                if a == 0:
                    pass
                ve.tensor_tensor(au[:, a, :], au[:, a, :], ps[:, 6 + a, :], ALU.mult).then_inc(s["mixA"], 1)
            dve.wait_ge(s["mixA"], l * 2 + 2)
            ve.memset(stA[:, 0, :], 0.0).then_inc(s["sg_dve"], 1)
            dve.wait_ge(s["ga_ps2"], l * 4 + 1)
            up4 = C("upper64").unsqueeze(1).to_broadcast([P, 16, CH])
            for h in range(4):
                ve.tensor_tensor(pA[:, h], ps[:, h, 0:256].rearrange("p (t i) -> p t i", i=CH), up4[:, 0:4, :], ALU.mult).then_inc(*((s["ga_dve"], 1) if h == 3 else (s["ga_pA"], 1)))
            dve.wait_ge(s["ga_ps2"], l * 4 + 3)
            for c in range(NCH - 1):
                ve.scalar_tensor_tensor(out=stA[:, c + 1, :], in0=stA[:, c, :], scalar=gtA[:, c:c + 1], in1=ps[:, 6 + c % 2, (c // 2) * CH:(c // 2 + 1) * CH],
                                        op0=ALU.mult, op1=ALU.add).then_inc(s["ga_dve"], 1)
                dve.wait_ge(s["ga_dve"], a0 + 9 + c)
            ve.memset(state[:, 0], 0.0).then_inc(s["rc_st"], 1)
            ve.memset(nega[0:1, 1:2], 0.0).then_inc(s["ga_dve"], 1)

            def gate(a):
                ve.tensor_tensor(cr[:, a, :], cr[:, a, :], oA[:, a, :], ALU.mult).then_inc(s["mixC"], 1)
            heads_norm_dve(dve, oA_tiles(), [pkt[:, PK_LAN:PK_LAN + 1]] * 2, hn + 8, gate)

            dve.wait_ge(s["tok_ps"], l * 2 + 2)
            dve.wait_ge(s["mixC"], l * 2 + 2)
            ve.tensor_copy(vN[:, :, :, :], ps[:, 4:8, :].rearrange("p a (c t) -> p a c t", t=CH)).then_inc(s["tok_sb"], 1)
            dve.wait_ge(s["col_ps"], l + 1)
            ve.tensor_copy(gN[:, :, :].rearrange("p a b -> p (a b)"), ps[:, 4, 0:32]).then_inc(s["col_sb"], 1)
            ve.tensor_copy(bN[:, :, :].rearrange("p a b -> p (a b)"), ps[:, 5, 0:32]).then_inc(s["col_sb"], 1)
            dve.wait_ge(s["col_sb"], l * 2 + 2)
            for pr in range(PAIRS):
                b4, d0 = 4 * (pr % 2), l * 44 + pr * 11
                a1 = l * 12 + pr * 3
                p0 = l * 24 + pr * 6
                R, bR, kk, qk = (chunks(ps[:, b4 + m, :]) for m in range(4))

                def done(n):
                    dve.wait_ge(s["dp_dve"], d0 + n)
                dve.wait_ge(s["dp_ps"], l * 4 + pr + 1)
                done(0)
                ve.tensor_tensor(chunks(tmp[:, 0, :]), R, col(gN[:, :, pr]), ALU.subtract).then_inc(s["dp_dve"], 1)
                ve.tensor_copy(glast[:, :, pr], R[:, :, 63]).then_inc(s["dp_dve"], 1)
                done(1)
                dve.wait_ge(s["dp_pool"], p0)
                ve.tensor_scalar(tmp[:, 2, :], tmp[:, 0, :], 0.0, None, ALU.min).then_inc(s["dp_dve"], 1)
                done(3)
                ve.tensor_scalar(tmp[:, 0, :], tmp[:, 0, :], 0.0, None, ALU.max).then_inc(s["dp_dve"], 1)
                dve.wait_ge(s["dp_act"], a1 + 1)
                ve.tensor_tensor(qT[:, pr, :], qT[:, pr, :], tmp[:, 1, :], ALU.mult).then_inc(s["dp_dve"], 1)
                dve.wait_ge(s["dp_act"], a1 + 2)
                ve.tensor_tensor(pT[:, pr], qk, chunks(tmp[:, 2, :]), ALU.mult).then_inc(s["dp_dve"], 1)
                dve.wait_ge(s["dp_pool"], p0 + 2)
                ve.tensor_tensor(chunks(tmp[:, 3, :]), chunks(tmp[:, 3, :]), bR, ALU.mult).then_inc(s["dp_dve"], 1)
                done(7)
                ve.tensor_tensor(LT[:, pr], chunks(tmp[:, 3, :]), kk, ALU.mult).then_inc(s["dp_dve"], 1)
                dve.wait_ge(s["dp_act"], a1 + 3)
                ve.tensor_tensor(chunks(tmp[:, 0, :]), chunks(tmp[:, 0, :]), col(bN[:, :, pr]), ALU.mult).then_inc(s["dp_dve"], 1)
                done(9)
                ve.tensor_tensor(chunks(tmp[:, 4, :]), chunks(tmp[:, 0, :]), kk, ALU.mult).then_inc(s["dp_dve"], 1)
                dve.wait_ge(s["dp_pool"], p0 + 6)
                ve.memset(nega[0:1, 2:3], 0.0).then_inc(s["dp_dve"], 1)
            k0 = l * 6
            ve.tensor_tensor(kdN[:, :, :], glast[:, :, :], gN[:, :, :], ALU.subtract).then_inc(s["kv_dve"], 1)
            dve.wait_ge(s["kv_act"], l * 3 + 2)
            ve.tensor_tensor(bgN[:, :, :], bN[:, :, :], egN[:, :, :], ALU.mult).then_inc(s["kv_dve"], 1)

            def by_token(v):
                return v[:, :, :].rearrange("p c a -> p a c").unsqueeze(3).to_broadcast([P, PAIRS, NCH, CH])
            dve.wait_ge(s["kv_dve"], k0 + 2)
            ve.tensor_tensor(bk[:, :, :, :], kN[:, :, :, :], by_token(bgN), ALU.mult).then_inc(s["kv_dve"], 1)
            dve.wait_ge(s["kv_act"], l * 3 + 3)
            dve.wait_ge(s["kv_dve"], k0 + 3)
            ve.tensor_tensor(kN[:, :, :, :], kN[:, :, :, :], by_token(kdN), ALU.mult).then_inc(s["kv_dve"], 1)
            ve.tensor_tensor(vN[:, :, :, :], vN[:, :, :, :], by_token(bN), ALU.mult).then_inc(s["kv_dve"], 1)
            ve.memset(nega[0:1, 3:4], 0.0).then_inc(s["kv_dve"], 1)
            with dve.Fori(0, 5) as lev:
                for pr in range(PAIRS):
                    dve.wait_ge(s["lv_t"], l * 20 + lev * 4 + pr + 1)
                    for a, M in enumerate((Tm, TT)):
                        ve.tensor_tensor(M[:, pr], M[:, pr], chunks(ps[:, 4 + 2 * (pr % 2) + a, :]), ALU.subtract).then_inc(s["lv_dve"], 1)
            dve.wait_ge(s["wu_ps"], l * 2 + 2)
            ve.tensor_copy(ub[:, :, :, :], ps[:, 4:8, :].rearrange("p a (c t) -> p a c t", t=CH)).then_inc(s["wu_sb"], 1)
            dve.wait_ge(s["wu_sb"], l * 2 + 2)
            for c in range(NCH):
                dve.wait_ge(s["rc_u"], l * 8 + c + 1)
                if c:
                    dve.wait_ge(s["rc_o"], l * 8 + c)
                ve.tensor_tensor(unew[:, :, :], ub[:, :, c, :], ps[:, 0, 0:256].rearrange("p (a t) -> p a t", t=CH), ALU.add).then_inc(s["rc_un"], 1)
                dve.wait_ge(s["rc_st"], l * 9 + c + 1)
                if c:
                    dve.wait_ge(s["rc_sg"], l * 8 + c)
                ve.tensor_tensor(tmp[:, 0, 0:256].rearrange("p (a t) -> p a t", t=CH), state[:, c % 2], gtot[:, c, :].unsqueeze(2).to_broadcast([P, PAIRS, CH]),
                                 ALU.mult).then_inc(s["rc_sg"], 1)
                dve.wait_ge(s["rc_sg"], l * 8 + c + 1)
                dve.wait_ge(s["rc_ds"], l * 8 + c + 1)
                ve.tensor_tensor(state[:, (c + 1) % 2], tmp[:, 0, 0:256].rearrange("p (a t) -> p a t", t=CH), ps[:, 3, 0:256].rearrange("p (a t) -> p a t", t=CH),
                                 ALU.add).then_inc(s["rc_st"], 1)

            def gate_z(pr):
                ve.tensor_tensor(oT[:, pr, :], oT[:, pr, :], zs[:, pr, :], ALU.mult).then_inc(s["mixB"], 1)
            dve.wait_ge(s["rc_ov"], l * 8 + 8)
            heads_norm_dve(dve, o_tiles(), [pkt[:, PK_GN:PK_GN + 1]] * 4, hn + 10, gate_z)


        def view(v, r):
            return v.rearrange("p (l r) -> p r l", r=r)

        def own(v, r):
            return v.rearrange("p (r l) -> p r l", r=r)

        def key_tiles(g, i):
            return [j for j in (i - 1, i, i + 1) if 0 <= j < 4] if WIDE[g] else [i]

        def bias_of(g, h, i):
            if not WIDE[g]:
                return (bt1, bt2)[g == 3][:, h, :]
            a = P if i == 0 else 0
            return btw[:, h, a:a + P * len(key_tiles(g, i))]

        def block1_pool(pool):
            gp = nc.gpsimd
            pool.dma_start(relb[0:32, :], rel).then_inc(s["b_rel"], 16)
            pool.dma_start(pk1[:, :], p1).then_inc(s["b_par"], 16)
            for k in range(KT):
                pool.wait_ge(s["b_hh"], k + 1)
                gp.tensor_tensor(xl[:, k, :], hb[:, k % 4, :], xh[:, k, :].bitcast(F32), ALU.subtract).then_inc(s["b_hl"], 1)
            pool.wait_ge(s["b_row"], 4)
            for g in range(4):
                src = brow[0:8, g, :].unsqueeze(1).to_broadcast([8, P, 512])
                pool.dma_start(scr[g].rearrange("m h r -> h m r"), src).then_inc(s["b_scr"], 16)
            pool.wait_ge(s["b_scr"], 64)

            def toeplitz(g, dst, p0, n, m0, m, first):
                src = bass.AP(scr_t, g * P * 8 * 512 + first, [[8 * 512 - 1, n], [512, 8], [1, m]])
                return pool.dma_start(dst[p0:p0 + n, :, m0:m0 + m], src)
            toeplitz(0, btw, 0, P, 0, 384, 127).then_inc(s["b_bw"], 16)
            toeplitz(2, bt1, 0, P, 0, P, 127).then_inc(s["b_b1"], 16)
            toeplitz(3, bt2, 0, P, 0, P, 127).then_inc(s["b_b2"], 16)
            pool.wait_ge(s["at_l"], 32)
            toeplitz(1, btw, 0, P, 0, 384, 127).then_inc(s["b_bw"], 16)
            for pr in range(PAIRS):
                pool.wait_ge(s["y_w"], 4 * pr + 4)
                gp.tensor_tensor(og[:, 1, pr, :], og[:, 1, pr, :], og[:, 2, pr, :], ALU.add).then_inc(s["y_s"], 1)
                pool.wait_ge(s["y_s"], 2 * pr + 1)
                gp.tensor_tensor(og[:, 1, pr, :], og[:, 1, pr, :], og[:, 3, pr, :], ALU.add).then_inc(s["y_s"], 1)
                for b in range(2):
                    k = 2 * pr + b
                    pool.wait_ge(s["y_h"], k + 1)
                    gp.tensor_tensor(yl[:, 4 * b + pr, :], og[:, b, pr, :], yh[:, 4 * b + pr, :].bitcast(F32), ALU.subtract).then_inc(s["y_l"], 1)
            for f in range(4):
                pool.wait_ge(s["mg_h"], f + 1)
                gp.tensor_tensor(ml[:, 2 * f:2 * f + 2, :], mt[:, 2, :, :], mh[:, 2 * f:2 * f + 2, :].bitcast(F32), ALU.subtract).then_inc(s["mg_l"], 1)
            for k in range(KT):
                pool.wait_ge(s["x1_h"], k + 1)
                gp.tensor_tensor(xl[:, k, :], x[:, k, :], xh[:, k, :].bitcast(F32), ALU.subtract).then_inc(s["x_ready"], 1)

        def block1_act(act, round_chunk):
            ac = nc.scalar
            for p in range(2):
                act.wait_ge(landed[p], 16)
                ac.activation(wh[:, p, :], raw[:, p, :], ACT.Copy).then_inc(s["hi_done"], 1)
            act.wait_ge(s["x_in"], 16)
            for k in range(KT):
                if k >= 2:
                    act.wait_ge(s["b_ms"], k - 1)
                ac.activation(bsq[:, k % 2, :], x[:, k, :], ACT.Square).then_inc(s["b_x2"], 1)
            act.wait_ge(s["b_ms"], KT)
            act.wait_ge(s["eps"], 4)
            ac.activation(bsq[:, 2, :], ps[:, 5, :], ACT.Sqrt, bias=eps_col("eps_l2")).then_inc(s["b_xs"], 1)
            for k in range(KT):
                act.wait_ge(s["b_h"], k + 1)
                ac.activation(xh[:, k, :], hb[:, k % 4, :], ACT.Copy).then_inc(s["b_hh"], 1)
            n = tile = u = 0
            for g in ORDER:
                for kind in KINDS[g]:
                    p = n % 2
                    act.wait_ge(s["used"], n + 1)
                    if kind[0] != "v":
                        for t in range(2):
                            if tile + t >= 2:
                                act.wait_ge(s["b_hm"], tile + t - 1)
                            ac.activation(bsq[:, (tile + t) % 2, :], ps[:, 2 * p + t, :], ACT.Square).then_inc(s["b_sq"], 1)
                    round_chunk(n + 2, p)
                    if kind[0] != "v":
                        for t in range(2):
                            m = tile + t
                            act.wait_ge(s["b_hm"], m + 1)
                            if m >= 2:
                                act.wait_ge(s["b_rc"], m - 1)
                            ac.activation(bsq[:, 2 + m % 2, :], ps[:, 6 + m % 2, :], ACT.Sqrt, bias=eps_col("eps_l2")).then_inc(s["b_sd"], 1)
                        tile += 2
                    n += 1
                for h in range(8):
                    for i in range(4):
                        w = P * len(key_tiles(g, i))
                        c = i * 8 + h
                        act.wait_ge(s["at_l"], u + 1)
                        if u >= 3:
                            act.wait_ge(s["at_t"], u - 2)
                        ac.activation(pb[:, u % 3, 0:w], lg[:, u % 2, 0:w], ACT.Exp, scale=-1.0, bias=nmc[:, g, c:c + 1],
                                      accum_out=lc[:, g, c:c + 1]).then_inc(s["at_p"], 1)
                        u += 1
                        if h >= 2 and h % 2 == 0 and i == 3:
                            out_pair(act, g, u - 4, h // 2 - 1)
                out_pair(act, g, u, 3)
            act.wait_ge(s["st_ps"], 8)
            for g in range(4):
                ac.activation(view(rw[0:8, g, :], VIEW[g]), own(ps[0:8, g, :], VIEW[g]), ACT.Copy).then_inc(s["st_a"], 1)
            act.wait_ge(s["st_d"], 4 + 5)
            ac.activation(rw[0:8, 9:12, :], rw[0:8, 9:12, :], ACT.Exp).then_inc(s["st_e"], 1)
            ac.activation(rw[0:8, 8, :], rw[0:8, 8, :], ACT.Exp).then_inc(s["st_e"], 1)
            ac.activation(sgl[0:8, 0, :], sgl[0:8, 0, :], ACT.Exp, bias=pk1[0:8, P1_SINK:P1_SINK + 1]).then_inc(s["st_e"], 1)
            for half in range(2):
                for b in range(2):
                    p = n % 2
                    act.wait_ge(s["used"], n + 1)
                    if half:
                        act.wait_ge(s["y_d"], 4)
                    ac.activation(zg[:, 2 * b:2 * b + 2, :], ps[:, 2 * p:2 * p + 2, :], ACT.Silu).then_inc(evac[p], 1)
                    round_chunk(n + 2, p)
                    n += 1
                for pr in (2 * half, 2 * half + 1):
                    for b in range(2):
                        act.wait_ge(s["y_d"], 2 * pr + b + 1)
                        ac.activation(yh[:, 4 * b + pr, :], og[:, b, pr, :], ACT.Copy).then_inc(s["y_h"], 1)
            for f in range(4):
                for b in range(3):
                    p = n % 2
                    act.wait_ge(s["used"], n + 1)
                    if b < 2:
                        if f and b == 0:
                            act.wait_ge(s["mg_d"], 2 * f)
                        for t in range(2):
                            c = P1_BM + 8 * b + 2 * f + t
                            ac.activation(mt[:, b, t, :], ps[:, 2 * p + t, :], ACT.Sigmoid, bias=pk1[:, c:c + 1]).then_inc(
                                *((s["mg_a"], 1) if t == 0 else (evac[p], 1)))
                    round_chunk(n + 2, p)
                    n += 1
                act.wait_ge(s["mg_d"], 2 * f + 2)
                ac.activation(mh[:, 2 * f:2 * f + 2, :], mt[:, 2, :, :], ACT.Copy).then_inc(s["mg_h"], 1)
            for j in range(4):
                p = n % 2
                act.wait_ge(evac[p], n // 2 + 1)
                for t in range(2):
                    k = 2 * j + t
                    ac.activation(xh[:, k, :], x[:, k, :], ACT.Copy).then_inc(s["x1_h"], 1)
                round_chunk(n + 2, p)
                n += 1

        def out_pair(act, g, u, pr):
            act.wait_ge(s["at_v"], u)
            nc.scalar.activation(view(og[:, g, pr, :], VIEW[g]), own(ps[:, pr % 2, :], VIEW[g]), ACT.Copy).then_inc(s["at_o"], 1)

        def block1_dve(dve, rest_chunk):
            ve = nc.vector
            for p in range(2):
                rest_chunk(p, p)
            dve.wait_ge(s["b_par"], 16)
            ve.tensor_scalar(cols[:, 3:4], pk1[:, P1_QN:P1_QN + 1], -0.125, None, ALU.mult).then_inc(s["b_c"], 1)
            ve.tensor_scalar(cols[:, 4:5], pk1[:, P1_QN + 2:P1_QN + 3], -0.125, None, ALU.mult).then_inc(s["b_c"], 1)
            ve.tensor_scalar(cols[:, 5:6], pk1[:, P1_SINK:P1_SINK + 1], -1.0, None, ALU.mult).then_inc(s["b_c"], 1)
            dve.wait_ge(s["b_xs"], 1)
            ve.reciprocal(bsq[:, 4, :], bsq[:, 2, :]).then_inc(s["b_xr"], 1)
            dve.wait_ge(s["b_xr"], 1)
            for k in range(KT):
                if k >= 4:
                    dve.wait_ge(s["b_hl"], k - 3)
                ve.scalar_tensor_tensor(out=hb[:, k % 4, :], in0=x[:, k, :], scalar=pk1[:, k:k + 1], in1=bsq[:, 4, :], op0=ALU.mult, op1=ALU.mult).then_inc(s["b_h"], 1)
            dve.wait_ge(s["b_rp"], 1)
            for g in range(4):
                ve.scalar_tensor_tensor(out=brow[0:8, g, :], in0=ps[0:8, g, :], scalar=-1.0, in1=c2[0:8, 1024 + 512 * g:1536 + 512 * g],
                                        op0=ALU.mult, op1=ALU.add).then_inc(s["b_row"], 1)
            dve.wait_ge(s["b_scr"], 64)
            n = tile = u = 0
            for gi, g in enumerate(ORDER):
                if gi:
                    dve.wait_ge(s["at_o"], 4 * gi)
                for kind in KINDS[g]:
                    p = n % 2
                    if kind[0] == "v":
                        dve.wait_ge(s["used"], n + 1)
                        w = VW[g]
                        v0 = w * int(kind[1])
                        src = ps[:, 2 * p:2 * p + 2, 0:2 * w].rearrange("p a (b c) -> p a b c", b=2)
                        dst = vg[:, :, v0:v0 + w].rearrange("p (a b) c -> p a b c", b=2)
                        ve.tensor_copy(dst, src).then_inc(evac[p], 1)
                        rest_chunk(n + 2, p)
                    else:
                        rest_chunk(n + 2, p)
                        for t in range(2):
                            m = tile + t
                            dve.wait_ge(s["b_sd"], m + 1)
                            ve.reciprocal(bsq[:, 4 + m % 2, :], bsq[:, 2 + m % 2, :]).then_inc(s["b_rc"], 1)
                            dve.wait_ge(s["b_rc"], m + 1)
                            dst = (qg if kind[0] == "q" else kg)[:, 2 * int(kind[1]) + t, :]
                            if kind[0] == "q":
                                f = cols[:, 3:4] if g == 0 else cols[:, 4:5]
                            else:
                                f = pk1[:, P1_QN + 1:P1_QN + 2] if g == 0 else pk1[:, P1_QN + 3:P1_QN + 4]
                            if t:
                                dve.wait_ge(s["b_q"], m // 2 + 1)
                            ve.scalar_tensor_tensor(out=own(dst, VIEW[g]), in0=view(ps[:, 2 * p + t, :], VIEW[g]), scalar=f, in1=view(bsq[:, 4 + m % 2, :], VIEW[g]),
                                                    op0=ALU.mult, op1=ALU.mult).then_inc(evac[p] if t else s["b_q"], 1)
                        dve.wait_ge(evac[p], n // 2 + 1)
                        tile += 2
                    n += 1
                if gi == 0:
                    dve.wait_ge(s["b_bw"], 16)
                if gi == 1:
                    dve.wait_ge(s["b_b1"], 16)
                if gi == 2:
                    dve.wait_ge(s["b_bw"], 32)
                if gi == 3:
                    dve.wait_ge(s["b_b2"], 16)
                base_u = u
                for m in range(32 + 2):
                    if m < 32:
                        h, i = m // 4, m % 4
                        w = P * len(key_tiles(g, i))
                        c = i * 8 + h
                        dve.wait_ge(s["at_s"], u + 1)
                        if u >= 2:
                            dve.wait_ge(s["at_p"], u - 1)
                        ve.tensor_tensor_reduce(out=lg[:, u % 2, 0:w], in0=ps[:, 4 + u % 2, 0:w], in1=bias_of(g, h, i), scale=1.0, scalar=3e38,
                                                op0=ALU.add, op1=ALU.min, accum_out=nmc[:, g, c:c + 1]).then_inc(s["at_l"], 1)
                        u += 1
                    if m >= 2:
                        v = base_u + m - 2
                        i = (m - 2) % 4
                        w = P * len(key_tiles(g, i))
                        dve.wait_ge(s["at_t"], v + 1)
                        if v >= 2:
                            dve.wait_ge(s["at_v"], v - 1)
                        ve.tensor_copy(pt[:, v % 2, 0:w], ps[:, 6 + v % 2, 0:w]).then_inc(s["at_e"], 1)
            dve.wait_ge(s["st_ps"], 8)
            for g in range(4):
                ve.tensor_copy(view(rw[0:8, 4 + g, :], VIEW[g]), own(ps[0:8, 4 + g, :], VIEW[g])).then_inc(s["st_d"], 1)
            dve.wait_ge(s["st_a"], 4)
            ve.tensor_scalar(sgl[0:8, 0, :], rw[0:8, 0, :], cols[0:8, 5:6], None, ALU.min).then_inc(s["st_d"], 1)
            ve.tensor_tensor(sgl[0:8, 1, :], rw[0:8, 1, :], rw[0:8, 2, :], ALU.min).then_inc(s["st_d"], 1)
            dve.wait_ge(s["st_d"], 6)
            ve.tensor_tensor(sgl[0:8, 1, :], sgl[0:8, 1, :], rw[0:8, 3, :], ALU.min).then_inc(s["st_d"], 1)
            ve.tensor_tensor(rw[0:8, 8, :], sgl[0:8, 0, :], rw[0:8, 0, :], ALU.subtract).then_inc(s["st_d"], 1)
            dve.wait_ge(s["st_d"], 7)
            ve.tensor_tensor(rw[0:8, 9:12, :], sgl[0:8, 1, :].unsqueeze(1).to_broadcast([8, 3, TOK]), rw[0:8, 1:4, :], ALU.subtract).then_inc(s["st_d"], 1)
            dve.wait_ge(s["st_e"], 3)
            ve.tensor_tensor(rw[0:8, 4:8, :], rw[0:8, 4:8, :], rw[0:8, 8:12, :], ALU.mult).then_inc(s["st_f"], 1)
            dve.wait_ge(s["st_f"], 1)
            ve.tensor_tensor(sgl[0:8, 0, :], sgl[0:8, 0, :], rw[0:8, 4, :], ALU.add).then_inc(s["st_f"], 1)
            ve.tensor_tensor(sgl[0:8, 1, :], rw[0:8, 5, :], rw[0:8, 6, :], ALU.add).then_inc(s["st_f"], 1)
            dve.wait_ge(s["st_f"], 3)
            ve.tensor_tensor(sgl[0:8, 1, :], sgl[0:8, 1, :], rw[0:8, 7, :], ALU.add).then_inc(s["st_f"], 1)
            dve.wait_ge(s["st_f"], 4)
            ve.reciprocal(sgl[0:8, :, :], sgl[0:8, :, :]).then_inc(s["st_f"], 1)
            dve.wait_ge(s["st_f"], 5)
            ve.tensor_tensor(rw[0:8, 8, :], rw[0:8, 8, :], sgl[0:8, 0, :], ALU.mult).then_inc(s["st_f"], 1)
            ve.tensor_tensor(rw[0:8, 9:12, :], rw[0:8, 9:12, :], sgl[0:8, 1, :].unsqueeze(1).to_broadcast([8, 3, TOK]), ALU.mult).then_inc(s["st_f"], 1)
            for half in range(2):
                rest_chunk(n + 2, 0)
                rest_chunk(n + 3, 1)
                for pr in (2 * half, 2 * half + 1):
                    dve.wait_ge(s["y_ps"], pr + 1)
                    for g in range(4):
                        ve.tensor_tensor(og[:, g, pr, :], og[:, g, pr, :], ps[:, 4 + g, :], ALU.mult).then_inc(s["y_w"], 1)
                    for b in range(2):
                        dve.wait_ge(evac[b], (n + b) // 2 + 1)
                        dve.wait_ge(s["y_w"], 4 * pr + 4)
                        if b:
                            dve.wait_ge(s["y_s"], 2 * pr + 2)
                        ve.tensor_tensor(og[:, b, pr, :], og[:, b, pr, :], zg[:, 2 * b + pr % 2, :], ALU.mult).then_inc(s["y_d"], 1)
                n += 2
            for f in range(4):
                for b in range(3):
                    p = n % 2
                    if b == 2:
                        dve.wait_ge(s["used"], n + 1)
                        dve.wait_ge(evac[1 - p], (n - 1) // 2 + 1)
                        dve.wait_ge(evac[p], n // 2)
                        if f:
                            dve.wait_ge(s["mg_l"], f)
                        ve.tensor_tensor(mt[:, 2, :, :], mt[:, 0, :, :], ps[:, 2 * p:2 * p + 2, :], ALU.mult).then_inc(evac[p], 1)
                        ve.tensor_tensor(mt[:, 1, :, :], mt[:, 1, :, :], ps[:, 4 + 2 * (f % 2):6 + 2 * (f % 2), :], ALU.mult).then_inc(s["mg_d"], 1)
                        dve.wait_ge(s["mg_d"], 2 * f + 1)
                        dve.wait_ge(evac[p], n // 2 + 1)
                        ve.tensor_tensor(mt[:, 2, :, :], mt[:, 2, :, :], mt[:, 1, :, :], ALU.add).then_inc(s["mg_d"], 1)
                        dve.wait_ge(s["mg_d"], 2 * f + 2)
                    rest_chunk(n + 2, p)
                    n += 1
            for j in range(4):
                p = n % 2
                dve.wait_ge(s["used"], n + 1)
                ve.tensor_tensor(x[:, 2 * j:2 * j + 2, :], x[:, 2 * j:2 * j + 2, :], ps[:, 2 * p:2 * p + 2, :], ALU.add).then_inc(evac[p], 1)
                rest_chunk(n + 2, p)
                n += 1

        def block1_pe(pe):
            te = nc.tensor
            for k in range(KT):
                pe.wait_ge(s["b_x2"], k + 1)
                te.matmul(ps[:, 5, :], C("feat_mean"), bsq[:, k % 2, :], start=(k == 0), stop=(k == KT - 1)).then_inc(s["b_ms"], 1)
            pe.wait_ge(s["b_rel"], 16)
            for g in range(4):
                o = 512 * (g // 2)
                mm = te.matmul(ps[0:8, g, :], relb[0:32, 8 * g:8 * g + 8], c2[0:32, o:o + 512], start=True, stop=True)
            mm.then_inc(s["b_rp"], 1)
            pe.wait_ge(s["b_row"], 4)
            pe.wait_ge(s["b_hl"], KT)
            n = tile = u = 0
            pending = []

            def head_means():
                for m in pending:
                    pe.wait_ge(s["b_sq"], m + 1)
                    if m >= 2:
                        pe.wait_ge(s["b_sd"], m - 1)
                    te.matmul(ps[:, 6 + m % 2, :], C("head_mean"), bsq[:, m % 2, :], start=True, stop=True).then_inc(s["b_hm"], 1)
                pending.clear()

            def begin(n):
                pe.wait_ge(s["lo_done"], n + 1)
                if n >= 2:
                    pe.wait_ge(evac[n % 2], n // 2)

            def features(n, kk, rh, rl, dst, w0, width, block):
                p = n % 2
                steps = [(w, r, k) for k in range(kk) for w, r in ((wh, rh), (wh, rl), (wl, rh))]
                for m, (w, r, k) in enumerate(steps):
                    mm = te.matmul(dst, w[:, p, w0 + k * block:w0 + k * block + P], r(k), start=(m == 0), stop=(m == len(steps) - 1))
                return mm

            def h_chunk(n):
                begin(n)
                for t in range(2):
                    mm = features(n, KT, lambda k: xh[:, k, :], lambda k: xl[:, k, :], ps[:, 2 * (n % 2) + t, :], t * P, P, 256)
                    if t == 0:
                        head_means()
                mm.then_inc(s["used"], 1)

            def tokens(v, r, t):
                if r == 1:
                    return v[:, t * P:(t + 1) * P]
                return view(v, r)[:, t, :]

            for gi, g in enumerate(ORDER):
                for kind in KINDS[g]:
                    if kind[0] != "v":
                        h_chunk(n)
                        pending += [tile, tile + 1]
                        tile += 2
                    else:
                        begin(n)
                        w, p = VW[g], n % 2
                        for t in range(4):
                            dst = ps[:, 2 * p + t // 2, w * (t % 2):w * (t % 2) + w]
                            steps = [(a, b, k) for k in range(KT) for a, b in ((xh, wh), (xl, wh), (xh, wl))]
                            for m, (a, b, k) in enumerate(steps):
                                mm = te.matmul(dst, tokens(a[:, k, :], VIEW[g], t), b[:, p, k * w:(k + 1) * w], start=(m == 0), stop=(m == len(steps) - 1))
                            if t == 1:
                                head_means()
                        mm.then_inc(s["used"], 1)
                    n += 1
                pe.wait_ge(s["b_q"], tile // 2)
                for p in range(2):
                    pe.wait_ge(evac[p], (n + 1 - p) // 2)
                base_u = u
                for m in range(32 + 3):
                    if m < 32:
                        h, i = m // 4, m % 4
                        js = key_tiles(g, i)
                        b = 64 * (h % 2)
                        kt_ = kg[b:b + 64, h // 4 if g == 0 else h // 2, js[0] * P:(js[-1] + 1) * P]
                        if u >= 2:
                            pe.wait_ge(s["at_l"], u - 1)
                        te.matmul(ps[:, 4 + u % 2, 0:P * len(js)], qg[b:b + 64, h // 2, i * P:(i + 1) * P], kt_, start=True, stop=True).then_inc(s["at_s"], 1)
                        u += 1
                    if 2 <= m < 34:
                        v = base_u + m - 2
                        i = (m - 2) % 4
                        pe.wait_ge(s["at_p"], v + 1)
                        if v >= 2:
                            pe.wait_ge(s["at_e"], v - 1)
                        for a in range(len(key_tiles(g, i))):
                            mm = te.transpose(ps[:, 6 + v % 2, a * P:(a + 1) * P], pb[:, v % 3, a * P:(a + 1) * P], C("ident"))
                        mm.then_inc(s["at_t"], 1)
                    if m >= 3:
                        v = base_u + m - 3
                        h, i = (m - 3) // 4, (m - 3) % 4
                        pe.wait_ge(s["at_e"], v + 1)
                        if h % 2 == 0 and i == 0 and h >= 4:
                            pe.wait_ge(s["at_o"], 4 * gi + h // 2 - 1)
                        js = key_tiles(g, i)
                        hv = h // 4 if g == 0 else h
                        b = 64 * (h % 2)
                        for a, j in enumerate(js):
                            mm = te.matmul(ps[b:b + 64, (h // 2) % 2, i * P:(i + 1) * P], vg[:, j, 64 * hv:64 * hv + 64], pt[:, v % 2, a * P:(a + 1) * P],
                                           start=(a == 0), stop=(a == len(js) - 1))
                        mm.then_inc(s["at_v"], 1)
                pe.wait_ge(s["at_o"], 4 * gi + 4)
            for kind, src in ((0, nmc), (1, lc)):
                for g in range(4):
                    for i in range(4):
                        mm = te.transpose(ps[0:8, 4 * kind + g, i * P:(i + 1) * P], src[:, g, 8 * i:8 * i + 8], C("ident"))
                    mm.then_inc(s["st_ps"], 1)
            pe.wait_ge(s["st_a"], 4)
            pe.wait_ge(s["st_d"], 4)
            for half in range(2):
                for b in range(2):
                    h_chunk(n)
                    n += 1
                pe.wait_ge(s["st_f"], 7)
                for pr in (2 * half, 2 * half + 1):
                    if pr:
                        pe.wait_ge(s["y_w"], 4 * pr)
                    for g in range(4):
                        mm = te.matmul(ps[:, 4 + g, :], sel[0:8, pr, :], rw[0:8, 8 + g, :], start=True, stop=True)
                    mm.then_inc(s["y_ps"], 1)
            pe.wait_ge(s["y_l"], 8)
            for f in range(4):
                h_chunk(n)
                h_chunk(n + 1)
                begin(n + 2)
                p = n % 2
                if f >= 2:
                    pe.wait_ge(s["mg_d"], 2 * f - 2)
                for b in range(2):
                    for t in range(2):
                        dst = ps[:, (2 * p if b == 0 else 4 + 2 * (f % 2)) + t, :]
                        mm = features(n + 2, 4, lambda k: yh[:, 4 * b + k, :], lambda k: yl[:, 4 * b + k, :], dst, 1024 * b + t * P, P, 256)
                mm.then_inc(s["used"], 1)
                n += 3
            pe.wait_ge(s["mg_l"], 4)
            for j in range(4):
                begin(n)
                for t in range(2):
                    mm = features(n, KT, lambda k: mh[:, k, :], lambda k: ml[:, k, :], ps[:, 2 * (n % 2) + t, :], t * P, P, 256)
                mm.then_inc(s["used"], 1)
                n += 1

        @block.sync
        def _(sp):
            sp.dma_start(cst[:, :], consts).then_inc(s["c_in"], 16)
            for p in range(2):
                sp.dma_start(raw[:, p, :], stream[p]).then_inc(landed[p], 16)
            sp.dma_start(x[:, :, :], x_in).then_inc(s["x_in"], 16)
            sp.dma_start(c2[:, :], consts2).then_inc(s["c2_in"], 16)
            with sp.Fori(1, N_CHUNKS // 2) as i:
                for p in range(2):
                    sp.wait_ge(s["lo_done"], i * 2 + p - 1)
                    sp.dma_start(raw[:, p, :], stream[bass.ds(i * 2 + p, 1)].rearrange("a p n -> (a p) n")).then_inc(landed[p], 16)

        @block.gpsimd
        def _(pool):
            gp = nc.gpsimd

            def hidden_rest(l, w, i):
                n = l * 22 + w * 11 + i + 1
                pool.wait_ge(s["h_hi"], n)
                gp.tensor_tensor(hl[:, bass.ds(i * 2, 2), :], hf[:, :, :], hh[:, bass.ds(i * 2, 2), :].bitcast(F32), ALU.subtract).then_inc(s["h_lo"], 1)

            def norm_rest(l, w):
                for k in range(KT):
                    pool.wait_ge(s["ln_h"], l * 24 + w * 8 + k + 1)
                    gp.tensor_tensor(xl[:, k, :], x[:, k, :], xh[:, k, :].bitcast(F32), ALU.subtract).then_inc(s["x_ready"], 1)

            block1_pool(pool)
            with pool.Fori(0, LAYERS) as l:
                pool.wait_ge(s["x_ready"], l * 24 + 8)
                pool.dma_start(pkt[:, :], pk[bass.ds(l, 1)].rearrange("a p n -> (a p) n")).then_inc(s["par_in"], 16)
                with pool.Fori(0, UP // 2) as i:
                    hidden_rest(l, 0, i)
                norm_rest(l, 0)
                pool.dma_start(sgp[:, :], sg[bass.ds(l, 1)].rearrange("a p n -> (a p) n")).then_inc(s["sgp_in"], 16)
                mixer_pool(l, pool)
                norm_rest(l, 1)
                with pool.Fori(0, UP // 2) as i:
                    hidden_rest(l, 1, i)
                norm_rest(l, 2)

        @block.scalar
        def _(act):
            ac = nc.scalar

            def round_chunk(n, p):
                act.wait_ge(landed[p], (n - p) * 8 + 16)
                act.wait_ge(s["used"], n - 1)
                ac.activation(wh[:, p, :], raw[:, p, :], ACT.Copy).then_inc(s["hi_done"], 1)

            def up(l, w, i, off):
                n = c_no(l, off) + i * 2
                act.wait_ge(s["used"], n + 1)
                act.wait_ge(evac[1], n_evac(l, 1, off) + i)
                ac.activation(sg_t[:, :, :], ps[:, 0:2, :], ACT.Silu).then_inc(evac[0], 1)
                round_chunk(n + 2, 0)
                act.wait_ge(evac[1], n_evac(l, 1, off) + i + 1)
                ac.activation(hh[:, bass.ds(i * 2, 2), :], hf[:, :, :], ACT.Copy).then_inc(s["h_hi"], 1)
                round_chunk(n + 3, 1)

            def norm(l, w):
                for k in range(KT):
                    act.wait_ge(s["ln_zc"], l * 24 + w * 8 + k + 1)
                    if k >= 2:
                        act.wait_ge(s["ln_var"], l * 24 + w * 8 + k - 1)
                    ac.activation(sq[:, k % 2, :], x[:, k, :], ACT.Square).then_inc(s["ln_sq"], 1)
                act.wait_ge(s["ln_var"], l * 24 + w * 8 + 8)
                ac.activation(std[:, :], ps[:, 5, :], ACT.Sqrt, bias=eps_col("eps_ln")).then_inc(s["ln_std"], 1)
                for k in range(KT):
                    act.wait_ge(s["ln_t"], l * 24 + w * 8 + k + 1)
                    c = PK_LN + 16 * w + k
                    ac.activation(x[:, k, :], x[:, k, :], ACT.Identity, scale=pkt[:, c:c + 1], bias=pkt[:, c + 8:c + 9]).then_inc(s["ln_x"], 1)
                    act.wait_ge(s["ln_x"], l * 24 + w * 8 + k + 1)
                    ac.activation(xh[:, k, :], x[:, k, :], ACT.Copy).then_inc(s["ln_h"], 1)

            act.wait_ge(s["c_in"], 16)
            block1_act(act, round_chunk)
            with act.Fori(0, LAYERS) as l:
                act.wait_ge(s["par_in"], l * 16 + 16)
                with act.Fori(0, UP // 2) as i:
                    up(l, 0, i, OFF_UP1)
                with act.Fori(0, KT) as f:
                    for p in range(2):
                        round_chunk(c_no(l, OFF_DN1) + f * 2 + p + 2, p)
                norm(l, 0)
                in_products_act(l, act, round_chunk)
                mixer_act(l, act)
                for j in range(OUTP):
                    round_chunk(c_no(l, OFF_OUT) + j + 2, j % 2)
                norm(l, 1)
                with act.Fori(0, UP // 2) as i:
                    up(l, 1, i, OFF_UP2)
                with act.Fori(0, KT) as f:
                    for p in range(2):
                        round_chunk(c_no(l, OFF_DN2) + f * 2 + p + 2, p)
                norm(l, 2)
            act.wait_ge(s["x_ready"], 8 + 24 * LAYERS)
            act.dma_start(out, x[:, :, :]).then_inc(s["stored"], 16)
            act.wait_ge(s["stored"], 16)

        @block.vector
        def _(dve):
            ve = nc.vector

            def rest_chunk(n, p):
                dve.wait_ge(s["hi_done"], n + 1)
                ve.tensor_tensor(wl[:, p, :], raw[:, p, :], wh[:, p, :].bitcast(F32), ALU.subtract).then_inc(s["lo_done"], 1)

            def up(l, w, i, off):
                n = c_no(l, off) + i * 2
                rest_chunk(n + 2, 0)
                dve.wait_ge(s["used"], n + 2)
                dve.wait_ge(evac[0], n_evac(l, 0, off) + i + 1)
                dve.wait_ge(s["h_lo"], l * 22 + w * 11 + i)
                ve.tensor_tensor(hf[:, :, :], ps[:, 2:4, :], sg_t[:, :, :], ALU.mult).then_inc(evac[1], 1)
                rest_chunk(n + 3, 1)

            def down(l, w, i, off):
                for q in range(2):
                    f = i * 2 + q
                    n = c_no(l, off) + i * 4 + q * 2
                    rest_chunk(n + 2, 0)
                    dve.wait_ge(s["used"], n + 2)
                    xf = x[:, bass.ds(f, 1), :].rearrange("p a t -> p (a t)")
                    ve.scalar_tensor_tensor(out=xf, in0=ps[:, 2 * q, :], scalar=0.5 / ALPHA, in1=xf, op0=ALU.mult, op1=ALU.add).then_inc(evac[1], 1)
                    dve.wait_ge(evac[1], n_evac(l, 1, off) + f + 1)
                    dve.wait_ge(s["z_sum"], l * 27 + w * 9 + f + 1)
                    ve.tensor_tensor(zacc[:, :], zacc[:, :], xf, ALU.add).then_inc(s["z_sum"], 1)
                    rest_chunk(n + 3, 1)

            def norm(l, w):
                dve.wait_ge(s["ln_mean"], l * 3 + w + 1)
                for k in range(KT):
                    ve.tensor_tensor(x[:, k, :], x[:, k, :], ps[:, 4, :], ALU.subtract).then_inc(s["ln_zc"], 1)
                dve.wait_ge(s["ln_std"], l * 3 + w + 1)
                ve.reciprocal(rstd[:, :], std[:, :]).then_inc(s["ln_rs"], 1)
                dve.wait_ge(s["ln_rs"], l * 3 + w + 1)
                for k in range(KT):
                    ve.tensor_tensor(x[:, k, :], x[:, k, :], rstd[:, :], ALU.mult).then_inc(s["ln_t"], 1)

            dve.memset(cols[:, 0:1], EPS2 / ALPHA ** 2).then_inc(s["eps"], 1)
            dve.memset(cols[:, 1:2], EPS2).then_inc(s["eps"], 1)
            dve.memset(cols[:, 2:3], EPS_L2).then_inc(s["eps"], 1)
            dve.memset(nega[:, :], 0.0).then_inc(s["eps"], 1)
            dve.wait_ge(s["eps"], 4)
            block1_dve(dve, rest_chunk)
            with dve.Fori(0, LAYERS) as l:
                with dve.Fori(0, UP // 2) as i:
                    up(l, 0, i, OFF_UP1)
                dve.wait_ge(evac[1], n_evac(l, 1, OFF_DN1))
                ve.memset(zacc[:, :], 0.0).then_inc(s["z_sum"], 1)
                with dve.Fori(0, KT // 2) as i:
                    down(l, 0, i, OFF_DN1)
                norm(l, 0)
                in_products_dve(l, dve, rest_chunk)
                mixer_dve(l, dve)
                dve.wait_ge(s["mixB"], l * 4 + 4)
                ve.memset(zacc[:, :], 0.0).then_inc(s["z_sum"], 1)
                for j in range(OUTP):
                    n = c_no(l, OFF_OUT) + j
                    p = j % 2
                    dve.wait_ge(s["used"], n + 1)
                    ve.scalar_tensor_tensor(out=x[:, 2 * j:2 * j + 2, :], in0=ps[:, 2 * p:2 * p + 2, :], scalar=1.0 / ALPHA, in1=x[:, 2 * j:2 * j + 2, :], op0=ALU.mult, op1=ALU.add).then_inc(evac[p], 1)
                    dve.wait_ge(evac[p], n_evac(l, p, OFF_OUT) + j // 2 + 1)
                    for k in range(2):
                        dve.wait_ge(s["z_sum"], l * 27 + 9 + 2 * j + k + 1)
                        ve.tensor_tensor(zacc[:, :], zacc[:, :], x[:, 2 * j + k, :], ALU.add).then_inc(s["z_sum"], 1)
                    rest_chunk(n + 2, p)
                norm(l, 1)
                with dve.Fori(0, UP // 2) as i:
                    up(l, 1, i, OFF_UP2)
                dve.wait_ge(evac[1], n_evac(l, 1, OFF_DN2))
                ve.memset(zacc[:, :], 0.0).then_inc(s["z_sum"], 1)
                with dve.Fori(0, KT // 2) as i:
                    down(l, 2, i, OFF_DN2)
                norm(l, 2)

        @block.tensor
        def _(pe):
            te = nc.tensor
            H, L_ = 0, 1

            def product_t(n, p, w_lo, outs, rhs_h, rhs_l, k0, first, last):
                pass

            def parts(w, rh, rl):
                return

            def accumulate(dst, ks, wslice, rh, rl, start, stop, moving_w=False, inc=None):
                steps = []
                for k in ks:
                    steps += [(wh, rh, k), (wh, rl, k), (wl, rh, k)]
                for m, (w, r, k) in enumerate(steps):
                    a, b = wslice(w, k), r(k)
                    if moving_w:
                        a, b = b, a
                    mm = te.matmul(dst, a, b, start=(start and m == 0), stop=(stop and m == len(steps) - 1))
                return mm

            def chunk_t(l, off, i, p, cols=256, xr=None):
                n = c_no(l, off) + i
                pe.wait_ge(s["lo_done"], n + 1)
                for j in range(cols // P):
                    mm = accumulate(ps[:, 2 * p + j, :], range(KT),
                                    lambda w, k: w[:, p, k * cols + j * P:k * cols + (j + 1) * P],
                                    lambda k: xh[:, k, :], lambda k: xl[:, k, :], True, True)
                mm.then_inc(s["used"], 1)

            def chunk_n(l, off, i, p):
                n = c_no(l, off) + i
                pe.wait_ge(s["lo_done"], n + 1)
                for t in range(4):
                    steps = [(xx, w, k) for k in range(KT) for xx, w in ((xh, wh), (xl, wh), (xh, wl))]
                    dst = ps[:, 2 * p + t // 2, 256 * (t % 2):256 * (t % 2) + 256]
                    for m, (a, w, k) in enumerate(steps):
                        mm = te.matmul(dst, a[:, k, t * P:(t + 1) * P], w[:, p, k * 256:(k + 1) * 256],
                                       start=(m == 0), stop=(m == len(steps) - 1))
                mm.then_inc(s["used"], 1)

            def up(l, w, i, off):
                for p in range(2):
                    pe.wait_ge(evac[p], n_evac(l, p, off) + i)
                    chunk_t(l, off, i * 2 + p, p)

            def down(l, w, i, off):
                for q in range(2):
                    pe.wait_ge(evac[1], n_evac(l, 1, off) + i * 2 + q - (1 if q else 1))
                    for p in range(2):
                        n = c_no(l, off) + i * 4 + q * 2 + p
                        pe.wait_ge(s["lo_done"], n + 1)
                        mm = accumulate(ps[:, 2 * q, :], range(11), lambda w_, k: w_[:, p, k * P:(k + 1) * P],
                                        lambda k: hh[:, 11 * p + k, :], lambda k: hl[:, 11 * p + k, :], p == 0, p == 1)
                        mm.then_inc(s["used"], 1)

            def norm(l, w):
                pe.wait_ge(s["z_sum"], l * 27 + w * 9 + 9)
                te.matmul(ps[:, 4, :], C("feat_mean"), zacc[:, :], start=True, stop=True).then_inc(s["ln_mean"], 1)
                for k in range(KT):
                    pe.wait_ge(s["ln_sq"], l * 24 + w * 8 + k + 1)
                    te.matmul(ps[:, 5, :], C("feat_mean"), sq[:, k % 2, :], start=(k == 0), stop=(k == KT - 1)).then_inc(s["ln_var"], 1)

            pe.wait_ge(s["c_in"], 16)
            pe.wait_ge(s["c2_in"], 16)
            block1_pe(pe)
            with pe.Fori(0, LAYERS) as l:
                pe.wait_ge(s["x_ready"], l * 24 + 8)
                pe.sem_inc(s["apart_pe"], 1)
                with pe.Fori(0, UP // 2) as i:
                    up(l, 0, i, OFF_UP1)
                pe.wait_ge(s["h_lo"], l * 22 + 11)
                pe.wait_ge(evac[0], n_evac(l, 0, OFF_DN1))
                pe.wait_ge(evac[1], n_evac(l, 1, OFF_DN1))
                pe.sem_inc(s["apart_pe"], 1)
                with pe.Fori(0, KT // 2) as i:
                    down(l, 0, i, OFF_DN1)
                norm(l, 0)
                pe.wait_ge(s["x_ready"], l * 24 + 16)
                in_products_pe(l, pe, chunk_t, chunk_n)
                mixer_pe(l, pe)
                for j in range(OUTP):
                    pe.wait_ge(evac[j % 2], n_evac(l, j % 2, OFF_OUT) + j // 2)
                    chunk_t(l, OFF_OUT, j, j % 2)
                norm(l, 1)
                pe.wait_ge(s["x_ready"], l * 24 + 24)
                pe.sem_inc(s["apart_pe"], 1)
                with pe.Fori(0, UP // 2) as i:
                    up(l, 1, i, OFF_UP2)
                pe.wait_ge(s["h_lo"], l * 22 + 22)
                pe.wait_ge(evac[0], n_evac(l, 0, OFF_DN2))
                pe.wait_ge(evac[1], n_evac(l, 1, OFF_DN2))
                pe.sem_inc(s["apart_pe"], 1)
                with pe.Fori(0, KT // 2) as i:
                    down(l, 1, i, OFF_DN2)
                norm(l, 2)


def blocks(w, cols):
    k, n = w.shape
    return w.reshape(k // P, P, n // cols, cols).transpose(2, 1, 0, 3).reshape(n // cols, P, k // P * cols)


def pad(c):
    out = np.zeros(c.shape[:2] + (2048,), c.dtype)
    out[:, :, :c.shape[2]] = c
    return out


def up_chunks(w1, w3):
    return np.stack([blocks(w1, 256), blocks(w3, 256)], 1).reshape(-1, P, 2048)


def down_chunks(w2):
    b = w2.reshape(2, FT // 2, P, KT, P).transpose(3, 0, 2, 1, 4).reshape(2 * KT, P, FT // 2 * P)
    return pad(b)


def layer_chunks(a, l):
    w = a["w_in_2"][l]
    small = np.zeros((D, P), w.dtype)
    small[:, 64:80] = w[:, 3344:3360]
    small[:, 32:40] = w[:, 2568:2576]
    small[:, 0:8] = w[:, 2560:2568]
    order = [blocks(w[:, c:c + 256], 256) for c in (0, 256, 2048, 2304, 2576, 3088, 2832)]
    order += [pad(blocks(small, P))] + [blocks(w[:, 512 + 256 * q:768 + 256 * q], 256) for q in range(6)]
    return [up_chunks(a["ffn1_w1_2"][l], a["ffn1_w3_2"][l]), down_chunks(a["ffn1_w2_2"][l])] + order + [
        blocks(a["w_out_2"][l], 256), up_chunks(a["ffn2_w1_2"][l], a["ffn2_w3_2"][l]), down_chunks(a["ffn2_w2_2"][l])]


def layer_params(a, l):
    pk = np.zeros((P, NPK), np.float32)
    for w, (g, b) in enumerate((("ln1_g_2", "ln1_b_2"), ("ln2_g_2", "ln2_b_2"), ("ln3_g_2", "ln3_b_2"))):
        pk[:, PK_LN + 16 * w:PK_LN + 16 * w + 8] = a[g][l].reshape(KT, P).T
        pk[:, PK_LN + 16 * w + 8:PK_LN + 16 * w + 16] = a[b][l].reshape(KT, P).T
    pk[:, PK_CONV:PK_CONV + 48] = a["gdn_conv_w_2"][l].reshape(4, 12, P).transpose(2, 1, 0).reshape(P, 48)
    pk[:, PK_GN] = np.concatenate([a["gdn_norm_g_2"][l]] * 2)
    pk[:, PK_LAN] = np.concatenate([a["gla_norm_g_2"][l]] * 2)
    pk[32:40, PK_ALOG] = a["gdn_a_log_2"][l]
    pk[32:40, PK_DT] = a["gdn_dt_bias_2"][l]
    pk[:, PK_GB] = a["gla_gate_b_2"][l]
    pk[64:80, PK_UP:PK_UP + P] = a["gla_gate_up_2"][l]
    sg = np.zeros((P, NSG), np.float32)
    sg[:, SG_G:SG_G + 256] = a["sgu_ln_g_2"][l][None, :]
    sg[:, SG_B:SG_B + 256] = a["sgu_ln_b_2"][l][None, :]
    sg[:, SG_BS:SG_BS + 256] = np.repeat(a["sgu_b_2"][l].reshape(2, 2, P).transpose(1, 0, 2).reshape(2, 256), 64, 0)
    sg[:, SG_W:SG_W + 512] = a["sgu_w_2"][l].transpose(2, 0, 1).reshape(P, 512)
    return pk, sg


def first_chunks(a):
    w = a["w_in"][0]
    qa, ka, va, qb, kb, vb, ga, gb, mg = (w[:, c:c + n] for c, n in (
        (0, 512), (512, 128), (640, 128), (768, 1536), (2304, 1536), (3840, 1536), (5376, 512), (5888, 512), (6400, 2048)))
    k2 = np.concatenate([ka[:, 64 * h:64 * h + 64] for h in (0, 0, 1, 1)], 1)
    out = []
    for g in ORDER:
        if g == 0:
            out += [blocks(qa, 256), blocks(k2, 256), pad(blocks(va, 128))]
        else:
            c = slice(512 * (g - 1), 512 * g)
            out += [blocks(qb[:, c], 256), blocks(kb[:, c], 256), blocks(vb[:, c], 256)]
    for h in range(2):
        c = slice(256 * h, 256 * h + 256)
        out += [blocks(ga[:, c], 256), blocks(gb[:, c], 256)]
    wa, wb = blocks(a["w_branch_a"][0], 256), blocks(a["w_branch_b"][0], 256)
    for f in range(4):
        c = 256 * f
        out += [blocks(mg[:, c:c + 256], 256), blocks(mg[:, D + c:D + c + 256], 256), np.concatenate([wa[f:f + 1], wb[f:f + 1]], 2)]
    return out + [blocks(a["w_out"][0], 256)]


def first_params(a):
    p = np.zeros((P, 32), np.float32)
    p[:, 0:8] = a["norm_gain"][0].reshape(KT, P).T
    for m, name in enumerate(("q_norm_a", "k_norm_a", "q_norm_b", "k_norm_b")):
        p[:, P1_QN + m] = np.concatenate([a[name][0]] * 2)
    p[0:8, P1_SINK] = a["sink_a"][0]
    p[:, P1_BM:P1_BM + 16] = a["b_merge"][0].reshape(16, P).T
    return p


def lay_out(a):
    parts = first_chunks(a)
    for l in range(LAYERS):
        parts += layer_chunks(a, l)
    parts.append(np.zeros((2, P, 2048), np.float32))
    small = [layer_params(a, l) for l in range(LAYERS)]
    return {
        "stream": np.concatenate(parts, 0),
        "pk": np.stack([p for p, _ in small]),
        "sg": np.stack([g for _, g in small]),
        "consts": CONSTS,
        "consts2": bias_constants(),
        "rel": np.ascontiguousarray(a["rel_bias"]),
        "p1": first_params(a),
        "x_in": np.ascontiguousarray(a["x"][0].reshape(TOK, KT, P).transpose(2, 1, 0)),
    }


def kernel(**inputs):
    import concourse.bacc as bacc
    from concourse.bass_utils import run_bass_kernel_spmd

    nc = bacc.Bacc("TRN2", target_bir_lowering=False, num_devices=1)
    arrays = lay_out({name: np.asarray(v) for name, v in inputs.items()})
    aps = {name: nc.dram_tensor(name, v.shape, F32, kind="ExternalInput").ap() for name, v in arrays.items()}
    out = nc.dram_tensor("out", (P, KT, TOK), F32, kind="ExternalOutput").ap()
    program(nc, out=out, **aps)
    r = run_bass_kernel_spmd(nc, [arrays], core_ids=[0])
    y = r.results[0]["out"]
    return np.ascontiguousarray(y.transpose(2, 1, 0)).reshape(1, TOK, D)
```

```python
from contextlib import ExitStack

import numpy as np
import concourse.bass as bass
from concourse import mybir

F32 = mybir.dt.float32
F32R = mybir.dt.float32r
ALU = mybir.AluOpType
ACT = mybir.ActivationFunctionType
AXX = mybir.AxisListType.X

P = 128
TOK = 512
D = 1024
KT = D // P
DFF = 2816
FT = DFF // P
LAYERS = 2
ALPHA = (2.0 * LAYERS) ** 0.25
EPS2 = 1e-5
EPS_L2 = 1e-6
CH = 64
NCH = TOK // CH
PAIRS = 4

UP = 2 * FT // 2
DOWN = 2 * KT
INP = 14
OUTP = KT // 2
PER = 2 * UP + 2 * DOWN + INP + OUTP
OFF_UP1, OFF_DN1 = 0, UP
OFF_IN = UP + DOWN
OFF_OUT = OFF_IN + INP
OFF_UP2 = OFF_OUT + OUTP
OFF_DN2 = OFF_UP2 + UP

K1 = 1024

VIEW = (1, 1, 4, 4)
HALF = (128, 64, 64, 64)
WIDE = (True, True, False, False)
ORDER = (0, 2, 1, 3)
KINDS = {0: ("q0", "q1", "k0", "v0")} | {g: ("q0", "q1", "k0", "k1", "v0", "v1") for g in (1, 2, 3)}
VW = (128, 256, 256, 256)
BASE = 4 + 18 + 4 + 12 + 4
P1_QN, P1_SINK, P1_BM = 8, 12, 16


def buckets(rel):
    half, exact, far = 16, 8, 1024
    n = np.abs(rel)
    nf = np.maximum(n, exact).astype(np.float32)
    large = exact + (np.log(nf / np.float32(exact)) / np.float32(np.log(far / exact)) * np.float32(half - exact)).astype(np.int32)
    return (rel > 0) * half + np.where(n < exact, n, np.minimum(large, half - 1))


def bias_constants():
    out = np.zeros((P, 2048), np.float32)
    r = np.arange(512)
    for t, (stride, mid) in enumerate(((1, 255), (4, 127))):
        out[buckets((r - mid) * stride), 512 * t + r] = 1
    for g, (mid, step) in enumerate(((255, 1), (255, 1), (127, 1), (127, 4))):
        near = ((r - mid) % step == 0) & (np.abs(r - mid) <= HALF[g] * step)
        row, c = 8 * (g % 2), 1024 + 512 * (g // 2)
        out[row:row + 8, c:c + 512] = np.where(near, 0.0, 1e30)
    return out


def const_columns():
    at, parts = {}, []
    n = 0

    def put(name, a):
        nonlocal n
        a = np.asarray(a, np.float32).reshape(P, -1)
        at[name] = (n, a.shape[1])
        parts.append(a)
        n += a.shape[1]

    r = np.arange(P)
    put("ident", np.eye(P))
    put("head_mean", (r[:, None] // 64 == r[None, :] // 64) / 64.0)
    put("feat_mean", np.full((P, P), 1.0 / D))
    i, j = r[:, None] % CH, np.arange(CH)[None, :]
    put("eye64", i == j)
    put("upper64", i <= j)
    put("strict64", i < j)
    put("low1", (i == j + 1) & (j % 2 == 0))
    put("upT1", (j == i + 1) & (i % 2 == 0))
    for s in (2, 4, 8, 16, 32):
        put(f"upT{s}", ((i // s) % 2 == 0) & (j // s == i // s + 1))
    put("upper128", r[:, None] <= r[None, :])
    put("keep", np.tile((np.arange(TOK) % CH != 0)[None, :], (P, 1)))
    sel = np.zeros((P, PAIRS, P))
    for base in (0, 32):
        for h in range(8):
            sel[base + h, h // 2, 64 * (h % 2):64 * (h % 2) + 64] = 1
    put("sel", sel)
    seln = np.zeros((P, 2, PAIRS))
    for base in (0, 32):
        for h in range(8):
            seln[base + h, h % 2, h // 2] = 1
    put("seln", seln)
    return at, np.concatenate(parts, 1)


CONST_AT, CONSTS = const_columns()
NC = CONSTS.shape[1]
PK_LN, PK_CONV, PK_GN, PK_LAN, PK_ALOG, PK_DT, PK_GB, PK_UP = 0, 48, 96, 97, 98, 99, 100, 104
NPK = 232
SG_G, SG_B, SG_BS, SG_W = 0, 256, 512, 768
NSG = 1280


def at(l, per, n):
    return n if l is None else l * per + n


LV_DVE = 4 * 8 + 4

SIGNALS = """
fm_set
apart_pe apart_dve apart_pool
c_in x_in xh0 par_in sgp_in eps hi_done lo_done used xr0 xr1 h_hi h_lo z_sum
ln_mean ln_zc ln_sq ln_var ln_std ln_rs ln_t ln_x ln_h conv_a conv_d conv_s
hn_sq hn_ps hn_std hn_rc hn_d ga_ps ga_ps2 ga_act ga_act2 ga_dve ga_pA ga_o gt_act gt_dve
sg_pool sg_ps sg_act sg_dve mixA mixB mixC mix_hi mix_lo tok_ps tok_sb col_ps col_sb
b_rel b_par b_far b_hh b_hl b_row b_scr b_bw b_b1 b_b2 b_x2 b_ms b_xs b_xr b_h b_c b_rp b_sq b_hm b_sd b_rc b_q
at_s at_l at_p at_t at_e at_v at_o st_ps st_a st_d st_e st_f y_w y_s y_h y_l y_ps y_d mg_h mg_l mg_a mg_d x1_h c2_in
dp_ps dp_dve dp_act dp_pool kv_act kv_dve lv_x lv_t lv_act lv_dve lv_pool wu_ps wu_sb
rc_st rc_u rc_un rc_ds rc_o rc_ov rc_sg tr_ps tr_sb stored
"""


def program(nc, stream, pk, sg, consts, consts2, rel, p1, x_in, out):
    base = BASE
    with ExitStack() as ctx:
        scr_t = nc.dram_tensor("bias_rows", (4, P, 8, 512), F32)
        scr = scr_t.ap()
        used_sems = {}

        def sem(name):
            used_sems[name] = ctx.enter_context(nc.semaphore(name))
            return used_sems[name]

        def sb(name, kb, shape, dt=F32):
            return nc.alloc_sbuf_tensor_at(name, shape, dt, offset=OFS + int(kb * K1))

        OFS = (nc.sbuf_base + 31) // 32 * 32
        raw = sb("raw", 0, [P, 2, 2048])
        wh = sb("wh", 16, [P, 2, 2048], F32R)
        wl = sb("wl", 32, [P, 2, 2048], F32R)
        x = sb("x", 48, [P, KT, TOK])
        xh = sb("xh", 64, [P, KT, TOK], F32R)
        xl = sb("xl", 80, [P, KT, TOK], F32R)
        hh = sb("hh", 96, [P, FT, TOK], F32R)
        hl = sb("hl", 140, [P, FT, TOK], F32R)
        sg_t = sb("sg_t", 184, [P, 2, TOK])
        hf = sb("hf", 188, [P, 2, TOK])
        zacc = sb("zacc", 184, [P, TOK])
        zn = sb("zn", 96, [P, KT, TOK])
        sq = sb("sq", 112, [P, 4, TOK])
        rstd = sb("rstd", 192, [P, TOK])
        std = sb("std", 194, [P, TOK])
        cst = sb("cst", 196, [P, NC])
        pkt = sb("pkt", 196 + NC * 4 / K1 + 0.03125, [P, NPK])

        qkv = sb("qkv", 96, [P, 12, TOK])
        qT, kT, vT = qkv[:, 0:4, :], qkv[:, 4:8, :], qkv[:, 8:12, :]
        kN = sb("kN", 120, [P, PAIRS, NCH, CH])
        vN = sb("vN", 128, [P, PAIRS, NCH, CH])
        pT = sb("pT", 136, [P, PAIRS, NCH, CH])
        LT = sb("LT", 144, [P, PAIRS, NCH, CH])
        Tm = sb("Tm", 152, [P, PAIRS, NCH, CH])
        TT = sb("TT", 160, [P, PAIRS, NCH, CH])
        tmp = sb("tmp", 168, [P, 6, TOK])
        zs = sb("zs", 180, [P, PAIRS, TOK])
        rows = sb("rows", 188, [P, TOK])
        gam = sb("gam", 190, [P, TOK])
        gN = sb("gN", 192, [P, NCH, PAIRS])
        bN = sb("bN", 192.125, [P, NCH, PAIRS])
        bgN = sb("bgN", 192.25, [P, NCH, PAIRS])
        kdN = sb("kdN", 192.375, [P, NCH, PAIRS])
        glast = sb("glast", 192.5, [P, NCH, PAIRS])
        gtot = sb("gtot", 192.625, [P, NCH, PAIRS])
        egN = sb("egN", 192.75, [P, NCH, PAIRS])
        nega = sb("nega", 192.875, [P, 8])
        state = sb("state", 193, [P, 2, PAIRS, CH])
        unew = sb("unew", 195, [P, PAIRS, CH])
        au = sb("au", 144, [P, 2, TOK])
        av = sb("av", 148, [P, 4, 256])
        cqk = sb("cqk", 152, [P, 2, TOK])
        cr = sb("cr", 156, [P, 2, TOK])
        cv = sb("cv", 160, [P, 4, 256])
        sgp = sb("sgp", 136, [P, NSG])
        bcum = sb("bcum", 164, [P, TOK])
        la = sb("la", 166, [P, TOK])
        pA = sb("pA", 120, [P, 4, 4, CH])
        kdA = sb("kdA", 124, [P, 4, P])
        stA = sb("stA", 126, [P, NCH, CH])
        oA = sb("oA", 128, [P, 2, TOK])
        stat = sb("stat", 132, [P, 4, 6])
        mv = sb("mv", 132.125, [P, 4, 2])
        sgt = sb("sgt", 132.25, [P, 4])
        gtA = sb("gtA", 132.5, [P, NCH])
        cols = sb("cols", 206.25, [P, 8])
        ps = nc.alloc_psum_tensor("ps", [P, 8, TOK], F32)

        Xb = qkv[:, 8:12, :].rearrange("p a (c t) -> p a c t", t=CH)
        oT = qkv[:, 8:12, :]
        bk = qkv[:, 4:8, :].rearrange("p a (c t) -> p a c t", t=CH)
        nwT, ub = Tm, LT
        sgw = sgp[:, SG_W:SG_W + 512].rearrange("p (h i) -> p h i", i=P)
        qg = sb("qg", 96, [P, 4, TOK])
        kg = sb("kg", 104, [P, 4, TOK])
        vg = sb("vg", 112, [P, 4, TOK])
        btw = sb("btw", 120, [P, 8, 384])
        og = sb("og", 132, [P, 4, 4, TOK])
        lg = sb("lg", 164, [P, 2, 384])
        pb = sb("pb", 167, [P, 3, 384])
        pt = sb("pt", 171.5, [P, 2, 384])
        nmc = sb("nmc", 174.5, [P, 4, 32])
        lc = sb("lc", 175, [P, 4, 32])
        bsq = sb("bsq", 175.5, [P, 6, TOK])
        bt1 = sb("bt1", 187.5, [P, 8, P])
        bt2 = sb("bt2", 191.5, [P, 8, P])
        pk1 = sb("pk1", 206.5, [P, 32])
        fm = sb("fm", 128, [P, P])
        c2 = sb("c2", 132, [P, 2048])
        brow = sb("brow", 146, [P, 2, TOK])
        relb = sb("relb", 154, [P, 32])
        hb = sb("hb", 155, [P, 4, TOK])
        rw = sb("rw", 96, [P, 12, TOK])
        sgl = sb("sgl", 120, [P, 2, TOK])
        zg = sb("zg", 124, [P, 4, TOK])
        yh = sb("yh", 164, [P, 8, TOK], F32R)
        yl = sb("yl", 180, [P, 8, TOK], F32R)
        mt = sb("mt", 96, [P, 3, 2, TOK])
        mh = sb("mh", 132, [P, 8, TOK], F32R)
        ml = sb("ml", 148, [P, 8, TOK], F32R)

        def C(name, *shape):
            a, w = CONST_AT[name]
            v = cst[:, a:a + w]
            return v

        sel = C("sel").rearrange("p (a b) -> p a b", a=PAIRS)
        seln = C("seln").rearrange("p (a b) -> p a b", a=2)

        def bc(v, n=NCH):
            return v.unsqueeze(1).to_broadcast([P, n, v.shape[1]])

        def col(v):
            return v.unsqueeze(2).to_broadcast([P, v.shape[1], CH])

        def chunks(v):
            return v.rearrange("p (c t) -> p c t", t=CH)

        landed = [sem("landed0"), sem("landed1")]
        evac = [sem("evac0"), sem("evac1")]
        s = {name: sem(name) for name in SIGNALS.split()}
        xr = [s["xr0"], s["xr1"]]
        block = ctx.enter_context(nc.Block())

        def n_evac(l, p, off):
            n = (min(off, OFF_DN1) + (max(off - OFF_IN, 0) if off <= OFF_DN2 else OFF_DN2 - OFF_IN)) // 2
            if p:
                n += max(min(off, OFF_IN) - OFF_DN1, 0) // 2 + max(off - OFF_DN2, 0) // 2
            return l * (E0_PER + p * 2 * KT) + BASE_E + n

        def c_no(l, off):
            return l * PER + base + off

        BASE_E = base // 2
        E0_PER = (OFF_DN1 + OFF_DN2 - OFF_IN) // 2
        N_CHUNKS = base + LAYERS * PER + 2

        def eps_col(name):
            k = ("eps_ln", "eps2", "eps_l2").index(name)
            return cols[:, k:k + 1]


        IN_ROWS, IN_CQK, IN_CV, IN_AU, IN_AV, IN_CR, IN_Z = range(6, 13)

        def in_products_pe(l, pe, chunk_t, chunk_n, ready):
            te = nc.tensor
            for j in range(INP):
                pe.wait_ge(evac[j % 2], n_evac(l, j % 2, OFF_IN) + j // 2)
                if j in (IN_CV, IN_AV):
                    chunk_n(l, OFF_IN, j, j % 2)
                else:
                    chunk_t(l, OFF_IN, j, j % 2, 128 if j == IN_ROWS else 256, ready=None if j else ready)
                if 2 <= j < 6:
                    heads_norm_pe(pe, 2, l * 14 + 2 * (j - 2), first=(j == 2))
                if j == IN_CQK:
                    pe.wait_ge(evac[0], n_evac(l, 0, OFF_IN) + IN_ROWS // 2 + 1)
                    te.matmul(ps[:, 4, :], pkt[64:80, PK_UP:PK_UP + P], rows[64:80, :], start=True, stop=True).then_inc(s["ga_ps"], 1)
                if j == IN_Z:
                    pe.wait_ge(s["sg_pool"], l * 3 + 3)
                    for a in range(2):
                        for t in range(4):
                            for b in range(2):
                                h = 2 * a + b
                                mm = te.matmul(ps[64 * b:64 * b + 64, 6 + a, t * P:(t + 1) * P], av[:, t, 64 * h:64 * h + 64],
                                               sgw[:, h, :], start=True, stop=True)
                        mm.then_inc(s["sg_ps"], 1)

        def in_products_act(l, act, round_chunk):
            ac = nc.scalar
            into = {IN_AU: (au, ACT.Gelu_apprx_tanh), IN_AV: (av, ACT.Gelu_apprx_tanh), IN_Z: (zs[:, 0:2, :], ACT.Silu),
                    IN_Z + 1: (zs[:, 2:4, :], ACT.Silu), IN_CR: (cr, ACT.Silu)}
            for j in range(INP):
                p = j % 2
                n = c_no(l, OFF_IN) + j
                act.wait_ge(s["used"], n + 1)
                if j in into:
                    dst, fn = into[j]
                    if j == IN_AV:
                        src = ps[:, 2 * p:2 * p + 2, :].rearrange("p a (b c) -> p (a b) c", b=2)
                    else:
                        src = ps[:, 2 * p:2 * p + 2, :]
                    ac.activation(dst[:, :, :], src, fn).then_inc(evac[p], 1)
                if j < 6:
                    for k in range(2):
                        t = 2 * j + k
                        ac.activation(qkv[:, t, :], ps[:, 2 * p + k, :], ACT.Copy, scale=pkt[:, PK_CONV + 4 * t + 3:PK_CONV + 4 * t + 4]).then_inc(s["conv_a"], 1)
                round_chunk(n + 2, p)
                if 1 <= j <= 6:
                    conv_silu(l, act, j - 1)
                if 1 <= j < 5:
                    act.wait_ge(s["conv_s"], l * 6 + j)
                    norm_squares(act, qk_tiles()[2 * j - 2:2 * j], l * 14 + 2 * (j - 1), first=(j == 1))
                if 2 <= j < 6:
                    norm_roots(act, 2, l * 14 + 2 * (j - 2), 64.0, eps_col("eps_l2"), first=(j == 2))
                if j == IN_CQK:
                    gates_act(l, act)
                if j == IN_AU:
                    act.wait_ge(s["ga_dve"], l * 16 + 3)
                    ac.activation(tmp[:, 0, :], bcum[:, :], ACT.Exp, scale=1 / 16).then_inc(s["ga_act"], 1)
                    ac.activation(tmp[:, 1, :], bcum[:, :], ACT.Exp, scale=-1 / 16).then_inc(s["ga_act"], 1)
                    ac.activation(gtA[:, :], chunks(bcum[:, :])[:, :, 63], ACT.Exp, scale=1 / 16).then_inc(s["ga_act"], 1)
                    act.wait_ge(s["ga_dve"], l * 16 + 4)
                    ac.activation(tmp[:, 2, :], tmp[:, 2, :], ACT.Exp, scale=1 / 16).then_inc(s["ga_act"], 1)
                if j == IN_CR:
                    act.wait_ge(s["sg_dve"], l * 16 + 8)
                    ac.activation(sgt[:, :], mv[:, :, 1], ACT.Sqrt, bias=eps_col("eps2")).then_inc(s["sg_act"], 1)

        def gates_act(l, act):
            ac = nc.scalar
            act.wait_ge(s["ga_ps"], l + 1)
            ac.activation(la[:, :], ps[:, 4, :], ACT.Abs, bias=pkt[:, PK_GB:PK_GB + 1]).then_inc(s["ga_act"], 1)
            act.wait_ge(evac[0], n_evac(l, 0, OFF_IN) + IN_ROWS // 2 + 1)
            ac.activation(tmp[32:40, 3, :], rows[32:40, :], ACT.Abs, bias=pkt[32:40, PK_DT:PK_DT + 1]).then_inc(s["gt_act"], 1)
            act.wait_ge(s["ga_act"], l * 7 + 1)
            ac.activation(la[:, :], la[:, :], ACT.Exp, scale=-1.0).then_inc(s["ga_act"], 1)
            act.wait_ge(s["gt_act"], l * 5 + 1)
            ac.activation(tmp[32:40, 3, :], tmp[32:40, 3, :], ACT.Exp, scale=-1.0).then_inc(s["gt_act"], 1)
            ac.activation(nega[32:40, 0:1], pkt[32:40, PK_ALOG:PK_ALOG + 1], ACT.Exp).then_inc(s["gt_act"], 1)
            act.wait_ge(s["ga_act"], l * 7 + 2)
            ac.activation(la[:, :], la[:, :], ACT.Ln, bias=1.0).then_inc(s["ga_act"], 1)
            act.wait_ge(s["gt_act"], l * 5 + 2)
            ac.activation(tmp[32:40, 3, :], tmp[32:40, 3, :], ACT.Ln, bias=1.0).then_inc(s["gt_act"], 1)

        def conv_silu(l, act, q):
            act.wait_ge(evac[q % 2], n_evac(l, q % 2, OFF_IN) + q // 2 + 1)
            nc.scalar.activation(qkv[:, 2 * q:2 * q + 2, :], qkv[:, 2 * q:2 * q + 2, :], ACT.Silu).then_inc(s["conv_s"], 1)

        def in_products_dve(l, dve, rest_chunk):
            ve = nc.vector
            for j in range(INP):
                p = j % 2
                n = c_no(l, OFF_IN) + j
                if j in (IN_ROWS, IN_CQK, IN_CV):
                    dve.wait_ge(s["used"], n + 1)
                    banks = ps[:, 2 * p:2 * p + 2, :]
                    if j == IN_CQK:
                        ve.tensor_copy(cqk[:, :, :], banks).then_inc(evac[p], 1)
                    if j == IN_CV:
                        ve.tensor_copy(cv[:, :, :], banks.rearrange("p a (b c) -> p (a b) c", b=2)).then_inc(evac[p], 1)
                    if j == IN_ROWS:
                        ve.tensor_copy(rows[:, :], ps[:, 2 * p, :]).then_inc(evac[p], 1)
                if j < 6:
                    q = j
                    m = 0
                    for tap in (2, 1, 0):
                        for k in range(2):
                            t = 2 * q + k
                            sh = 3 - tap
                            if tap == 2:
                                dve.wait_ge(s["conv_a"], l * 12 + 2 * q + k + 1)
                            else:
                                dve.wait_ge(s["conv_d"], l * 30 + 5 * q + m - 1)
                            y = qkv[:, t, sh:TOK]
                            m += 1
                            c = PK_CONV + 4 * t + tap
                            ve.scalar_tensor_tensor(out=y, in0=ps[:, 2 * p + k, 0:TOK - sh], scalar=pkt[:, c:c + 1], in1=y,
                                                    op0=ALU.mult, op1=ALU.add).then_inc(*((s["conv_d"], 1) if m < 6 else (evac[p], 1)))
                if 2 <= j < 6:
                    q = j - 2
                    heads_norm_dve(dve, qk_tiles()[2 * q:2 * q + 2], [0.125 if q < 2 else 1.0] * 2, l * 14 + 2 * q, first=(q == 0))
                if j == IN_CV:
                    gates_dve(l, dve)
                if j == IN_AU:
                    decayed_qk(l, dve)
                if j == IN_CR:
                    spatial_norm(l, dve)


        def gates_dve(l, dve):
            ve = nc.vector
            a0 = l * 16
            dve.wait_ge(s["ga_act"], l * 7 + 3)
            ve.tensor_scalar(bcum[:, :], ps[:, 4, :], pkt[:, PK_GB:PK_GB + 1], 0.0, ALU.add, ALU.min).then_inc(s["ga_dve"], 1)
            dve.wait_ge(s["ga_dve"], a0 + 1)
            ve.tensor_tensor(la[:, :], bcum[:, :], la[:, :], ALU.subtract).then_inc(s["ga_dve"], 1)
            dve.wait_ge(s["ga_dve"], a0 + 2)
            ve.tensor_tensor_scan(bcum[:, :], C("keep"), la[:, :], 0.0, ALU.mult, ALU.add).then_inc(s["ga_dve"], 1)
            dve.wait_ge(s["ga_dve"], a0 + 3)
            ve.tensor_tensor(chunks(tmp[:, 2, :]), chunks(bcum[:, :])[:, :, 63].unsqueeze(2).to_broadcast([P, NCH, CH]), chunks(bcum[:, :]),
                             ALU.subtract).then_inc(s["ga_dve"], 1)
            dve.wait_ge(s["gt_act"], l * 5 + 4)
            ve.tensor_scalar(rows[32:40, :], rows[32:40, :], pkt[32:40, PK_DT:PK_DT + 1], 0.0, ALU.add, ALU.max).then_inc(s["gt_dve"], 1)
            dve.wait_ge(s["gt_dve"], l * 4 + 1)
            ve.tensor_tensor(rows[32:40, :], rows[32:40, :], tmp[32:40, 3, :], ALU.add).then_inc(s["gt_dve"], 1)
            dve.wait_ge(s["gt_dve"], l * 4 + 2)
            ve.tensor_scalar(rows[32:40, :], rows[32:40, :], nega[32:40, 0:1], -1.0, ALU.mult, ALU.mult).then_inc(s["gt_dve"], 1)
            dve.wait_ge(s["gt_dve"], l * 4 + 3)
            ve.tensor_tensor_scan(gam[32:40, :], C("keep")[32:40, :], rows[32:40, :], 0.0, ALU.mult, ALU.add).then_inc(s["gt_dve"], 1)

        def decayed_qk(l, dve):
            ve = nc.vector
            a0 = l * 16
            dve.wait_ge(s["ga_act"], l * 7 + 5)
            ve.scalar_tensor_tensor(out=cqk[:, 0, :], in0=cqk[:, 0, :], scalar=32.0 ** -0.5, in1=tmp[:, 0, :], op0=ALU.mult, op1=ALU.mult).then_inc(s["ga_dve"], 1)
            ve.tensor_tensor(tmp[:, 1, :], tmp[:, 1, :], cqk[:, 1, :], ALU.mult).then_inc(s["ga_dve"], 1)
            dve.wait_ge(s["ga_act"], l * 7 + 7)
            dve.wait_ge(s["ga_dve"], a0 + 6)
            ve.tensor_tensor(cqk[:, 1, :], cqk[:, 1, :], tmp[:, 2, :], ALU.mult).then_inc(s["ga_dve"], 1)

        def spatial_norm(l, dve):
            ve = nc.vector
            g0 = l * 16
            dve.wait_ge(evac[0], n_evac(l, 0, OFF_IN) + IN_AV // 2 + 1)
            for t in range(4):
                ve.bn_stats(stat[:, t, :], av[:, t, :]).then_inc(s["sg_dve"], 1)
            for t in range(4):
                dve.wait_ge(s["sg_dve"], g0 + t + 1)
                dve.sem_inc(s["apart_dve"], 1)
                ve.bn_aggr(mv[:, t, :], stat[:, t, :]).then_inc(s["sg_dve"], 1)
            dve.wait_ge(s["sg_act"], l + 1)
            ve.reciprocal(sgt[:, :], sgt[:, :]).then_inc(s["sg_dve"], 1)
            dve.wait_ge(s["sg_dve"], g0 + 9)
            for t in range(4):
                ve.tensor_scalar(av[:, t, :], av[:, t, :], mv[:, t, 0:1], sgt[:, t:t + 1], ALU.subtract, ALU.mult).then_inc(s["sg_dve"], 1)

        def norm_squares(act, tiles, n0, first=False, t0=0):
            for t, tile in enumerate(tiles):
                if not first:
                    act.wait_ge(s["hn_ps"], n0 + t - 1)
                nc.scalar.activation(tmp[:, (t0 + t) % 2, :], tile, ACT.Square).then_inc(s["hn_sq"], 1)

        def norm_roots(act, tiles, n0, scale, eps, first=False, t0=0):
            for t in range(tiles):
                act.wait_ge(s["hn_ps"], n0 + t + 1)
                if not first:
                    act.wait_ge(s["hn_rc"], n0 + t - 1)
                nc.scalar.activation(tmp[:, 2 + (t0 + t) % 2, :], ps[:, 6 + (t0 + t) % 2, :], ACT.Sqrt, scale=scale, bias=eps).then_inc(s["hn_std"], 1)

        def heads_norm_act(act, tiles, n0, scale, eps):
            for t in range(len(tiles) + 1):
                if t < len(tiles):
                    norm_squares(act, tiles[t:t + 1], n0 + t, t0=t)
                if t:
                    norm_roots(act, 1, n0 + t - 1, scale, eps, t0=t - 1)

        def heads_norm_pe(pe, n_tiles, n0, first=False):
            for t in range(n_tiles):
                n = n0 + t
                pe.wait_ge(s["hn_sq"], n + 1)
                if not first:
                    pe.wait_ge(s["hn_std"], n - 1)
                nc.tensor.matmul(ps[:, 6 + t % 2, :], C("head_mean"), tmp[:, t % 2, :], start=True, stop=True).then_inc(s["hn_ps"], 1)

        def heads_norm_dve(dve, tiles, factors, n0, then=None, first=False):
            for t in range(len(tiles)):
                n = n0 + t
                dve.wait_ge(s["hn_std"], n + 1)
                if not first:
                    dve.wait_ge(s["hn_d"], n - 1)
                nc.vector.reciprocal(tmp[:, 4 + t % 2, :], tmp[:, 2 + t % 2, :]).then_inc(s["hn_rc"], 1)
                dve.wait_ge(s["hn_rc"], n + 1)
                nc.vector.scalar_tensor_tensor(out=tiles[t], in0=tiles[t], scalar=factors[t], in1=tmp[:, 4 + t % 2, :],
                                               op0=ALU.mult, op1=ALU.mult).then_inc(s["hn_d"], 1)
                if then:
                    dve.wait_ge(s["hn_d"], n + 1)
                    then(t)

        HN = 8 + 2 + 4 + 0

        def qk_tiles():
            return [qkv[:, t, :] for t in range(8)]

        def o_tiles():
            return [oT[:, pr, :] for pr in range(PAIRS)]

        def oA_tiles():
            return [oA[:, a, :] for a in range(2)]

        def mixer_pe(l, pe):
            te = nc.tensor
            hn = l * 14
            for p in range(2):
                pe.wait_ge(evac[p], n_evac(l, p, OFF_IN) + INP // 2)
            pe.wait_ge(s["ga_dve"], l * 16 + 6)
            for c in range(NCH):
                for h in range(4):
                    mm = te.matmul(ps[64 * (c % 2):64 * (c % 2) + 64, h, (c // 2) * CH:(c // 2 + 1) * CH],
                                   tmp[32 * h:32 * h + 32, 1, c * CH:(c + 1) * CH],
                                   cqk[32 * h:32 * h + 32, 0, c * CH:(c + 1) * CH], start=True, stop=True)
            mm.then_inc(s["ga_ps2"], 1)
            pe.wait_ge(s["ga_dve"], l * 16 + 7)
            for t in range(4):
                mm = te.transpose(ps[:, 5, t * P:(t + 1) * P], cqk[:, 1, t * P:(t + 1) * P], C("ident"))
            mm.then_inc(s["ga_ps2"], 1)
            pe.wait_ge(s["ga_act2"], l * 1 + 1)
            pe.wait_ge(s["sg_dve"], l * 16 + 16)
            pe.sem_inc(s["apart_pe"], 1)
            for c in range(NCH):
                b, t = 64 * (c % 2), c // 2
                for h in range(4):
                    mm = te.matmul(ps[32 * h:32 * h + 32, 6 + c % 2, t * CH:(t + 1) * CH], kdA[b:b + 64, t, 32 * h:32 * h + 32],
                                   cv[b:b + 64, t, 64 * h:64 * h + 64], start=True, stop=True)
            mm.then_inc(s["ga_ps2"], 1)
            pe.wait_ge(s["ga_dve"], l * 16 + 16)
            for c in range(NCH):
                b, t = 64 * (c % 2), c // 2
                for h in range(4):
                    dst = ps[64 * (h % 2):64 * (h % 2) + 64, 2 * (h // 2) + c % 2, t * CH:(t + 1) * CH]
                    te.matmul(dst, stA[32 * h:32 * h + 32, c, :], cqk[32 * h:32 * h + 32, 0, c * CH:(c + 1) * CH], start=True, stop=False)
                    mm = te.matmul(dst, cv[b:b + 64, t, 64 * h:64 * h + 64], pA[b:b + 64, h, t, :], start=False, stop=True)
            mm.then_inc(s["ga_ps2"], 1)
            heads_norm_pe(pe, 2, hn + 8)

            pe.wait_ge(s["hn_std"], l * 14 + 10)
            pe.sem_inc(s["apart_pe"], 1)
            for src, b0 in ((kT, 0), (vT, 4)):
                for pr in range(PAIRS):
                    for c in range(NCH):
                        for b in (0, 64):
                            mm = te.matmul(ps[b:b + 64, b0 + pr, c * CH:(c + 1) * CH], src[b:b + 64, pr, c * CH:(c + 1) * CH],
                                           C("eye64")[b:b + 64, :], start=True, stop=True)
                mm.then_inc(s["tok_ps"], 1)
            pe.wait_ge(s["tok_sb"], l * 2 + 2)
            pe.wait_ge(s["gt_dve"], l * 4 + 4)
            pe.wait_ge(s["gt_act"], l * 5 + 5)
            for base_, bank in ((32, 4), (0, 5)):
                for c in range(NCH):
                    for b in range(2):
                        mm = te.matmul(ps[64 * b:64 * b + 64, bank, c * PAIRS:(c + 1) * PAIRS], gam[base_:base_ + 8, c * CH:(c + 1) * CH],
                                       seln[base_:base_ + 8, b, :], start=True, stop=True)
            mm.then_inc(s["col_ps"], 1)
            for pr in range(PAIRS):
                b4 = 4 * (pr % 2)
                if pr == 1:
                    pe.wait_ge(s["col_sb"], l * 2 + 2)
                if pr >= 2:
                    pe.wait_ge(s["dp_dve"], l * 44 + (pr - 2) * 11 + 12)
                te.matmul(ps[:, b4, :], sel[32:40, pr, :], gam[32:40, :], start=True, stop=True)
                te.matmul(ps[:, b4 + 1, :], sel[0:8, pr, :], gam[0:8, :], start=True, stop=True)
                for c in range(NCH):
                    for b in (0, 64):
                        te.matmul(ps[b:b + 64, b4 + 2, c * CH:(c + 1) * CH], kT[b:b + 64, pr, c * CH:(c + 1) * CH],
                                  kT[b:b + 64, pr, c * CH:(c + 1) * CH], start=True, stop=True)
                for c in range(NCH):
                    for b in (0, 64):
                        mm = te.matmul(ps[b:b + 64, b4 + 3, c * CH:(c + 1) * CH], kT[b:b + 64, pr, c * CH:(c + 1) * CH],
                                       qT[b:b + 64, pr, c * CH:(c + 1) * CH], start=True, stop=True)
                mm.then_inc(s["dp_ps"], 1)
            pe.wait_ge(s["dp_dve"], l * 44 + 45)
            pe.sem_inc(s["apart_pe"], 1)

            def level(lev, last):
                for pr in range(PAIRS):
                    pe.wait_ge(s["lv_pool"], l * 20 + lev * 4 + pr + 1)
                    pe.wait_ge(s["lv_dve"], l * LV_DVE + lev * 8 + 2 * pr + 1)
                    pe.sem_inc(s["apart_pe"], 1)
                    for c in range(NCH):
                        for b in (0, 64):
                            mm = te.matmul(ps[b:b + 64, pr, c * CH:(c + 1) * CH], tmp[b:b + 64, pr, c * CH:(c + 1) * CH],
                                           Tm[b:b + 64, pr, c, :], start=True, stop=True)
                    mm.then_inc(s["lv_x"], 1)
                for pr in range(PAIRS):
                    pe.wait_ge(s["lv_act"], l * 20 + lev * 4 + pr + 1)
                    pe.wait_ge(s["lv_dve"], l * LV_DVE + lev * 8 + (pr + 7 if last and pr >= 2 else 2 * pr + 6))
                    pe.sem_inc(s["apart_pe"], 1)
                    for a, (lt, rt) in enumerate(((TT, Xb), (Xb, TT))):
                        if a or not last:
                            for c in range(NCH):
                                for b in (0, 64):
                                    mm = te.matmul(ps[b:b + 64, 4 + 2 * (pr % 2) + a, c * CH:(c + 1) * CH], lt[b:b + 64, pr, c, :],
                                                   rt[b:b + 64, pr, c, :], start=True, stop=True)
                    mm.then_inc(s["lv_t"], 1)
            with pe.Fori(0, 4) as lev:
                level(lev, False)
            level(4, True)
            pe.wait_ge(s["lv_dve"], l * LV_DVE + 8 + LV_DVE)
            pe.wait_ge(s["kv_dve"], l * 6 + 6)
            pe.sem_inc(s["apart_pe"], 1)
            for pr in range(PAIRS):
                for c in range(NCH):
                    for b in (0, 64):
                        mm = te.matmul(ps[b:b + 64, pr, c * CH:(c + 1) * CH], bk[b:b + 64, pr, c, :], TT[b:b + 64, pr, c, :], start=True, stop=True)
            mm.then_inc(s["wu_ps"], 1)
            for pr in range(PAIRS):
                for c in range(NCH):
                    for b in (0, 64):
                        mm = te.matmul(ps[b:b + 64, 4 + pr, c * CH:(c + 1) * CH], TT[b:b + 64, pr, c, :], vN[b:b + 64, pr, c, :], start=True, stop=True)
            mm.then_inc(s["wu_ps"], 1)
            pe.wait_ge(s["wu_sb"], l * 2 + 2)
            pe.sem_inc(s["apart_pe"], 1)
            HEADS = [(pr, b) for pr in range(PAIRS) for b in (0, 64)]
            for c in range(NCH):
                st = state[:, c % 2]
                pe.wait_ge(s["rc_st"], l * 9 + c + 1)
                pe.sem_inc(s["apart_pe"], 1)
                for pr, b in HEADS:
                    mm = te.matmul(ps[b:b + 64, 0, pr * CH:(pr + 1) * CH], nwT[b:b + 64, pr, c, :], st[b:b + 64, pr, :], start=True, stop=True)
                mm.then_inc(s["rc_u"], 1)
                if c >= 2:
                    pe.wait_ge(s["rc_ov"], l * 8 + c - 1)
                    pe.sem_inc(s["apart_pe"], 1)
                out_at = [ps[b:b + 64, 1 + c % 2, pr * CH:(pr + 1) * CH] for pr, b in HEADS]
                for dst, (pr, b) in zip(out_at, HEADS):
                    te.matmul(dst, st[b:b + 64, pr, :], qT[b:b + 64, pr, c * CH:(c + 1) * CH], start=(pr == 0), stop=False)
                pe.wait_ge(s["rc_un"], l * 8 + c + 1)
                pe.sem_inc(s["apart_pe"], 1)
                for pr, b in HEADS:
                    mm = te.matmul(ps[b:b + 64, 3, pr * CH:(pr + 1) * CH], kN[b:b + 64, pr, c, :], unew[b:b + 64, pr, :], start=True, stop=True)
                mm.then_inc(s["rc_ds"], 1)
                for dst, (pr, b) in zip(out_at, HEADS):
                    mm = te.matmul(dst, unew[b:b + 64, pr, :], pT[b:b + 64, pr, c, :], start=False, stop=(pr == PAIRS - 1))
                mm.then_inc(s["rc_o"], 1)
            heads_norm_pe(pe, 4, hn + 10)

        def mixer_act(l, act):
            ac = nc.scalar
            hn = l * 14
            act.wait_ge(s["ga_ps2"], l * 4 + 2)
            ac.activation(kdA[:, :, :].rearrange("p a b -> p (a b)"), ps[:, 5, :], ACT.Copy).then_inc(s["ga_act2"], 1)
            act.wait_ge(s["ga_ps2"], l * 4 + 4)
            for a in range(2):
                for b in range(2):
                    ac.activation(oA[:, a, :].rearrange("p (t b i) -> p b t i", b=2, i=CH)[:, b], ps[:, 2 * a + b, 0:256].rearrange("p (t i) -> p t i", i=CH),
                                  ACT.Copy).then_inc(s["ga_o"], 1)
            act.wait_ge(s["ga_o"], l * 4 + 4)
            heads_norm_act(act, oA_tiles(), hn + 8, 1.0, eps_col("eps2"))
            ac.activation(gam[0:8, :], rows[0:8, :], ACT.Sigmoid).then_inc(s["gt_act"], 1)
            mix_hi(l, act, ((0, au[:, 0, :], "mixA", 1), (1, au[:, 1, :], "mixA", 2), (6, cr[:, 0, :], "mixC", 1), (7, cr[:, 1, :], "mixC", 2)), 0)

            act.wait_ge(s["tok_ps"], l * 2 + 1)
            ac.activation(kN[:, :, :, :], ps[:, 0:4, :].rearrange("p a (c t) -> p a c t", t=CH), ACT.Copy).then_inc(s["tok_sb"], 1)
            for pr in range(PAIRS):
                b4, d0 = 4 * (pr % 2), l * 44 + pr * 11 + 1
                act.wait_ge(s["dp_dve"], d0 + 2)
                ac.activation(tmp[:, 1, :], ps[:, b4, :], ACT.Exp).then_inc(s["dp_act"], 1)
                act.wait_ge(s["dp_dve"], d0 + 3)
                ac.activation(tmp[:, 2, :], tmp[:, 2, :], ACT.Exp).then_inc(s["dp_act"], 1)
                act.wait_ge(s["dp_dve"], d0 + 4)
                ac.activation(tmp[:, 0, :], tmp[:, 0, :], ACT.Exp, scale=-1.0).then_inc(s["dp_act"], 1)
            act.wait_ge(s["dp_dve"], l * 44 + 45)
            ac.activation(gtot[:, :, :], glast[:, :, :], ACT.Exp).then_inc(s["kv_act"], 1)
            ac.activation(egN[:, :, :], gN[:, :, :], ACT.Exp).then_inc(s["kv_act"], 1)
            act.wait_ge(s["kv_dve"], l * 6 + 1)
            ac.activation(kdN[:, :, :], kdN[:, :, :], ACT.Exp).then_inc(s["kv_act"], 1)
            with act.Fori(0, 5) as lev:
                for pr in range(PAIRS):
                    act.wait_ge(s["lv_x"], l * 20 + lev * 4 + pr + 5)
                    act.wait_ge(s["lv_t"], l * 20 + lev * 4 + pr + 1)
                    ac.activation(Xb[:, pr, :, :], chunks(ps[:, pr, :]), ACT.Copy).then_inc(s["lv_act"], 1)
            act.wait_ge(s["wu_ps"], l * 2 + 1)
            ac.activation(nwT[:, :, :, :], ps[:, 0:4, :].rearrange("p a (c t) -> p a c t", t=CH), ACT.Copy, scale=-1.0).then_inc(s["wu_sb"], 1)
            for c in range(NCH):
                act.wait_ge(s["rc_o"], l * 8 + c + 1)
                ac.activation(oT[:, :, c * CH:(c + 1) * CH], ps[:, 1 + c % 2, 0:256].rearrange("p (a t) -> p a t", t=CH), ACT.Copy).then_inc(s["rc_ov"], 1)
            act.wait_ge(s["rc_ov"], l * 8 + 8)
            act.wait_ge(s["rc_st"], l * 9 + 9)
            heads_norm_act(act, o_tiles(), hn + 10, 1.0, eps_col("eps2"))
            mix_hi(l, act, [(2 + pr, oT[:, pr, :], "mixB", pr + 1) for pr in range(PAIRS)], 4)

        def mix_hi(l, act, tiles, n0):
            for m, (k, src, name, n) in enumerate(tiles):
                act.wait_ge(s[name], l * {"mixA": 2, "mixB": 4, "mixC": 2}[name] + n)
                nc.scalar.activation(xh[:, k, :], src, ACT.Copy).then_inc(s["mix_hi"], 1)

        def mix_rest(l, pool, tiles, n0):
            for m, (k, src) in enumerate(tiles):
                pool.wait_ge(s["mix_hi"], l * 8 + n0 + m + 1)
                nc.gpsimd.tensor_tensor(xl[:, k, :], src, xh[:, k, :].bitcast(F32), ALU.subtract).then_inc(s["mix_lo"], 1)

        def mixer_pool(l, pool):
            gp = nc.gpsimd
            for j in range(IN_CR + 1):
                rest(pool, c_no(l, OFF_IN) + j + 2, j % 2)
                if j == 2:
                    pool.wait_ge(s["sgp_in"], l * 16 + 16)
                    gp.tensor_tensor(sgw, sgw, C("upper128").unsqueeze(1).to_broadcast([P, 4, P]), ALU.mult).then_inc(s["sg_pool"], 1)
            pool.wait_ge(s["sg_dve"], l * 16 + 13)
            gp.tensor_tensor(av[:, :, :], av[:, :, :], sgp[:, SG_G:SG_G + 256].unsqueeze(1).to_broadcast([P, 4, 256]), ALU.mult).then_inc(s["sg_pool"], 1)
            pool.wait_ge(s["sg_pool"], l * 3 + 2)
            gp.tensor_tensor(av[:, :, :], av[:, :, :], sgp[:, SG_B:SG_B + 256].unsqueeze(1).to_broadcast([P, 4, 256]), ALU.add).then_inc(s["sg_pool"], 1)
            for j in (IN_Z, IN_Z + 1):
                rest(pool, c_no(l, OFF_IN) + j + 2, j % 2)
            mix_rest(l, pool, ((0, au[:, 0, :]), (1, au[:, 1, :]), (6, cr[:, 0, :]), (7, cr[:, 1, :])), 0)
            for pr in range(PAIRS):
                d0 = l * 44 + pr * 11 + 1
                p0 = l * 24 + pr * 6 + 1
                pool.wait_ge(s["dp_dve"], d0 + 6)
                gp.tensor_tensor(pT[:, pr], pT[:, pr], bc(C("upper64")), ALU.mult).then_inc(s["dp_pool"], 1)
                pool.wait_ge(s["dp_act"], l * 12 + pr * 3 + 2)
                pool.wait_ge(s["dp_pool"], p0)
                gp.tensor_tensor(chunks(tmp[:, 3, :]), chunks(tmp[:, 2, :]), bc(C("strict64")), ALU.mult).then_inc(s["dp_pool"], 1)
                pool.wait_ge(s["dp_dve"], d0 + 8)
                gp.tensor_tensor(chunks(tmp[:, 5, :]), LT[:, pr], bc(C("upT1")), ALU.mult).then_inc(s["dp_pool"], 1)
                pool.wait_ge(s["dp_pool"], p0 + 3)
                gp.tensor_tensor(TT[:, pr], bc(C("eye64")), chunks(tmp[:, 5, :]), ALU.subtract).then_inc(s["dp_pool"], 1)
                pool.wait_ge(s["dp_dve"], d0 + 10)
                gp.tensor_tensor(chunks(tmp[:, 4, :]), chunks(tmp[:, 4, :]), bc(C("low1")), ALU.mult).then_inc(s["dp_pool"], 1)
                pool.wait_ge(s["dp_pool"], p0 + 5)
                gp.tensor_tensor(Tm[:, pr], bc(C("eye64")), chunks(tmp[:, 4, :]), ALU.subtract).then_inc(s["dp_pool"], 1)
            a0 = CONST_AT["upT2"][0]
            with pool.Fori(0, 5) as lev:
                for pr in range(PAIRS):
                    pool.wait_ge(s["lv_x"], l * 20 + lev * 4 + pr + 1)
                    pool.sem_inc(s["apart_pool"], 1)
                    gp.tensor_tensor(chunks(tmp[:, pr, :]), LT[:, pr], bc(cst[:, bass.ds(lev * 64 + a0, 64)]), ALU.mult).then_inc(s["lv_pool"], 1)
            mix_rest(l, pool, [(2 + pr, oT[:, pr, :]) for pr in range(PAIRS)], 4)

        def mixer_dve(l, dve):
            ve = nc.vector
            hn = l * 14
            g0 = l * 16
            a0 = l * 16
            for a in range(2):
                dve.wait_ge(s["sg_ps"], l * 2 + a + 1)
                z4 = ps[:, 6 + a, :].rearrange("p (t i) -> p t i", i=P)
                bs = sgp[:, SG_BS + a * P:SG_BS + (a + 1) * P].unsqueeze(1).to_broadcast([P, 4, P])
                ve.tensor_tensor(z4, z4, bs, ALU.add).then_inc(s["sg_dve"], 1)
                dve.wait_ge(s["sg_dve"], g0 + 14 + a)
                ve.tensor_tensor(au[:, a, :], au[:, a, :], ps[:, 6 + a, :], ALU.mult).then_inc(s["mixA"], 1)
            dve.wait_ge(s["mixA"], l * 2 + 2)
            ve.memset(stA[:, 0, :], 0.0).then_inc(s["sg_dve"], 1)
            dve.wait_ge(s["ga_ps2"], l * 4 + 1)
            up4 = C("upper64").unsqueeze(1).to_broadcast([P, 16, CH])
            for h in range(4):
                ve.tensor_tensor(pA[:, h], ps[:, h, 0:256].rearrange("p (t i) -> p t i", i=CH), up4[:, 0:4, :], ALU.mult).then_inc(*((s["ga_dve"], 1) if h == 3 else (s["ga_pA"], 1)))
            dve.wait_ge(s["ga_ps2"], l * 4 + 3)
            for c in range(NCH - 1):
                ve.scalar_tensor_tensor(out=stA[:, c + 1, :], in0=stA[:, c, :], scalar=gtA[:, c:c + 1], in1=ps[:, 6 + c % 2, (c // 2) * CH:(c // 2 + 1) * CH],
                                        op0=ALU.mult, op1=ALU.add).then_inc(s["ga_dve"], 1)
                dve.wait_ge(s["ga_dve"], a0 + 9 + c)
            ve.memset(state[:, 0], 0.0).then_inc(s["rc_st"], 1)
            ve.memset(nega[0:1, 1:2], 0.0).then_inc(s["ga_dve"], 1)

            def gate(a):
                ve.tensor_tensor(cr[:, a, :], cr[:, a, :], oA[:, a, :], ALU.mult).then_inc(s["mixC"], 1)
            heads_norm_dve(dve, oA_tiles(), [pkt[:, PK_LAN:PK_LAN + 1]] * 2, hn + 8, gate)

            dve.wait_ge(s["tok_ps"], l * 2 + 2)
            dve.wait_ge(s["mixC"], l * 2 + 2)
            ve.tensor_copy(vN[:, :, :, :], ps[:, 4:8, :].rearrange("p a (c t) -> p a c t", t=CH)).then_inc(s["tok_sb"], 1)
            dve.wait_ge(s["col_ps"], l + 1)
            ve.tensor_copy(gN[:, :, :].rearrange("p a b -> p (a b)"), ps[:, 4, 0:32]).then_inc(s["col_sb"], 1)
            ve.tensor_copy(bN[:, :, :].rearrange("p a b -> p (a b)"), ps[:, 5, 0:32]).then_inc(s["col_sb"], 1)
            dve.wait_ge(s["col_sb"], l * 2 + 2)
            for pr in range(PAIRS):
                b4, d0 = 4 * (pr % 2), l * 44 + pr * 11 + 1
                a1 = l * 12 + pr * 3
                p0 = l * 24 + pr * 6 + 1
                R, bR, kk, qk = (chunks(ps[:, b4 + m, :]) for m in range(4))

                def done(n):
                    dve.wait_ge(s["dp_dve"], d0 + n)
                dve.wait_ge(s["dp_ps"], l * 4 + pr + 1)
                done(0)
                ve.tensor_tensor(chunks(tmp[:, 0, :]), R, col(gN[:, :, pr]), ALU.subtract).then_inc(s["dp_dve"], 1)
                ve.tensor_copy(glast[:, :, pr], R[:, :, 63]).then_inc(s["dp_dve"], 1)
                done(1)
                dve.wait_ge(s["dp_pool"], p0)
                ve.tensor_scalar(tmp[:, 2, :], tmp[:, 0, :], 0.0, None, ALU.min).then_inc(s["dp_dve"], 1)
                done(3)
                ve.tensor_scalar(tmp[:, 0, :], tmp[:, 0, :], 0.0, None, ALU.max).then_inc(s["dp_dve"], 1)
                dve.wait_ge(s["dp_act"], a1 + 1)
                ve.tensor_tensor(qT[:, pr, :], qT[:, pr, :], tmp[:, 1, :], ALU.mult).then_inc(s["dp_dve"], 1)
                dve.wait_ge(s["dp_act"], a1 + 2)
                ve.tensor_tensor(pT[:, pr], qk, chunks(tmp[:, 2, :]), ALU.mult).then_inc(s["dp_dve"], 1)
                dve.wait_ge(s["dp_pool"], p0 + 2)
                ve.tensor_tensor(chunks(tmp[:, 3, :]), chunks(tmp[:, 3, :]), bR, ALU.mult).then_inc(s["dp_dve"], 1)
                done(7)
                ve.tensor_tensor(LT[:, pr], chunks(tmp[:, 3, :]), kk, ALU.mult).then_inc(s["dp_dve"], 1)
                dve.wait_ge(s["dp_act"], a1 + 3)
                ve.tensor_tensor(chunks(tmp[:, 0, :]), chunks(tmp[:, 0, :]), col(bN[:, :, pr]), ALU.mult).then_inc(s["dp_dve"], 1)
                done(9)
                ve.tensor_tensor(chunks(tmp[:, 4, :]), chunks(tmp[:, 0, :]), kk, ALU.mult).then_inc(s["dp_dve"], 1)
                dve.wait_ge(s["dp_pool"], p0 + 6)
                ve.memset(nega[0:1, 2:3], 0.0).then_inc(s["dp_dve"], 1)
            k0 = l * 6
            ve.tensor_tensor(kdN[:, :, :], glast[:, :, :], gN[:, :, :], ALU.subtract).then_inc(s["kv_dve"], 1)
            dve.wait_ge(s["kv_act"], l * 3 + 2)
            ve.tensor_tensor(bgN[:, :, :], bN[:, :, :], egN[:, :, :], ALU.mult).then_inc(s["kv_dve"], 1)

            def by_token(v):
                return v[:, :, :].rearrange("p c a -> p a c").unsqueeze(3).to_broadcast([P, PAIRS, NCH, CH])
            dve.wait_ge(s["kv_dve"], k0 + 2)
            ve.tensor_tensor(bk[:, :, :, :], kN[:, :, :, :], by_token(bgN), ALU.mult).then_inc(s["kv_dve"], 1)
            dve.wait_ge(s["kv_act"], l * 3 + 3)
            dve.wait_ge(s["kv_dve"], k0 + 3)
            ve.tensor_tensor(kN[:, :, :, :], kN[:, :, :, :], by_token(kdN), ALU.mult).then_inc(s["kv_dve"], 1)
            ve.tensor_tensor(vN[:, :, :, :], vN[:, :, :, :], by_token(bN), ALU.mult).then_inc(s["kv_dve"], 1)
            ve.memset(nega[0:1, 3:4], 0.0).then_inc(s["kv_dve"], 1)

            def level(lev, last):
                for pr in range(PAIRS):
                    dve.wait_ge(s["lv_t"], l * 20 + lev * 4 + pr + 5)
                    for a, M in enumerate((Tm, TT)):
                        if a or not last:
                            ve.tensor_tensor(M[:, pr], M[:, pr], chunks(ps[:, 4 + 2 * (pr % 2) + a, :]), ALU.subtract).then_inc(s["lv_dve"], 1)
            with dve.Fori(0, 4) as lev:
                level(lev, False)
            level(4, True)
            dve.wait_ge(s["wu_ps"], l * 2 + 2)
            ve.tensor_copy(ub[:, :, :, :], ps[:, 4:8, :].rearrange("p a (c t) -> p a c t", t=CH)).then_inc(s["wu_sb"], 1)
            dve.wait_ge(s["wu_sb"], l * 2 + 2)
            for c in range(NCH):
                dve.wait_ge(s["rc_u"], l * 8 + c + 1)
                if c:
                    dve.wait_ge(s["rc_o"], l * 8 + c)
                ve.tensor_tensor(unew[:, :, :], ub[:, :, c, :], ps[:, 0, 0:256].rearrange("p (a t) -> p a t", t=CH), ALU.add).then_inc(s["rc_un"], 1)
                dve.wait_ge(s["rc_st"], l * 9 + c + 1)
                if c:
                    dve.wait_ge(s["rc_sg"], l * 8 + c)
                ve.tensor_tensor(tmp[:, 0, 0:256].rearrange("p (a t) -> p a t", t=CH), state[:, c % 2], gtot[:, c, :].unsqueeze(2).to_broadcast([P, PAIRS, CH]),
                                 ALU.mult).then_inc(s["rc_sg"], 1)
                dve.wait_ge(s["rc_sg"], l * 8 + c + 1)
                dve.wait_ge(s["rc_ds"], l * 8 + c + 1)
                ve.tensor_tensor(state[:, (c + 1) % 2], tmp[:, 0, 0:256].rearrange("p (a t) -> p a t", t=CH), ps[:, 3, 0:256].rearrange("p (a t) -> p a t", t=CH),
                                 ALU.add).then_inc(s["rc_st"], 1)

            def gate_z(pr):
                ve.tensor_tensor(oT[:, pr, :], oT[:, pr, :], zs[:, pr, :], ALU.mult).then_inc(s["mixB"], 1)
            dve.wait_ge(s["rc_ov"], l * 8 + 8)
            heads_norm_dve(dve, o_tiles(), [pkt[:, PK_GN:PK_GN + 1]] * 4, hn + 10, gate_z)


        def view(v, r):
            return v.rearrange("p (l r) -> p r l", r=r)

        def own(v, r):
            return v.rearrange("p (r l) -> p r l", r=r)

        def key_tiles(g, i):
            return [j for j in (i - 1, i, i + 1) if 0 <= j < 4] if WIDE[g] else [i]

        def bias_of(g, h, i):
            if not WIDE[g]:
                return (bt1, bt2)[g == 3][:, h, :]
            a = P if i == 0 else 0
            return btw[:, h, a:a + P * len(key_tiles(g, i))]

        def rest(pool, n, p):
            pool.wait_ge(s["hi_done"], n + 1)
            pool.wait_ge(s["lo_done"], n)
            nc.gpsimd.tensor_tensor(wl[:, p, :], raw[:, p, :], wh[:, p, :].bitcast(F32), ALU.subtract).then_inc(s["lo_done"], 1)

        def block1_pool(pool):
            gp = nc.gpsimd
            pool.dma_start(relb[0:32, :], rel).then_inc(s["b_rel"], 16)
            pool.dma_start(pk1[:, :], p1).then_inc(s["b_par"], 16)
            for k in range(KT):
                pool.wait_ge(s["b_hh"], k + 1)
                gp.tensor_tensor(xl[:, k, :], hb[:, k % 4, :], xh[:, k, :].bitcast(F32), ALU.subtract).then_inc(s["b_hl"], 1)
            pool.wait_ge(s["b_row"], 2)
            for g in range(4):
                src = brow[8 * (g % 2):8 * (g % 2) + 8, g // 2, :].unsqueeze(1).to_broadcast([8, P, 512])
                pool.dma_start(scr[g].rearrange("m h r -> h m r"), src).then_inc(s["b_scr"], 16)
            for n in range(2):
                rest(pool, n + 2, n)
            pool.wait_ge(s["b_scr"], 64)

            def toeplitz(g, dst, p0, n, m0, m, first):
                src = bass.AP(scr_t, g * P * 8 * 512 + first, [[8 * 512 - 1, n], [512, 8], [1, m]])
                return pool.dma_start(dst[p0:p0 + n, :, m0:m0 + m], src)
            toeplitz(0, btw, 0, P, 0, 384, 127).then_inc(s["b_bw"], 16)
            toeplitz(2, bt1, 0, P, 0, P, 127).then_inc(s["b_b1"], 16)
            toeplitz(3, bt2, 0, P, 0, P, 127).then_inc(s["b_b2"], 16)
            n = 0
            for gi, g in enumerate(ORDER):
                for kind in KINDS[g]:
                    if n >= 2:
                        rest(pool, n + 2, n % 2)
                    n += 1
                if gi == 0:
                    pool.wait_ge(s["at_l"], 32)
                    toeplitz(1, btw, 0, P, 0, 384, 127).then_inc(s["b_bw"], 16)
            for pr in range(PAIRS):
                pool.wait_ge(s["y_w"], 4 * pr + 4)
                gp.tensor_tensor(og[:, 1, pr, :], og[:, 1, pr, :], og[:, 2, pr, :], ALU.add).then_inc(s["y_s"], 1)
                pool.wait_ge(s["y_s"], 2 * pr + 1)
                gp.tensor_tensor(og[:, 1, pr, :], og[:, 1, pr, :], og[:, 3, pr, :], ALU.add).then_inc(s["y_s"], 1)
                for b in range(2):
                    k = 2 * pr + b
                    pool.wait_ge(s["y_h"], k + 1)
                    gp.tensor_tensor(yl[:, 4 * b + pr, :], og[:, b, pr, :], yh[:, 4 * b + pr, :].bitcast(F32), ALU.subtract).then_inc(s["y_l"], 1)
            for f in range(4):
                pool.wait_ge(s["mg_h"], f + 1)
                gp.tensor_tensor(ml[:, 2 * f:2 * f + 2, :], mt[:, 2, :, :], mh[:, 2 * f:2 * f + 2, :].bitcast(F32), ALU.subtract).then_inc(s["mg_l"], 1)
            for k in range(KT):
                pool.wait_ge(s["x1_h"], k + 1)
                gp.tensor_tensor(xl[:, k, :], x[:, k, :], xh[:, k, :].bitcast(F32), ALU.subtract).then_inc(xr[k % 2], 1)

        X_SLOT = (0, 1, 3, 5)

        def block1_act(act, round_chunk):
            ac = nc.scalar

            def first_chunk(p):
                act.wait_ge(landed[p], 16)
                ac.activation(wh[:, p, :], raw[:, p, :], ACT.Copy).then_inc(s["hi_done"], 1)
            act.wait_ge(s["x_in"], 16)
            for k in range(KT):
                if k >= 4:
                    act.wait_ge(s["b_ms"], k - 3)
                ac.activation(bsq[:, X_SLOT[k % 4], :], x[:, k, :], ACT.Square).then_inc(s["b_x2"], 1)
            first_chunk(0)
            act.wait_ge(s["b_ms"], KT)
            act.wait_ge(s["eps"], 4)
            ac.activation(bsq[:, 2, :], ps[:, 5, :], ACT.Sqrt, bias=eps_col("eps_l2")).then_inc(s["b_xs"], 1)
            first_chunk(1)
            for k in range(KT):
                act.wait_ge(s["b_h"], k + 1)
                ac.activation(xh[:, k, :], hb[:, k % 4, :], ACT.Copy).then_inc(s["b_hh"], 1)
            n = tile = u = 0
            for g in ORDER:
                for kind in KINDS[g]:
                    p = n % 2
                    act.wait_ge(s["used"], n + 1)
                    if kind[0] != "v":
                        for t in range(2):
                            if tile + t >= 2:
                                act.wait_ge(s["b_hm"], tile + t - 1)
                            ac.activation(bsq[:, (tile + t) % 2, :], ps[:, 2 * p + t, :], ACT.Square).then_inc(s["b_sq"], 1)
                    round_chunk(n + 2, p)
                    if kind[0] != "v":
                        for t in range(2):
                            m = tile + t
                            act.wait_ge(s["b_hm"], m + 1)
                            if m >= 2:
                                act.wait_ge(s["b_rc"], m - 1)
                            ac.activation(bsq[:, 2 + m % 2, :], ps[:, 6 + m % 2, :], ACT.Sqrt, bias=eps_col("eps_l2")).then_inc(s["b_sd"], 1)
                        tile += 2
                    n += 1
                act.wait_ge(s["b_scr"], 64)
                for h in range(8):
                    for i in range(4):
                        w = P * len(key_tiles(g, i))
                        c = i * 8 + h
                        act.wait_ge(s["at_l"], u + 1)
                        if u >= 3:
                            act.wait_ge(s["at_t"], u - 2)
                        ac.activation(pb[:, u % 3, 0:w], lg[:, u % 2, 0:w], ACT.Exp, scale=-1.0, bias=nmc[:, g, c:c + 1],
                                      accum_out=lc[:, g, c:c + 1]).then_inc(s["at_p"], 1)
                        u += 1
                        if h >= 2 and h % 2 == 0 and i == 3:
                            out_pair(act, g, u - 4, h // 2 - 1)
                out_pair(act, g, u, 3)
            act.wait_ge(s["st_ps"], 8)
            for g in range(4):
                ac.activation(view(rw[0:8, g, :], VIEW[g]), own(ps[0:8, g, :], VIEW[g]), ACT.Copy).then_inc(s["st_a"], 1)
            act.wait_ge(s["st_d"], 4 + 5)
            ac.activation(rw[0:8, 9:12, :], rw[0:8, 9:12, :], ACT.Exp).then_inc(s["st_e"], 1)
            ac.activation(rw[0:8, 8, :], rw[0:8, 8, :], ACT.Exp).then_inc(s["st_e"], 1)
            ac.activation(sgl[0:8, 0, :], sgl[0:8, 0, :], ACT.Exp, bias=pk1[0:8, P1_SINK:P1_SINK + 1]).then_inc(s["st_e"], 1)
            for half in range(2):
                for b in range(2):
                    p = n % 2
                    act.wait_ge(s["used"], n + 1)
                    if half:
                        act.wait_ge(s["y_d"], 4)
                    ac.activation(zg[:, 2 * b:2 * b + 2, :], ps[:, 2 * p:2 * p + 2, :], ACT.Silu).then_inc(evac[p], 1)
                    round_chunk(n + 2, p)
                    n += 1
                for pr in (2 * half, 2 * half + 1):
                    for b in range(2):
                        act.wait_ge(s["y_d"], 2 * pr + b + 1)
                        ac.activation(yh[:, 4 * b + pr, :], og[:, b, pr, :], ACT.Copy).then_inc(s["y_h"], 1)
            for f in range(4):
                for b in range(3):
                    p = n % 2
                    act.wait_ge(s["used"], n + 1)
                    if b < 2:
                        if f and b == 0:
                            act.wait_ge(s["mg_d"], 2 * f)
                        for t in range(2):
                            c = P1_BM + 8 * b + 2 * f + t
                            ac.activation(mt[:, b, t, :], ps[:, 2 * p + t, :], ACT.Sigmoid, bias=pk1[:, c:c + 1]).then_inc(
                                *((s["mg_a"], 1) if t == 0 else (evac[p], 1)))
                    round_chunk(n + 2, p)
                    n += 1
                act.wait_ge(s["mg_d"], 2 * f + 2)
                ac.activation(mh[:, 2 * f:2 * f + 2, :], mt[:, 2, :, :], ACT.Copy).then_inc(s["mg_h"], 1)
            for j in range(4):
                p = n % 2
                act.wait_ge(evac[p], n // 2 + 1)
                for t in range(2):
                    k = 2 * j + t
                    ac.activation(xh[:, k, :], x[:, k, :], ACT.Copy).then_inc(s["x1_h"], 1)
                round_chunk(n + 2, p)
                n += 1

        def out_pair(act, g, u, pr):
            act.wait_ge(s["at_v"], u)
            nc.scalar.activation(view(og[:, g, pr, :], VIEW[g]), own(ps[:, pr % 2, :], VIEW[g]), ACT.Copy).then_inc(s["at_o"], 1)

        def block1_dve(dve, rest_chunk):
            ve = nc.vector
            rest_chunk(0, 0)
            dve.wait_ge(s["b_par"], 16)
            ve.tensor_scalar(cols[:, 3:4], pk1[:, P1_QN:P1_QN + 1], -0.125, None, ALU.mult).then_inc(s["b_c"], 1)
            ve.tensor_scalar(cols[:, 4:5], pk1[:, P1_QN + 2:P1_QN + 3], -0.125, None, ALU.mult).then_inc(s["b_c"], 1)
            ve.tensor_scalar(cols[:, 5:6], pk1[:, P1_SINK:P1_SINK + 1], -1.0, None, ALU.mult).then_inc(s["b_c"], 1)
            dve.wait_ge(s["b_xs"], 1)
            ve.reciprocal(bsq[:, 4, :], bsq[:, 2, :]).then_inc(s["b_xr"], 1)
            dve.wait_ge(s["b_xr"], 1)
            for k in range(KT):
                if k >= 4:
                    dve.wait_ge(s["b_hl"], k - 3)
                ve.scalar_tensor_tensor(out=hb[:, k % 4, :], in0=x[:, k, :], scalar=pk1[:, k:k + 1], in1=bsq[:, 4, :], op0=ALU.mult, op1=ALU.mult).then_inc(s["b_h"], 1)
            rest_chunk(1, 1)
            dve.wait_ge(s["b_rp"], 1)
            for o in range(2):
                ve.scalar_tensor_tensor(out=brow[0:16, o, :], in0=ps[0:16, 4 + 2 * o, :], scalar=-1.0, in1=c2[0:16, 1024 + 512 * o:1536 + 512 * o],
                                        op0=ALU.mult, op1=ALU.add).then_inc(s["b_row"], 1)
            n = tile = u = 0
            for gi, g in enumerate(ORDER):
                if gi:
                    dve.wait_ge(s["at_o"], 4 * gi)
                for kind in KINDS[g]:
                    p = n % 2
                    if kind[0] == "v":
                        dve.wait_ge(s["used"], n + 1)
                        w = VW[g]
                        v0 = w * int(kind[1])
                        src = ps[:, 2 * p:2 * p + 2, 0:2 * w].rearrange("p a (b c) -> p a b c", b=2)
                        dst = vg[:, :, v0:v0 + w].rearrange("p (a b) c -> p a b c", b=2)
                        ve.tensor_copy(dst, src).then_inc(evac[p], 1)
                    else:
                        for t in range(2):
                            m = tile + t
                            dve.wait_ge(s["b_sd"], m + 1)
                            ve.reciprocal(bsq[:, 4 + m % 2, :], bsq[:, 2 + m % 2, :]).then_inc(s["b_rc"], 1)
                            dve.wait_ge(s["b_rc"], m + 1)
                            dst = (qg if kind[0] == "q" else kg)[:, 2 * int(kind[1]) + t, :]
                            if kind[0] == "q":
                                f = cols[:, 3:4] if g == 0 else cols[:, 4:5]
                            else:
                                f = pk1[:, P1_QN + 1:P1_QN + 2] if g == 0 else pk1[:, P1_QN + 3:P1_QN + 4]
                            if t:
                                dve.wait_ge(s["b_q"], m // 2 + 1)
                            ve.scalar_tensor_tensor(out=own(dst, VIEW[g]), in0=view(ps[:, 2 * p + t, :], VIEW[g]), scalar=f, in1=view(bsq[:, 4 + m % 2, :], VIEW[g]),
                                                    op0=ALU.mult, op1=ALU.mult).then_inc(evac[p] if t else s["b_q"], 1)
                        dve.wait_ge(evac[p], n // 2 + 1)
                        tile += 2
                    n += 1
                if gi == 0:
                    dve.wait_ge(s["b_bw"], 16)
                if gi == 1:
                    dve.wait_ge(s["b_b1"], 16)
                if gi == 2:
                    dve.wait_ge(s["b_bw"], 32)
                if gi == 3:
                    dve.wait_ge(s["b_b2"], 16)
                base_u = u
                for m in range(32 + 2):
                    if m < 32:
                        h, i = m // 4, m % 4
                        w = P * len(key_tiles(g, i))
                        c = i * 8 + h
                        dve.wait_ge(s["at_s"], u + 1)
                        if u >= 2:
                            dve.wait_ge(s["at_p"], u - 1)
                        ve.tensor_tensor_reduce(out=lg[:, u % 2, 0:w], in0=ps[:, 4 + u % 2, 0:w], in1=bias_of(g, h, i), scale=1.0, scalar=3e38,
                                                op0=ALU.add, op1=ALU.min, accum_out=nmc[:, g, c:c + 1]).then_inc(s["at_l"], 1)
                        u += 1
                    if m >= 2:
                        v = base_u + m - 2
                        i = (m - 2) % 4
                        w = P * len(key_tiles(g, i))
                        dve.wait_ge(s["at_t"], v + 1)
                        if v >= 2:
                            dve.wait_ge(s["at_v"], v - 1)
                        ve.tensor_copy(pt[:, v % 2, 0:w], ps[:, 6 + v % 2, 0:w]).then_inc(s["at_e"], 1)
            dve.wait_ge(s["st_ps"], 8)
            for g in range(4):
                ve.tensor_copy(view(rw[0:8, 4 + g, :], VIEW[g]), own(ps[0:8, 4 + g, :], VIEW[g])).then_inc(s["st_d"], 1)
            dve.wait_ge(s["st_a"], 4)
            ve.tensor_scalar(sgl[0:8, 0, :], rw[0:8, 0, :], cols[0:8, 5:6], None, ALU.min).then_inc(s["st_d"], 1)
            ve.tensor_tensor(sgl[0:8, 1, :], rw[0:8, 1, :], rw[0:8, 2, :], ALU.min).then_inc(s["st_d"], 1)
            dve.wait_ge(s["st_d"], 6)
            ve.tensor_tensor(sgl[0:8, 1, :], sgl[0:8, 1, :], rw[0:8, 3, :], ALU.min).then_inc(s["st_d"], 1)
            ve.tensor_tensor(rw[0:8, 8, :], sgl[0:8, 0, :], rw[0:8, 0, :], ALU.subtract).then_inc(s["st_d"], 1)
            dve.wait_ge(s["st_d"], 7)
            ve.tensor_tensor(rw[0:8, 9:12, :], sgl[0:8, 1, :].unsqueeze(1).to_broadcast([8, 3, TOK]), rw[0:8, 1:4, :], ALU.subtract).then_inc(s["st_d"], 1)
            dve.wait_ge(s["st_e"], 3)
            ve.tensor_tensor(rw[0:8, 4:8, :], rw[0:8, 4:8, :], rw[0:8, 8:12, :], ALU.mult).then_inc(s["st_f"], 1)
            dve.wait_ge(s["st_f"], 1)
            ve.tensor_tensor(sgl[0:8, 0, :], sgl[0:8, 0, :], rw[0:8, 4, :], ALU.add).then_inc(s["st_f"], 1)
            ve.tensor_tensor(sgl[0:8, 1, :], rw[0:8, 5, :], rw[0:8, 6, :], ALU.add).then_inc(s["st_f"], 1)
            dve.wait_ge(s["st_f"], 3)
            ve.tensor_tensor(sgl[0:8, 1, :], sgl[0:8, 1, :], rw[0:8, 7, :], ALU.add).then_inc(s["st_f"], 1)
            dve.wait_ge(s["st_f"], 4)
            ve.reciprocal(sgl[0:8, :, :], sgl[0:8, :, :]).then_inc(s["st_f"], 1)
            dve.wait_ge(s["st_f"], 5)
            ve.tensor_tensor(rw[0:8, 8, :], rw[0:8, 8, :], sgl[0:8, 0, :], ALU.mult).then_inc(s["st_f"], 1)
            ve.tensor_tensor(rw[0:8, 9:12, :], rw[0:8, 9:12, :], sgl[0:8, 1, :].unsqueeze(1).to_broadcast([8, 3, TOK]), ALU.mult).then_inc(s["st_f"], 1)
            dve.wait_ge(s["lo_done"], n + 2)
            for half in range(2):
                rest_chunk(n + 2, 0)
                rest_chunk(n + 3, 1)
                for pr in (2 * half, 2 * half + 1):
                    dve.wait_ge(s["y_ps"], pr + 1)
                    for g in range(4):
                        ve.tensor_tensor(og[:, g, pr, :], og[:, g, pr, :], ps[:, 4 + g, :], ALU.mult).then_inc(s["y_w"], 1)
                    for b in range(2):
                        dve.wait_ge(evac[b], (n + b) // 2 + 1)
                        dve.wait_ge(s["y_w"], 4 * pr + 4)
                        if b:
                            dve.wait_ge(s["y_s"], 2 * pr + 2)
                        ve.tensor_tensor(og[:, b, pr, :], og[:, b, pr, :], zg[:, 2 * b + pr % 2, :], ALU.mult).then_inc(s["y_d"], 1)
                n += 2
            for f in range(4):
                for b in range(3):
                    p = n % 2
                    if b == 2:
                        dve.wait_ge(s["used"], n + 1)
                        dve.wait_ge(evac[1 - p], (n - 1) // 2 + 1)
                        dve.wait_ge(evac[p], n // 2)
                        if f:
                            dve.wait_ge(s["mg_l"], f)
                        ve.tensor_tensor(mt[:, 2, :, :], mt[:, 0, :, :], ps[:, 2 * p:2 * p + 2, :], ALU.mult).then_inc(evac[p], 1)
                        ve.tensor_tensor(mt[:, 1, :, :], mt[:, 1, :, :], ps[:, 4 + 2 * (f % 2):6 + 2 * (f % 2), :], ALU.mult).then_inc(s["mg_d"], 1)
                        dve.wait_ge(s["mg_d"], 2 * f + 1)
                        dve.wait_ge(evac[p], n // 2 + 1)
                        ve.tensor_tensor(mt[:, 2, :, :], mt[:, 2, :, :], mt[:, 1, :, :], ALU.add).then_inc(s["mg_d"], 1)
                        dve.wait_ge(s["mg_d"], 2 * f + 2)
                    rest_chunk(n + 2, p)
                    n += 1
            for j in range(4):
                p = n % 2
                dve.wait_ge(s["used"], n + 1)
                ve.tensor_tensor(x[:, 2 * j:2 * j + 2, :], x[:, 2 * j:2 * j + 2, :], ps[:, 2 * p:2 * p + 2, :], ALU.add).then_inc(evac[p], 1)
                rest_chunk(n + 2, p)
                n += 1

        def block1_pe(pe):
            te = nc.tensor
            pe.wait_ge(s["fm_set"], 1)
            for k in range(KT):
                pe.wait_ge(s["b_x2"], k + 1)
                te.matmul(ps[:, 5, :], fm[:, :], bsq[:, X_SLOT[k % 4], :], start=(k == 0), stop=(k == KT - 1)).then_inc(s["b_ms"], 1)
            pe.wait_ge(s["b_rel"], 16)
            pe.wait_ge(s["c_in"], 16)
            pe.wait_ge(s["c2_in"], 16)
            for o in range(2):
                mm = te.matmul(ps[0:16, 4 + 2 * o, :], relb[0:32, 16 * o:16 * o + 16], c2[0:32, 512 * o:512 * o + 512], start=True, stop=True)
            mm.then_inc(s["b_rp"], 1)
            n = tile = u = 0
            pending = []

            def head_means():
                for m in pending:
                    pe.wait_ge(s["b_sq"], m + 1)
                    if m >= 2:
                        pe.wait_ge(s["b_sd"], m - 1)
                    te.matmul(ps[:, 6 + m % 2, :], C("head_mean"), bsq[:, m % 2, :], start=True, stop=True).then_inc(s["b_hm"], 1)
                pending.clear()

            def begin(n):
                pe.wait_ge(s["lo_done"], n + 1)
                if n >= 2:
                    pe.wait_ge(evac[n % 2], n // 2)

            def features(n, kk, rh, rl, dst, w0, width, block, between=None):
                p = n % 2
                steps = [(w, r, k) for k in range(kk) for w, r in ((wh, rh), (wh, rl), (wl, rh))]
                for m, (w, r, k) in enumerate(steps):
                    mm = te.matmul(dst, w[:, p, w0 + k * block:w0 + k * block + P], r(k), start=(m == 0), stop=(m == len(steps) - 1))
                    if m == 8 and between:
                        between()
                return mm

            def h_first():
                begin(0)
                for k in range(KT):
                    pe.wait_ge(s["b_hl"], k + 1)
                    for t in range(2):
                        for a, (w, r) in enumerate(((wh, xh), (wh, xl), (wl, xh))):
                            mm = te.matmul(ps[:, t, :], w[:, 0, 256 * k + P * t:256 * k + P * t + P], r[:, k, :], start=(k == 0 and a == 0), stop=(k == KT - 1 and a == 2))
                mm.then_inc(s["used"], 1)
                pe.wait_ge(s["b_row"], 2)

            def h_chunk(n):
                begin(n)
                for t in range(2):
                    mm = features(n, KT, lambda k: xh[:, k, :], lambda k: xl[:, k, :], ps[:, 2 * (n % 2) + t, :], t * P, P, 256,
                                  None if t else head_means)
                mm.then_inc(s["used"], 1)

            def tokens(v, r, t):
                if r == 1:
                    return v[:, t * P:(t + 1) * P]
                return view(v, r)[:, t, :]

            for gi, g in enumerate(ORDER):
                for kind in KINDS[g]:
                    if kind[0] != "v":
                        h_chunk(n) if n else h_first()
                        pending += [tile, tile + 1]
                        tile += 2
                    else:
                        begin(n)
                        w, p = VW[g], n % 2
                        for t in range(4):
                            dst = ps[:, 2 * p + t // 2, w * (t % 2):w * (t % 2) + w]
                            steps = [(a, b, k) for k in range(KT) for a, b in ((xh, wh), (xl, wh), (xh, wl))]
                            for m, (a, b, k) in enumerate(steps):
                                mm = te.matmul(dst, tokens(a[:, k, :], VIEW[g], t), b[:, p, k * w:(k + 1) * w], start=(m == 0), stop=(m == len(steps) - 1))
                            if t == 0:
                                head_means()
                        mm.then_inc(s["used"], 1)
                    n += 1
                pe.wait_ge(s["b_q"], tile // 2)
                for p in range(2):
                    pe.wait_ge(evac[p], (n + 1 - p) // 2)
                base_u = u
                for m in range(32 + 3):
                    if m < 32:
                        h, i = m // 4, m % 4
                        js = key_tiles(g, i)
                        b = 64 * (h % 2)
                        kt_ = kg[b:b + 64, h // 4 if g == 0 else h // 2, js[0] * P:(js[-1] + 1) * P]
                        if u >= 2:
                            pe.wait_ge(s["at_l"], u - 1)
                        te.matmul(ps[:, 4 + u % 2, 0:P * len(js)], qg[b:b + 64, h // 2, i * P:(i + 1) * P], kt_, start=True, stop=True).then_inc(s["at_s"], 1)
                        u += 1
                    if 2 <= m < 34:
                        v = base_u + m - 2
                        i = (m - 2) % 4
                        pe.wait_ge(s["at_p"], v + 1)
                        if v >= 2:
                            pe.wait_ge(s["at_e"], v - 1)
                        for a in range(len(key_tiles(g, i))):
                            mm = te.transpose(ps[:, 6 + v % 2, a * P:(a + 1) * P], pb[:, v % 3, a * P:(a + 1) * P], C("ident"))
                        mm.then_inc(s["at_t"], 1)
                    if m >= 3:
                        v = base_u + m - 3
                        h, i = (m - 3) // 4, (m - 3) % 4
                        pe.wait_ge(s["at_e"], v + 1)
                        if h % 2 == 0 and i == 0 and h >= 4:
                            pe.wait_ge(s["at_o"], 4 * gi + h // 2 - 1)
                        js = key_tiles(g, i)
                        hv = h // 4 if g == 0 else h
                        b = 64 * (h % 2)
                        for a, j in enumerate(js):
                            mm = te.matmul(ps[b:b + 64, (h // 2) % 2, i * P:(i + 1) * P], vg[:, j, 64 * hv:64 * hv + 64], pt[:, v % 2, a * P:(a + 1) * P],
                                           start=(a == 0), stop=(a == len(js) - 1))
                        mm.then_inc(s["at_v"], 1)
                pe.wait_ge(s["at_o"], 4 * gi + 4)
            for kind, src in ((0, nmc), (1, lc)):
                for g in range(4):
                    for i in range(4):
                        mm = te.transpose(ps[0:8, 4 * kind + g, i * P:(i + 1) * P], src[:, g, 8 * i:8 * i + 8], C("ident"))
                    mm.then_inc(s["st_ps"], 1)
            pe.wait_ge(s["st_a"], 4)
            pe.wait_ge(s["st_d"], 4)
            for half in range(2):
                for b in range(2):
                    h_chunk(n)
                    n += 1
                pe.wait_ge(s["st_f"], 7)
                for pr in (2 * half, 2 * half + 1):
                    if pr:
                        pe.wait_ge(s["y_w"], 4 * pr)
                    for g in range(4):
                        mm = te.matmul(ps[:, 4 + g, :], sel[0:8, pr, :], rw[0:8, 8 + g, :], start=True, stop=True)
                    mm.then_inc(s["y_ps"], 1)
            for f in range(4):
                h_chunk(n)
                h_chunk(n + 1)
                begin(n + 2)
                p = n % 2
                if f == 0:
                    pe.wait_ge(s["y_l"], 8)
                if f >= 2:
                    pe.wait_ge(s["mg_d"], 2 * f - 2)
                for b in range(2):
                    for t in range(2):
                        dst = ps[:, (2 * p if b == 0 else 4 + 2 * (f % 2)) + t, :]
                        mm = features(n + 2, 4, lambda k: yh[:, 4 * b + k, :], lambda k: yl[:, 4 * b + k, :], dst, 1024 * b + t * P, P, 256)
                mm.then_inc(s["used"], 1)
                n += 3
            for j in range(4):
                begin(n)
                if j == 0:
                    for k in range(KT):
                        if k % 2 == 0:
                            pe.wait_ge(s["mg_l"], k // 2 + 1)
                        for t in range(2):
                            c = 256 * k + P * t
                            for a, (w, r) in enumerate(((wh, mh), (wh, ml), (wl, mh))):
                                mm = te.matmul(ps[:, 2 * (n % 2) + t, :], w[:, n % 2, c:c + P], r[:, k, :], start=(k == 0 and a == 0), stop=(k == KT - 1 and a == 2))
                for t in range(2 if j else 0):
                    mm = features(n, KT, lambda k: mh[:, k, :], lambda k: ml[:, k, :], ps[:, 2 * (n % 2) + t, :], t * P, P, 256)
                mm.then_inc(s["used"], 1)
                n += 1

        @block.sync
        def _(sp):
            sp.dma_start(x[:, :, :], x_in).then_inc(s["x_in"], 16)
            sp.dma_start(raw[:, 0, :], stream[0]).then_inc(landed[0], 16)
            sp.dma_start(cst[:, :], consts).then_inc(s["c_in"], 16)
            sp.dma_start(raw[:, 1, :], stream[1]).then_inc(landed[1], 16)
            sp.dma_start(c2[:, :], consts2).then_inc(s["c2_in"], 16)
            with sp.Fori(1, N_CHUNKS // 2) as i:
                for p in range(2):
                    sp.wait_ge(s["lo_done"], i * 2 + p - 1)
                    sp.dma_start(raw[:, p, :], stream[bass.ds(i * 2 + p, 1)].rearrange("a p n -> (a p) n")).then_inc(landed[p], 16)

        @block.gpsimd
        def _(pool):
            gp = nc.gpsimd

            def hidden_rest(l, w, i):
                n = l * 22 + w * 11 + i + 1
                pool.wait_ge(s["h_hi"], n)
                gp.tensor_tensor(hl[:, bass.ds(i * 2, 2), :], hf[:, :, :], hh[:, bass.ds(i * 2, 2), :].bitcast(F32), ALU.subtract).then_inc(s["h_lo"], 1)

            def down_rests(l, off):
                with pool.Fori(0, KT) as f:
                    for p in range(2):
                        rest(pool, c_no(l, off) + f * 2 + p + 2, p)

            def norm_rest(l, w):
                for k in range(0, KT, 2):
                    pool.wait_ge(s["ln_h"], l * 24 + w * 8 + k + 1)
                    pool.wait_ge(s["ln_x"], l * 24 + w * 8 + k // 2 + 1)
                    gp.tensor_tensor(xl[:, k, :], x[:, k, :], xh[:, k, :].bitcast(F32), ALU.subtract).then_inc(xr[0], 1)

            block1_pool(pool)
            pool.sem_inc(s["dp_pool"], 1)
            pool.sem_inc(s["h_lo"], 1)
            with pool.Fori(0, LAYERS) as l:
                for r in range(2):
                    pool.wait_ge(xr[r], l * 12 + 4)
                pool.dma_start(pkt[:, :], pk[bass.ds(l, 1)].rearrange("a p n -> (a p) n")).then_inc(s["par_in"], 16)
                with pool.Fori(0, UP // 2) as i:
                    hidden_rest(l, 0, i)
                down_rests(l, OFF_DN1)
                norm_rest(l, 0)
                pool.dma_start(sgp[:, :], sg[bass.ds(l, 1)].rearrange("a p n -> (a p) n")).then_inc(s["sgp_in"], 16)
                mixer_pool(l, pool)
                for j in range(OUTP):
                    rest(pool, c_no(l, OFF_OUT) + j + 2, j % 2)
                norm_rest(l, 1)
                with pool.Fori(0, UP // 2) as i:
                    hidden_rest(l, 1, i)
                down_rests(l, OFF_DN2)
                norm_rest(l, 2)
                pool.wait_ge(s["ln_x"], l * 24 + 24)

        @block.scalar
        def _(act):
            ac = nc.scalar

            def round_chunk(n, p):
                act.wait_ge(landed[p], (n - p) * 8 + 16)
                act.wait_ge(s["used"], n - 1)
                ac.activation(wh[:, p, :], raw[:, p, :], ACT.Copy).then_inc(s["hi_done"], 1)

            def up(l, w, i, off):
                n = c_no(l, off) + i * 2
                act.wait_ge(s["used"], n + 1)
                act.wait_ge(evac[1], n_evac(l, 1, off) + i)
                ac.activation(sg_t[:, :, :], ps[:, 0:2, :], ACT.Silu).then_inc(evac[0], 1)
                round_chunk(n + 2, 0)
                act.wait_ge(evac[1], n_evac(l, 1, off) + i + 1)
                ac.activation(hh[:, bass.ds(i * 2, 2), :], hf[:, :, :], ACT.Copy).then_inc(s["h_hi"], 1)
                round_chunk(n + 3, 1)

            def norm(l, w):
                for k in range(KT):
                    act.wait_ge(s["ln_zc"], l * 24 + w * 8 + k + 1)
                    if k >= 4:
                        act.wait_ge(s["ln_var"], l * 24 + w * 8 + k - 3)
                    ac.activation(sq[:, k % 4, :], x[:, k, :], ACT.Square).then_inc(s["ln_sq"], 1)
                act.wait_ge(s["ln_var"], l * 24 + w * 8 + 8)
                ac.activation(std[:, :], ps[:, 5, :], ACT.Sqrt, bias=eps_col("eps_ln")).then_inc(s["ln_std"], 1)
                c = PK_LN + 16 * w + 8
                for k in range(KT):
                    act.wait_ge(s["ln_t"], l * 24 + w * 8 + k + 1)
                    ac.activation(xh[:, k, :], zn[:, k, :], ACT.Identity, bias=pkt[:, c + k:c + k + 1]).then_inc(s["ln_h"], 1)
                    if k % 2 == 0:
                        ac.activation(x[:, k, :], zn[:, k, :], ACT.Identity, bias=pkt[:, c + k:c + k + 1]).then_inc(s["ln_x"], 1)
                for k in range(1, KT, 2):
                    ac.activation(x[:, k, :], zn[:, k, :], ACT.Identity, bias=pkt[:, c + k:c + k + 1]).then_inc(s["ln_x"], 1)
                act.wait_ge(s["ln_x"], l * 24 + w * 8 + 8)

            act.wait_ge(s["c_in"], 16)
            block1_act(act, round_chunk)
            with act.Fori(0, LAYERS) as l:
                act.wait_ge(s["par_in"], l * 16 + 16)
                with act.Fori(0, UP // 2) as i:
                    up(l, 0, i, OFF_UP1)
                with act.Fori(0, KT) as f:
                    for p in range(2):
                        round_chunk(c_no(l, OFF_DN1) + f * 2 + p + 2, p)
                norm(l, 0)
                in_products_act(l, act, round_chunk)
                mixer_act(l, act)
                for j in range(OUTP):
                    round_chunk(c_no(l, OFF_OUT) + j + 2, j % 2)
                norm(l, 1)
                with act.Fori(0, UP // 2) as i:
                    up(l, 1, i, OFF_UP2)
                with act.Fori(0, KT) as f:
                    for p in range(2):
                        round_chunk(c_no(l, OFF_DN2) + f * 2 + p + 2, p)
                norm(l, 2)
            act.wait_ge(s["ln_x"], 24 * LAYERS)
            for r in range(2):
                act.wait_ge(xr[r], 4 + 12 * LAYERS)
            act.dma_start(out, x[:, :, :]).then_inc(s["stored"], 16)
            act.wait_ge(s["stored"], 16)

        @block.vector
        def _(dve):
            ve = nc.vector

            def rest_chunk(n, p):
                dve.wait_ge(s["hi_done"], n + 1)
                ve.tensor_tensor(wl[:, p, :], raw[:, p, :], wh[:, p, :].bitcast(F32), ALU.subtract).then_inc(s["lo_done"], 1)

            def up(l, w, i, off):
                n = c_no(l, off) + i * 2
                rest_chunk(n + 2, 0)
                dve.wait_ge(s["used"], n + 2)
                dve.wait_ge(evac[0], n_evac(l, 0, off) + i + 1)
                dve.wait_ge(s["h_lo"], l * 22 + w * 11 + i + 1)
                ve.tensor_tensor(hf[:, :, :], ps[:, 2:4, :], sg_t[:, :, :], ALU.mult).then_inc(evac[1], 1)
                rest_chunk(n + 3, 1)

            def down(l, w, i, off):
                for q in range(2):
                    f = i * 2 + q
                    n = c_no(l, off) + i * 4 + q * 2
                    dve.wait_ge(s["used"], n + 2)
                    xf = x[:, bass.ds(f, 1), :].rearrange("p a t -> p (a t)")
                    ve.scalar_tensor_tensor(out=xf, in0=ps[:, 2 * q, :], scalar=0.5 / ALPHA, in1=xf, op0=ALU.mult, op1=ALU.add).then_inc(evac[1], 1)
                    dve.wait_ge(evac[1], n_evac(l, 1, off) + f + 1)
                    dve.wait_ge(s["z_sum"], l * 27 + w * 9 + f + 1)
                    ve.tensor_tensor(zacc[:, :], zacc[:, :], xf, ALU.add).then_inc(s["z_sum"], 1)

            def norm(l, w):
                dve.wait_ge(s["ln_mean"], l * 3 + w + 1)
                for k in range(KT):
                    ve.tensor_tensor(x[:, k, :], x[:, k, :], ps[:, 4, :], ALU.subtract).then_inc(s["ln_zc"], 1)
                dve.wait_ge(s["ln_std"], l * 3 + w + 1)
                ve.reciprocal(rstd[:, :], std[:, :]).then_inc(s["ln_rs"], 1)
                dve.wait_ge(s["ln_rs"], l * 3 + w + 1)
                for k in range(KT + 3):
                    if k < KT:
                        c = PK_LN + 16 * w + k
                        ve.scalar_tensor_tensor(out=zn[:, k, :], in0=x[:, k, :], scalar=pkt[:, c:c + 1], in1=rstd[:, :], op0=ALU.mult, op1=ALU.mult).then_inc(s["ln_t"], 1)
                    j = k - 2
                    if j > 0 and j % 2:
                        dve.wait_ge(s["ln_h"], l * 24 + w * 8 + j + 1)
                        dve.wait_ge(s["ln_t"], l * 24 + w * 8 + j + 1)
                        c = PK_LN + 16 * w + 8 + j
                        ve.scalar_tensor_tensor(out=xl[:, j, :], in0=zn[:, j, :], scalar=pkt[:, c:c + 1], in1=xh[:, j, :].bitcast(F32),
                                                op0=ALU.add, op1=ALU.subtract).then_inc(xr[1], 1)

            dve.memset(fm[:, :], 1.0 / D).then_inc(s["fm_set"], 1)
            dve.memset(cols[:, 0:1], EPS2 / ALPHA ** 2).then_inc(s["eps"], 1)
            dve.memset(cols[:, 1:2], EPS2).then_inc(s["eps"], 1)
            dve.memset(cols[:, 2:3], EPS_L2).then_inc(s["eps"], 1)
            dve.memset(nega[:, :], 0.0).then_inc(s["eps"], 1)
            dve.wait_ge(s["eps"], 4)
            dve.sem_inc(s["dp_dve"], 1)
            dve.sem_inc(s["lv_dve"], 8)
            block1_dve(dve, rest_chunk)
            with dve.Fori(0, LAYERS) as l:
                dve.wait_ge(s["lo_done"], c_no(l, OFF_UP1) + 2)
                dve.sem_inc(s["apart_dve"], 1)
                with dve.Fori(0, UP // 2) as i:
                    up(l, 0, i, OFF_UP1)
                dve.wait_ge(evac[1], n_evac(l, 1, OFF_DN1))
                ve.memset(zacc[:, :], 0.0).then_inc(s["z_sum"], 1)
                with dve.Fori(0, KT // 2) as i:
                    down(l, 0, i, OFF_DN1)
                norm(l, 0)
                in_products_dve(l, dve, rest_chunk)
                mixer_dve(l, dve)
                dve.wait_ge(s["mixB"], l * 4 + 4)
                ve.memset(zacc[:, :], 0.0).then_inc(s["z_sum"], 1)
                for j in range(OUTP):
                    n = c_no(l, OFF_OUT) + j
                    p = j % 2
                    dve.wait_ge(s["used"], n + 1)
                    ve.scalar_tensor_tensor(out=x[:, 2 * j:2 * j + 2, :], in0=ps[:, 2 * p:2 * p + 2, :], scalar=1.0 / ALPHA, in1=x[:, 2 * j:2 * j + 2, :], op0=ALU.mult, op1=ALU.add).then_inc(evac[p], 1)
                    dve.wait_ge(evac[p], n_evac(l, p, OFF_OUT) + j // 2 + 1)
                    for k in range(2):
                        dve.wait_ge(s["z_sum"], l * 27 + 9 + 2 * j + k + 1)
                        ve.tensor_tensor(zacc[:, :], zacc[:, :], x[:, 2 * j + k, :], ALU.add).then_inc(s["z_sum"], 1)
                norm(l, 1)
                dve.wait_ge(s["lo_done"], c_no(l, OFF_UP2) + 2)
                dve.sem_inc(s["apart_dve"], 1)
                with dve.Fori(0, UP // 2) as i:
                    up(l, 1, i, OFF_UP2)
                dve.wait_ge(evac[1], n_evac(l, 1, OFF_DN2))
                ve.memset(zacc[:, :], 0.0).then_inc(s["z_sum"], 1)
                with dve.Fori(0, KT // 2) as i:
                    down(l, 2, i, OFF_DN2)
                norm(l, 2)

        @block.tensor
        def _(pe):
            te = nc.tensor
            H, L_ = 0, 1

            def product_t(n, p, w_lo, outs, rhs_h, rhs_l, k0, first, last):
                pass

            def parts(w, rh, rl):
                return

            def accumulate(dst, ks, wslice, rh, rl, start, stop, moving_w=False, inc=None):
                steps = []
                for k in ks:
                    steps += [(wh, rh, k), (wh, rl, k), (wl, rh, k)]
                for m, (w, r, k) in enumerate(steps):
                    a, b = wslice(w, k), r(k)
                    if moving_w:
                        a, b = b, a
                    mm = te.matmul(dst, a, b, start=(start and m == 0), stop=(stop and m == len(steps) - 1))
                return mm

            def chunk_t(l, off, i, p, cols=256, order=range(KT), ready=None):
                n = c_no(l, off) + i
                pe.wait_ge(s["lo_done"], n + 1)
                if ready:
                    for m, k in enumerate(order):
                        ready(k)
                        for j in range(cols // P):
                            cs = slice(k * cols + j * P, k * cols + (j + 1) * P)
                            for a, (w, r) in enumerate(((wh, xh), (wh, xl), (wl, xh))):
                                mm = te.matmul(ps[:, 2 * p + j, :], w[:, p, cs], r[:, k, :], start=(m == 0 and a == 0), stop=(m == KT - 1 and a == 2))
                    mm.then_inc(s["used"], 1)
                    return
                for j in range(cols // P):
                    mm = accumulate(ps[:, 2 * p + j, :], range(KT),
                                    lambda w, k: w[:, p, k * cols + j * P:k * cols + (j + 1) * P],
                                    lambda k: xh[:, k, :], lambda k: xl[:, k, :], True, True)
                mm.then_inc(s["used"], 1)

            def chunk_n(l, off, i, p):
                n = c_no(l, off) + i
                pe.wait_ge(s["lo_done"], n + 1)
                for t in range(4):
                    steps = [(xx, w, k) for k in range(KT) for xx, w in ((xh, wh), (xl, wh), (xh, wl))]
                    dst = ps[:, 2 * p + t // 2, 256 * (t % 2):256 * (t % 2) + 256]
                    for m, (a, w, k) in enumerate(steps):
                        mm = te.matmul(dst, a[:, k, t * P:(t + 1) * P], w[:, p, k * 256:(k + 1) * 256],
                                       start=(m == 0), stop=(m == len(steps) - 1))
                mm.then_inc(s["used"], 1)

            def up(l, w, i, off, ready=None):
                for p in range(2):
                    pe.wait_ge(evac[p], n_evac(l, p, off) + i)
                    chunk_t(l, off, i * 2 + p, p, ready=None if p else ready)

            def normed(l, w):
                return lambda k: pe.wait_ge(xr[k % 2], l * 12 + w * 4 + k // 2 + 1)

            def down(l, w, i, off):
                for q in range(2):
                    pe.wait_ge(evac[1], n_evac(l, 1, off) + i * 2 + q - (1 if q else 1))
                    for p in range(2):
                        n = c_no(l, off) + i * 4 + q * 2 + p
                        pe.wait_ge(s["lo_done"], n + 1)
                        if p and q == 0:
                            pe.wait_ge(s["h_lo"], l * 22 + w * 11 + 12)
                        mm = accumulate(ps[:, 2 * q, :], range(11), lambda w_, k: w_[:, p, k * P:(k + 1) * P],
                                        lambda k: hh[:, 11 * p + k, :], lambda k: hl[:, 11 * p + k, :], p == 0, p == 1)
                        mm.then_inc(s["used"], 1)

            def norm(l, w):
                pe.wait_ge(s["z_sum"], l * 27 + w * 9 + 9)
                te.matmul(ps[:, 4, :], C("feat_mean"), zacc[:, :], start=True, stop=True).then_inc(s["ln_mean"], 1)
                for k in range(KT):
                    pe.wait_ge(s["ln_sq"], l * 24 + w * 8 + k + 1)
                    te.matmul(ps[:, 5, :], C("feat_mean"), sq[:, k % 4, :], start=(k == 0), stop=(k == KT - 1)).then_inc(s["ln_var"], 1)

            pe.sem_inc(s["lv_x"], 4)
            pe.sem_inc(s["lv_t"], 4)
            block1_pe(pe)
            with pe.Fori(0, LAYERS) as l:
                up(l, 0, 0, OFF_UP1, normed(l, 0))
                with pe.Fori(1, UP // 2) as i:
                    up(l, 0, i, OFF_UP1)
                pe.wait_ge(s["h_lo"], l * 22 + 7)
                pe.wait_ge(evac[0], n_evac(l, 0, OFF_DN1))
                pe.sem_inc(s["apart_pe"], 1)
                with pe.Fori(0, KT // 2) as i:
                    down(l, 0, i, OFF_DN1)
                norm(l, 0)
                in_products_pe(l, pe, chunk_t, chunk_n, normed(l, 1))
                mixer_pe(l, pe)
                for j in range(OUTP):
                    pe.wait_ge(evac[j % 2], n_evac(l, j % 2, OFF_OUT) + j // 2)
                    order = (0, 1, 6, 7, 2, 3, 4, 5)
                    chunk_t(l, OFF_OUT, j, j % 2, order=order,
                            ready=None if j else lambda k: pe.wait_ge(s["mix_lo"], l * 8 + order.index(k) + 1))
                norm(l, 1)
                up(l, 1, 0, OFF_UP2, normed(l, 2))
                with pe.Fori(1, UP // 2) as i:
                    up(l, 1, i, OFF_UP2)
                pe.wait_ge(s["h_lo"], l * 22 + 11 + 7)
                pe.wait_ge(evac[0], n_evac(l, 0, OFF_DN2))
                pe.sem_inc(s["apart_pe"], 1)
                with pe.Fori(0, KT // 2) as i:
                    down(l, 1, i, OFF_DN2)
                norm(l, 2)


def blocks(w, cols):
    k, n = w.shape
    return w.reshape(k // P, P, n // cols, cols).transpose(2, 1, 0, 3).reshape(n // cols, P, k // P * cols)


def pad(c):
    out = np.zeros(c.shape[:2] + (2048,), c.dtype)
    out[:, :, :c.shape[2]] = c
    return out


def up_chunks(w1, w3):
    return np.stack([blocks(w1, 256), blocks(w3, 256)], 1).reshape(-1, P, 2048)


def down_chunks(w2):
    b = w2.reshape(2, FT // 2, P, KT, P).transpose(3, 0, 2, 1, 4).reshape(2 * KT, P, FT // 2 * P)
    return pad(b)


def layer_chunks(a, l):
    w = a["w_in_2"][l]
    small = np.zeros((D, P), w.dtype)
    small[:, 64:80] = w[:, 3344:3360]
    small[:, 32:40] = w[:, 2568:2576]
    small[:, 0:8] = w[:, 2560:2568]
    order = [blocks(w[:, c:c + 256], 256) for c in (512, 768, 1024, 1280, 1536, 1792)]
    order += [pad(blocks(small, P))] + [blocks(w[:, c:c + 256], 256) for c in (2576, 2832, 0, 256, 3088, 2048, 2304)]
    return [up_chunks(a["ffn1_w1_2"][l], a["ffn1_w3_2"][l]), down_chunks(a["ffn1_w2_2"][l])] + order + [
        blocks(a["w_out_2"][l], 256), up_chunks(a["ffn2_w1_2"][l], a["ffn2_w3_2"][l]), down_chunks(a["ffn2_w2_2"][l])]


def layer_params(a, l):
    pk = np.zeros((P, NPK), np.float32)
    for w, (g, b) in enumerate((("ln1_g_2", "ln1_b_2"), ("ln2_g_2", "ln2_b_2"), ("ln3_g_2", "ln3_b_2"))):
        pk[:, PK_LN + 16 * w:PK_LN + 16 * w + 8] = a[g][l].reshape(KT, P).T
        pk[:, PK_LN + 16 * w + 8:PK_LN + 16 * w + 16] = a[b][l].reshape(KT, P).T
    pk[:, PK_CONV:PK_CONV + 48] = a["gdn_conv_w_2"][l].reshape(4, 12, P).transpose(2, 1, 0).reshape(P, 48)
    pk[:, PK_GN] = np.concatenate([a["gdn_norm_g_2"][l]] * 2)
    pk[:, PK_LAN] = np.concatenate([a["gla_norm_g_2"][l]] * 2)
    pk[32:40, PK_ALOG] = a["gdn_a_log_2"][l]
    pk[32:40, PK_DT] = a["gdn_dt_bias_2"][l]
    pk[:, PK_GB] = a["gla_gate_b_2"][l]
    pk[64:80, PK_UP:PK_UP + P] = a["gla_gate_up_2"][l]
    sg = np.zeros((P, NSG), np.float32)
    sg[:, SG_G:SG_G + 256] = a["sgu_ln_g_2"][l][None, :]
    sg[:, SG_B:SG_B + 256] = a["sgu_ln_b_2"][l][None, :]
    sg[:, SG_BS:SG_BS + 256] = np.repeat(a["sgu_b_2"][l].reshape(2, 2, P).transpose(1, 0, 2).reshape(2, 256), 64, 0)
    sg[:, SG_W:SG_W + 512] = a["sgu_w_2"][l].transpose(2, 0, 1).reshape(P, 512)
    return pk, sg


def first_chunks(a):
    w = a["w_in"][0]
    qa, ka, va, qb, kb, vb, ga, gb, mg = (w[:, c:c + n] for c, n in (
        (0, 512), (512, 128), (640, 128), (768, 1536), (2304, 1536), (3840, 1536), (5376, 512), (5888, 512), (6400, 2048)))
    k2 = np.concatenate([ka[:, 64 * h:64 * h + 64] for h in (0, 0, 1, 1)], 1)
    out = []
    for g in ORDER:
        if g == 0:
            out += [blocks(qa, 256), blocks(k2, 256), pad(blocks(va, 128))]
        else:
            c = slice(512 * (g - 1), 512 * g)
            out += [blocks(qb[:, c], 256), blocks(kb[:, c], 256), blocks(vb[:, c], 256)]
    for h in range(2):
        c = slice(256 * h, 256 * h + 256)
        out += [blocks(ga[:, c], 256), blocks(gb[:, c], 256)]
    wa, wb = blocks(a["w_branch_a"][0], 256), blocks(a["w_branch_b"][0], 256)
    for f in range(4):
        c = 256 * f
        out += [blocks(mg[:, c:c + 256], 256), blocks(mg[:, D + c:D + c + 256], 256), np.concatenate([wa[f:f + 1], wb[f:f + 1]], 2)]
    return out + [blocks(a["w_out"][0], 256)]


def first_params(a):
    p = np.zeros((P, 32), np.float32)
    p[:, 0:8] = a["norm_gain"][0].reshape(KT, P).T
    for m, name in enumerate(("q_norm_a", "k_norm_a", "q_norm_b", "k_norm_b")):
        p[:, P1_QN + m] = np.concatenate([a[name][0]] * 2)
    p[0:8, P1_SINK] = a["sink_a"][0]
    p[:, P1_BM:P1_BM + 16] = a["b_merge"][0].reshape(16, P).T
    return p


def lay_out(a):
    parts = first_chunks(a)
    for l in range(LAYERS):
        parts += layer_chunks(a, l)
    parts.append(np.zeros((2, P, 2048), np.float32))
    small = [layer_params(a, l) for l in range(LAYERS)]
    return {
        "stream": np.concatenate(parts, 0),
        "pk": np.stack([p for p, _ in small]),
        "sg": np.stack([g for _, g in small]),
        "consts": CONSTS,
        "consts2": bias_constants(),
        "rel": np.ascontiguousarray(a["rel_bias"]),
        "p1": first_params(a),
        "x_in": np.ascontiguousarray(a["x"][0].reshape(TOK, KT, P).transpose(2, 1, 0)),
    }


def kernel(**inputs):
    import concourse.bacc as bacc
    from concourse.bass_utils import run_bass_kernel_spmd

    nc = bacc.Bacc("TRN2", target_bir_lowering=False, num_devices=1)
    arrays = lay_out({name: np.asarray(v) for name, v in inputs.items()})
    aps = {name: nc.dram_tensor(name, v.shape, F32, kind="ExternalInput").ap() for name, v in arrays.items()}
    out = nc.dram_tensor("out", (P, KT, TOK), F32, kind="ExternalOutput").ap()
    program(nc, out=out, **aps)
    r = run_bass_kernel_spmd(nc, [arrays], core_ids=[0])
    y = r.results[0]["out"]
    return np.ascontiguousarray(y.transpose(2, 1, 0)).reshape(1, TOK, D)
```

```python
from contextlib import ExitStack

import numpy as np
import concourse.bass as bass
from concourse import mybir

F32 = mybir.dt.float32
F32R = mybir.dt.float32r
ALU = mybir.AluOpType
ACT = mybir.ActivationFunctionType
AXX = mybir.AxisListType.X

P = 128
TOK = 512
D = 1024
KT = D // P
DFF = 2816
FT = DFF // P
LAYERS = 2
ALPHA = (2.0 * LAYERS) ** 0.25
EPS2 = 1e-5
EPS_L2 = 1e-6
CH = 64
NCH = TOK // CH
PAIRS = 4

UP = 2 * FT // 2
DOWN = 2 * KT
INP = 14
OUTP = KT // 2
PER = 2 * UP + 2 * DOWN + INP + OUTP
OFF_UP1, OFF_DN1 = 0, UP
OFF_IN = UP + DOWN
OFF_OUT = OFF_IN + INP
OFF_UP2 = OFF_OUT + OUTP
OFF_DN2 = OFF_UP2 + UP

K1 = 1024

VIEW = (1, 1, 4, 4)
HALF = (128, 64, 64, 64)
WIDE = (True, True, False, False)
ORDER = (0, 2, 1, 3)
KINDS = {0: ("q0", "q1", "k0", "v0")} | {g: ("q0", "q1", "k0", "k1", "v0", "v1") for g in (1, 2, 3)}
VW = (128, 256, 256, 256)
BASE = sum(len(kinds) for kinds in KINDS.values()) + 4 + 12 + 4
P1_QN, P1_SINK, P1_BM = 8, 12, 16


def buckets(rel):
    half, exact, far = 16, 8, 1024
    n = np.abs(rel)
    nf = np.maximum(n, exact).astype(np.float32)
    large = exact + (np.log(nf / np.float32(exact)) / np.float32(np.log(far / exact)) * np.float32(half - exact)).astype(np.int32)
    return (rel > 0) * half + np.where(n < exact, n, np.minimum(large, half - 1))


def bias_constants():
    out = np.zeros((P, 2048), np.float32)
    r = np.arange(512)
    for t, (stride, mid) in enumerate(((1, 255), (4, 127))):
        out[buckets((r - mid) * stride), 512 * t + r] = 1
    for g, (mid, step) in enumerate(((255, 1), (255, 1), (127, 1), (127, 4))):
        near = ((r - mid) % step == 0) & (np.abs(r - mid) <= HALF[g] * step)
        row, c = 8 * (g % 2), 1024 + 512 * (g // 2)
        out[row:row + 8, c:c + 512] = np.where(near, 0.0, 1e30)
    return out


def const_columns():
    at, parts = {}, []
    n = 0

    def put(name, a):
        nonlocal n
        a = np.asarray(a, np.float32).reshape(P, -1)
        at[name] = (n, a.shape[1])
        parts.append(a)
        n += a.shape[1]

    r = np.arange(P)
    put("ident", np.eye(P))
    put("head_mean", (r[:, None] // 64 == r[None, :] // 64) / 64.0)
    put("feat_mean", np.full((P, P), 1.0 / D))
    i, j = r[:, None] % CH, np.arange(CH)[None, :]
    put("eye64", i == j)
    put("upper64", i <= j)
    put("strict64", i < j)
    put("low1", (i == j + 1) & (j % 2 == 0))
    put("upT1", (j == i + 1) & (i % 2 == 0))
    for s in (2, 4, 8, 16, 32):
        put(f"upT{s}", ((i // s) % 2 == 0) & (j // s == i // s + 1))
    put("upper128", r[:, None] <= r[None, :])
    put("keep", np.tile((np.arange(TOK) % CH != 0)[None, :], (P, 1)))
    sel = np.zeros((P, PAIRS, P))
    for base in (0, 32):
        for h in range(8):
            sel[base + h, h // 2, 64 * (h % 2):64 * (h % 2) + 64] = 1
    put("sel", sel)
    seln = np.zeros((P, 2, PAIRS))
    for base in (0, 32):
        for h in range(8):
            seln[base + h, h % 2, h // 2] = 1
    put("seln", seln)
    return at, np.concatenate(parts, 1)


CONST_AT, CONSTS = const_columns()
NC = CONSTS.shape[1]
PK_LN, PK_CONV, PK_GN, PK_LAN, PK_ALOG, PK_DT, PK_GB, PK_UP = 0, 48, 96, 97, 98, 99, 100, 104
NPK = 232
SG_G, SG_B, SG_BS, SG_W = 0, 256, 512, 768
NSG = 1280


LV_DVE = 4 * 8 + 4
PAIR_DVE = 13

SIGNALS = {
    "mean_matrix_set": "1 / D is written",
    "apart_pe": "nobody waits for these three: such an increment stands between a wait and",
    "apart_dve": "an instruction that is to carry no wait of its own",
    "apart_pool": "(the same, on GpSimd)",
    "columns_set": "VectorE has set the constant columns",
    "consts_in": "constants",
    "bias_consts_in": "constants of the bias rows",
    "x_in": "the input",
    "rel_in": "relative position table",
    "first_params_in": "first block's parameters",
    "layer_params_in": "a layer's parameters",
    "spatial_params_in": "a layer's spatial gating parameters",
    "stored": "the output is in DRAM",
    "chunk_hi": "ScalarE has rounded a chunk to its hi part",
    "chunk_lo": "a chunk's lo part is written",
    "chunk_used": "TensorE is through with a chunk",
    "x_parts_even": "an even tile of x and its parts are written",
    "x_parts_odd": "an odd tile's",
    "hidden_hi": "two hidden tiles' hi parts",
    "hidden_lo": "and their lo parts",
    "z_sum": "the running sum of z over tiles",
    "ln_mean": "mean",
    "ln_centred": "a centred tile",
    "ln_square": "its square",
    "ln_var": "added to the variance",
    "ln_std": "root",
    "ln_rstd": "reciprocal",
    "ln_scaled": "a tile times gain / std",
    "ln_x": "ScalarE has written a tile of x",
    "ln_hi": "its hi part",
    "conv_first": "first tap (ScalarE)",
    "conv_tap": "a further tap (VectorE)",
    "conv_silu": "silu of two tiles",
    "head_square": "squares of a tile",
    "head_ms": "each head's mean square",
    "head_std": "root",
    "head_rstd": "reciprocal",
    "head_normed": "normed tile",
    "gla_logits": "gate logits",
    "gla_pe": "TensorE: scores, keys by token, state increments, outputs",
    "gla_gate_act": "ScalarE: steps of the gates",
    "gla_keys": "keys by token",
    "gla_dve": "VectorE: gates, decayed q and k, states",
    "gla_scores": "masked scores of heads 0-2",
    "gla_out": "outputs",
    "gate_act": "ScalarE: steps of the decay logits, sigmoid of beta",
    "gate_dve": "VectorE: steps of the decay sums",
    "spatial_pool": "GpSimd: masked w, gain, bias",
    "spatial_pe": "mixed tokens of two heads",
    "spatial_std": "root of the variance",
    "spatial_dve": "VectorE: statistics, norm, bias",
    "spatial_done": "a tile of the spatial gating is done",
    "delta_done": "a tile of the delta rule",
    "gla_done": "a tile of the linear attention",
    "mixed_hi": "hi part of a branch's tile",
    "mixed_lo": "and its lo part",
    "by_token_ps": "keys, then values by token in PSUM",
    "by_token_sb": "and in SBUF",
    "columns_ps": "decay sums and betas by token in PSUM",
    "columns_sb": "and in SBUF",
    "sq_x": "square of a tile of x",
    "ms_x": "added to the mean square",
    "rms_x": "root",
    "rrms_x": "reciprocal",
    "h_tile": "a tile of h",
    "h_tile_hi": "its hi part",
    "h_tile_lo": "its lo part",
    "columns_negated": "negated columns (ahead of every use by the bias rows' signals)",
    "bias_ps": "bias rows in PSUM",
    "bias_row": "bias rows in SBUF",
    "bias_dram": "bias rows in DRAM",
    "bias_wide": "tiles of the wide windows",
    "bias_near": "tiles of dilation 4",
    "bias_far": "tiles of dilation 16",
    "qk_square": "squares of a tile of q or k",
    "qk_ms": "each head's mean square",
    "qk_std": "root",
    "qk_rstd": "reciprocal",
    "qk_first": "the first tile of a chunk is normed",
    "att_scores": "scores",
    "att_logits": "with bias, and their minimum (they are negated)",
    "att_probs": "exp and its sum",
    "att_probs_t": "transposed in PSUM",
    "att_probs_sb": "and in SBUF",
    "att_values": "times the values",
    "att_out": "a pair of heads' outputs in SBUF",
    "stat_ps": "maxima, then sums as rows in PSUM",
    "stat_max": "maxima in SBUF (ScalarE)",
    "stat_sum": "sums in SBUF, then steps of the shared maxima",
    "stat_exp": "factors' exponentials",
    "stat_factor": "steps of the factors",
    "y_factor": "a pair's factors over its features",
    "y_weighted": "outputs times factors",
    "y_sum": "sums of the dilated groups",
    "y_gated": "gated",
    "y_hi": "hi part",
    "y_lo": "lo part",
    "merge_gate": "sigmoid of a chunk's first tile",
    "merge_step": "gated branches, and their sum",
    "merge_hi": "hi part of the sum",
    "merge_lo": "lo part",
    "x1_hi": "hi part of the block's outcome",
    "pair_ps": "products of a pair",
    "pair_dve": "VectorE's steps",
    "pair_act": "ScalarE's",
    "pair_pool": "GpSimd's",
    "factor_act": "exponentials of the factors by token",
    "factor_dve": "keys and values times factors",
    "level_x": "X = (L masked) T in PSUM",
    "level_tx": "T X and its transpose in PSUM",
    "level_x_sb": "X in SBUF",
    "level_t": "T, or its transpose, brought up to date",
    "level_l": "masked L",
    "wu_ps": "-(T beta k exp(gamma))^T, then T beta v in PSUM",
    "wu_sb": "and in SBUF",
    "rec_state": "the state before a chunk",
    "rec_u": "the state's part of u in PSUM",
    "rec_unew": "u",
    "rec_decayed": "the decayed state",
    "rec_increment": "the state's increment in PSUM",
    "rec_out": "outputs in PSUM",
    "rec_out_sb": "and in SBUF",
}


def program(nc, stream, pk, sg, consts, bias_consts, rel, p1, x_in, out):
    with ExitStack() as ctx:
        bias_dram_t = nc.dram_tensor("bias_rows", (4, P, 8, 512), F32)
        bias_dram = bias_dram_t.ap()

        def sem(name):
            return ctx.enter_context(nc.semaphore(name))

        def sb(name, kb, shape, dt=F32):
            return nc.alloc_sbuf_tensor_at(name, shape, dt, offset=OFS + int(kb * K1))

        OFS = (nc.sbuf_base + 31) // 32 * 32
        raw = sb("raw", 0, [P, 2, 2048])
        wh = sb("wh", 16, [P, 2, 2048], F32R)
        wl = sb("wl", 32, [P, 2, 2048], F32R)
        x = sb("x", 48, [P, KT, TOK])
        xh = sb("xh", 64, [P, KT, TOK], F32R)
        xl = sb("xl", 80, [P, KT, TOK], F32R)
        hh = sb("hh", 96, [P, FT, TOK], F32R)
        hl = sb("hl", 140, [P, FT, TOK], F32R)
        silu_t = sb("sg_t", 184, [P, 2, TOK])
        hidden = sb("hf", 188, [P, 2, TOK])
        zacc = sb("zacc", 184, [P, TOK])
        zn = sb("zn", 96, [P, KT, TOK])
        sq = sb("sq", 112, [P, 4, TOK])
        rstd = sb("rstd", 192, [P, TOK])
        std = sb("std", 194, [P, TOK])
        const = sb("cst", 196, [P, NC])
        params = sb("pkt", 196 + NC * 4 / K1 + 0.03125, [P, NPK])

        qkv = sb("qkv", 96, [P, 12, TOK])
        qT, kT, vT = qkv[:, 0:4, :], qkv[:, 4:8, :], qkv[:, 8:12, :]
        kN = sb("kN", 120, [P, PAIRS, NCH, CH])
        vN = sb("vN", 128, [P, PAIRS, NCH, CH])
        pT = sb("pT", 136, [P, PAIRS, NCH, CH])
        LT = sb("LT", 144, [P, PAIRS, NCH, CH])
        Tm = sb("Tm", 152, [P, PAIRS, NCH, CH])
        TT = sb("TT", 160, [P, PAIRS, NCH, CH])
        tmp = sb("tmp", 168, [P, 6, TOK])
        zs = sb("zs", 180, [P, PAIRS, TOK])
        rows = sb("rows", 188, [P, TOK])
        decay_sum = sb("gam", 190, [P, TOK])
        gN = sb("gN", 192, [P, NCH, PAIRS])
        bN = sb("bN", 192.125, [P, NCH, PAIRS])
        bgN = sb("bgN", 192.25, [P, NCH, PAIRS])
        kdN = sb("kdN", 192.375, [P, NCH, PAIRS])
        glast = sb("glast", 192.5, [P, NCH, PAIRS])
        gtot = sb("gtot", 192.625, [P, NCH, PAIRS])
        egN = sb("egN", 192.75, [P, NCH, PAIRS])
        exp_a = sb("nega", 192.875, [P, 8])
        state = sb("state", 193, [P, 2, PAIRS, CH])
        unew = sb("unew", 195, [P, PAIRS, CH])
        au = sb("au", 144, [P, 2, TOK])
        av = sb("av", 148, [P, 4, 256])
        cqk = sb("cqk", 152, [P, 2, TOK])
        cr = sb("cr", 156, [P, 2, TOK])
        cv = sb("cv", 160, [P, 4, 256])
        sgp = sb("sgp", 136, [P, NSG])
        bcum = sb("bcum", 164, [P, TOK])
        la = sb("la", 166, [P, TOK])
        pA = sb("pA", 120, [P, 4, 4, CH])
        kdA = sb("kdA", 124, [P, 4, P])
        stA = sb("stA", 126, [P, NCH, CH])
        oA = sb("oA", 128, [P, 2, TOK])
        stat = sb("stat", 132, [P, 4, 6])
        mv = sb("mv", 132.125, [P, 4, 2])
        sgt = sb("sgt", 132.25, [P, 4])
        gtA = sb("gtA", 132.5, [P, NCH])
        cols = sb("cols", 206.25, [P, 8])
        ps = nc.alloc_psum_tensor("ps", [P, 8, TOK], F32)

        Xb = qkv[:, 8:12, :].rearrange("p a (c t) -> p a c t", t=CH)
        oT = qkv[:, 8:12, :]
        bk = qkv[:, 4:8, :].rearrange("p a (c t) -> p a c t", t=CH)
        nwT, u_own = Tm, LT
        sgw = sgp[:, SG_W:SG_W + 512].rearrange("p (h i) -> p h i", i=P)
        qg = sb("qg", 96, [P, 4, TOK])
        kg = sb("kg", 104, [P, 4, TOK])
        vg = sb("vg", 112, [P, 4, TOK])
        bias_wide = sb("btw", 120, [P, 8, 384])
        group_out = sb("og", 132, [P, 4, 4, TOK])
        logits = sb("lg", 164, [P, 2, 384])
        probs = sb("pb", 167, [P, 3, 384])
        probs_t = sb("pt", 171.5, [P, 2, 384])
        neg_max = sb("nmc", 174.5, [P, 4, 32])
        prob_sum = sb("lc", 175, [P, 4, 32])
        bsq = sb("bsq", 175.5, [P, 6, TOK])
        bias_near = sb("bt1", 187.5, [P, 8, P])
        bias_far = sb("bt2", 191.5, [P, 8, P])
        params1 = sb("pk1", 206.5, [P, 32])
        mean_matrix = sb("fm", 128, [P, P])
        bias_cst = sb("c2", 132, [P, 2048])
        bias_rows = sb("brow", 146, [P, 2, TOK])
        rel_table = sb("relb", 154, [P, 32])
        h_new = sb("hb", 155, [P, 4, TOK])
        stat_rows = sb("rw", 96, [P, 12, TOK])
        shared = sb("sgl", 120, [P, 2, TOK])
        zg = sb("zg", 124, [P, 4, TOK])
        yh = sb("yh", 164, [P, 8, TOK], F32R)
        yl = sb("yl", 180, [P, 8, TOK], F32R)
        merge = sb("mt", 96, [P, 3, 2, TOK])
        merge_h = sb("mh", 132, [P, 8, TOK], F32R)
        merge_l = sb("ml", 148, [P, 8, TOK], F32R)

        def C(name):
            a, w = CONST_AT[name]
            return const[:, a:a + w]

        sel = C("sel").rearrange("p (a b) -> p a b", a=PAIRS)
        seln = C("seln").rearrange("p (a b) -> p a b", a=2)

        def bc(v, n=NCH):
            return v.unsqueeze(1).to_broadcast([P, n, v.shape[1]])

        def col(v):
            return v.unsqueeze(2).to_broadcast([P, v.shape[1], CH])

        def chunks(v):
            return v.rearrange("p (c t) -> p c t", t=CH)

        landed = [sem("landed0"), sem("landed1")]
        evac = [sem("evac0"), sem("evac1")]
        s = {name: sem(name) for name in SIGNALS}
        xr = [s["x_parts_even"], s["x_parts_odd"]]
        block = ctx.enter_context(nc.Block())

        BASE_E = BASE // 2
        E0_PER = (OFF_DN1 + OFF_DN2 - OFF_IN) // 2
        N_CHUNKS = BASE + LAYERS * PER + 2

        def n_evac(l, p, off):
            n = (min(off, OFF_DN1) + (max(off - OFF_IN, 0) if off <= OFF_DN2 else OFF_DN2 - OFF_IN)) // 2
            if p:
                n += max(min(off, OFF_IN) - OFF_DN1, 0) // 2 + max(off - OFF_DN2, 0) // 2
            return l * (E0_PER + p * 2 * KT) + BASE_E + n

        def c_no(l, off):
            return l * PER + BASE + off


        def eps_col(name):
            k = ("eps_ln", "eps2", "eps_l2").index(name)
            return cols[:, k:k + 1]


        IN_ROWS, IN_CQK, IN_CV, IN_AU, IN_AV, IN_CR, IN_Z = range(6, 13)


        def in_products_pe(l, pe, chunk_t, chunk_n, ready):
            te = nc.tensor
            for j in range(INP):
                pe.wait_ge(evac[j % 2], n_evac(l, j % 2, OFF_IN) + j // 2)
                if j in (IN_CV, IN_AV):
                    chunk_n(l, OFF_IN, j, j % 2)
                else:
                    chunk_t(l, OFF_IN, j, j % 2, 128 if j == IN_ROWS else 256, ready=None if j else ready)
                if 2 <= j < 6:
                    heads_norm_pe(pe, 2, l * 14 + 2 * (j - 2), first=(j == 2))
                if j == IN_CQK:
                    pe.wait_ge(evac[0], n_evac(l, 0, OFF_IN) + IN_ROWS // 2 + 1)
                    te.matmul(ps[:, 4, :], params[64:80, PK_UP:PK_UP + P], rows[64:80, :], start=True, stop=True).then_inc(s["gla_logits"], 1)
                if j == IN_Z:
                    pe.wait_ge(s["spatial_pool"], l * 3 + 3)
                    for a in range(2):
                        for t in range(4):
                            for b in range(2):
                                h = 2 * a + b
                                mm = te.matmul(ps[64 * b:64 * b + 64, 6 + a, t * P:(t + 1) * P], av[:, t, 64 * h:64 * h + 64],
                                               sgw[:, h, :], start=True, stop=True)
                        mm.then_inc(s["spatial_pe"], 1)

        def in_products_act(l, act, round_chunk):
            ac = nc.scalar
            into = {IN_AU: (au, ACT.Gelu_apprx_tanh), IN_AV: (av, ACT.Gelu_apprx_tanh), IN_Z: (zs[:, 0:2, :], ACT.Silu),
                    IN_Z + 1: (zs[:, 2:4, :], ACT.Silu), IN_CR: (cr, ACT.Silu)}
            for j in range(INP):
                p = j % 2
                n = c_no(l, OFF_IN) + j
                act.wait_ge(s["chunk_used"], n + 1)
                if j in into:
                    dst, fn = into[j]
                    if j == IN_AV:
                        src = ps[:, 2 * p:2 * p + 2, :].rearrange("p a (b c) -> p (a b) c", b=2)
                    else:
                        src = ps[:, 2 * p:2 * p + 2, :]
                    ac.activation(dst[:, :, :], src, fn).then_inc(evac[p], 1)
                if j < 6:
                    for k in range(2):
                        t = 2 * j + k
                        ac.activation(qkv[:, t, :], ps[:, 2 * p + k, :], ACT.Copy, scale=params[:, PK_CONV + 4 * t + 3:PK_CONV + 4 * t + 4]).then_inc(s["conv_first"], 1)
                round_chunk(n + 2, p)
                if 1 <= j <= 6:
                    conv_silu(l, act, j - 1)
                if 1 <= j < 5:
                    act.wait_ge(s["conv_silu"], l * 6 + j)
                    norm_squares(act, qk_tiles()[2 * j - 2:2 * j], l * 14 + 2 * (j - 1), first=(j == 1))
                if 2 <= j < 6:
                    norm_roots(act, 2, l * 14 + 2 * (j - 2), 64.0, eps_col("eps_l2"), first=(j == 2))
                if j == IN_CQK:
                    gates_act(l, act)
                if j == IN_AU:
                    act.wait_ge(s["gla_dve"], l * 16 + 3)
                    ac.activation(tmp[:, 0, :], bcum[:, :], ACT.Exp, scale=1 / 16).then_inc(s["gla_gate_act"], 1)
                    ac.activation(tmp[:, 1, :], bcum[:, :], ACT.Exp, scale=-1 / 16).then_inc(s["gla_gate_act"], 1)
                    ac.activation(gtA[:, :], chunks(bcum[:, :])[:, :, 63], ACT.Exp, scale=1 / 16).then_inc(s["gla_gate_act"], 1)
                    act.wait_ge(s["gla_dve"], l * 16 + 4)
                    ac.activation(tmp[:, 2, :], tmp[:, 2, :], ACT.Exp, scale=1 / 16).then_inc(s["gla_gate_act"], 1)
                if j == IN_CR:
                    act.wait_ge(s["spatial_dve"], l * 16 + 8)
                    ac.activation(sgt[:, :], mv[:, :, 1], ACT.Sqrt, bias=eps_col("eps2")).then_inc(s["spatial_std"], 1)

        def gates_act(l, act):
            ac = nc.scalar
            act.wait_ge(s["gla_logits"], l + 1)
            ac.activation(la[:, :], ps[:, 4, :], ACT.Abs, bias=params[:, PK_GB:PK_GB + 1]).then_inc(s["gla_gate_act"], 1)
            act.wait_ge(evac[0], n_evac(l, 0, OFF_IN) + IN_ROWS // 2 + 1)
            ac.activation(tmp[32:40, 3, :], rows[32:40, :], ACT.Abs, bias=params[32:40, PK_DT:PK_DT + 1]).then_inc(s["gate_act"], 1)
            act.wait_ge(s["gla_gate_act"], l * 7 + 1)
            ac.activation(la[:, :], la[:, :], ACT.Exp, scale=-1.0).then_inc(s["gla_gate_act"], 1)
            act.wait_ge(s["gate_act"], l * 5 + 1)
            ac.activation(tmp[32:40, 3, :], tmp[32:40, 3, :], ACT.Exp, scale=-1.0).then_inc(s["gate_act"], 1)
            ac.activation(exp_a[32:40, 0:1], params[32:40, PK_ALOG:PK_ALOG + 1], ACT.Exp).then_inc(s["gate_act"], 1)
            act.wait_ge(s["gla_gate_act"], l * 7 + 2)
            ac.activation(la[:, :], la[:, :], ACT.Ln, bias=1.0).then_inc(s["gla_gate_act"], 1)
            act.wait_ge(s["gate_act"], l * 5 + 2)
            ac.activation(tmp[32:40, 3, :], tmp[32:40, 3, :], ACT.Ln, bias=1.0).then_inc(s["gate_act"], 1)

        def conv_silu(l, act, q):
            act.wait_ge(evac[q % 2], n_evac(l, q % 2, OFF_IN) + q // 2 + 1)
            nc.scalar.activation(qkv[:, 2 * q:2 * q + 2, :], qkv[:, 2 * q:2 * q + 2, :], ACT.Silu).then_inc(s["conv_silu"], 1)

        def in_products_dve(l, dve, rest_chunk):
            ve = nc.vector
            for j in range(INP):
                p = j % 2
                n = c_no(l, OFF_IN) + j
                if j in (IN_ROWS, IN_CQK, IN_CV):
                    dve.wait_ge(s["chunk_used"], n + 1)
                    banks = ps[:, 2 * p:2 * p + 2, :]
                    if j == IN_CQK:
                        ve.tensor_copy(cqk[:, :, :], banks).then_inc(evac[p], 1)
                    if j == IN_CV:
                        ve.tensor_copy(cv[:, :, :], banks.rearrange("p a (b c) -> p (a b) c", b=2)).then_inc(evac[p], 1)
                    if j == IN_ROWS:
                        ve.tensor_copy(rows[:, :], ps[:, 2 * p, :]).then_inc(evac[p], 1)
                if j < 6:
                    q = j
                    m = 0
                    for tap in (2, 1, 0):
                        for k in range(2):
                            t = 2 * q + k
                            sh = 3 - tap
                            if tap == 2:
                                dve.wait_ge(s["conv_first"], l * 12 + 2 * q + k + 1)
                            else:
                                dve.wait_ge(s["conv_tap"], l * 30 + 5 * q + m - 1)
                            y = qkv[:, t, sh:TOK]
                            m += 1
                            c = PK_CONV + 4 * t + tap
                            ve.scalar_tensor_tensor(out=y, in0=ps[:, 2 * p + k, 0:TOK - sh], scalar=params[:, c:c + 1], in1=y,
                                                    op0=ALU.mult, op1=ALU.add).then_inc(*((s["conv_tap"], 1) if m < 6 else (evac[p], 1)))
                if 2 <= j < 6:
                    q = j - 2
                    heads_norm_dve(dve, qk_tiles()[2 * q:2 * q + 2], [0.125 if q < 2 else 1.0] * 2, l * 14 + 2 * q, first=(q == 0))
                if j == IN_CV:
                    gates_dve(l, dve)
                if j == IN_AU:
                    decayed_qk(l, dve)
                if j == IN_CR:
                    spatial_norm(l, dve)


        def gates_dve(l, dve):
            ve = nc.vector
            a0 = l * 16
            dve.wait_ge(s["gla_gate_act"], l * 7 + 3)
            ve.tensor_scalar(bcum[:, :], ps[:, 4, :], params[:, PK_GB:PK_GB + 1], 0.0, ALU.add, ALU.min).then_inc(s["gla_dve"], 1)
            dve.wait_ge(s["gla_dve"], a0 + 1)
            ve.tensor_tensor(la[:, :], bcum[:, :], la[:, :], ALU.subtract).then_inc(s["gla_dve"], 1)
            dve.wait_ge(s["gla_dve"], a0 + 2)
            ve.tensor_tensor_scan(bcum[:, :], C("keep"), la[:, :], 0.0, ALU.mult, ALU.add).then_inc(s["gla_dve"], 1)
            dve.wait_ge(s["gla_dve"], a0 + 3)
            ve.tensor_tensor(chunks(tmp[:, 2, :]), chunks(bcum[:, :])[:, :, 63].unsqueeze(2).to_broadcast([P, NCH, CH]), chunks(bcum[:, :]),
                             ALU.subtract).then_inc(s["gla_dve"], 1)
            dve.wait_ge(s["gate_act"], l * 5 + 4)
            ve.tensor_scalar(rows[32:40, :], rows[32:40, :], params[32:40, PK_DT:PK_DT + 1], 0.0, ALU.add, ALU.max).then_inc(s["gate_dve"], 1)
            dve.wait_ge(s["gate_dve"], l * 4 + 1)
            ve.tensor_tensor(rows[32:40, :], rows[32:40, :], tmp[32:40, 3, :], ALU.add).then_inc(s["gate_dve"], 1)
            dve.wait_ge(s["gate_dve"], l * 4 + 2)
            ve.tensor_scalar(rows[32:40, :], rows[32:40, :], exp_a[32:40, 0:1], -1.0, ALU.mult, ALU.mult).then_inc(s["gate_dve"], 1)
            dve.wait_ge(s["gate_dve"], l * 4 + 3)
            ve.tensor_tensor_scan(decay_sum[32:40, :], C("keep")[32:40, :], rows[32:40, :], 0.0, ALU.mult, ALU.add).then_inc(s["gate_dve"], 1)

        def decayed_qk(l, dve):
            ve = nc.vector
            a0 = l * 16
            dve.wait_ge(s["gla_gate_act"], l * 7 + 5)
            ve.scalar_tensor_tensor(out=cqk[:, 0, :], in0=cqk[:, 0, :], scalar=32.0 ** -0.5, in1=tmp[:, 0, :], op0=ALU.mult, op1=ALU.mult).then_inc(s["gla_dve"], 1)
            ve.tensor_tensor(tmp[:, 1, :], tmp[:, 1, :], cqk[:, 1, :], ALU.mult).then_inc(s["gla_dve"], 1)
            dve.wait_ge(s["gla_gate_act"], l * 7 + 7)
            dve.wait_ge(s["gla_dve"], a0 + 6)
            ve.tensor_tensor(cqk[:, 1, :], cqk[:, 1, :], tmp[:, 2, :], ALU.mult).then_inc(s["gla_dve"], 1)

        def spatial_norm(l, dve):
            ve = nc.vector
            g0 = l * 16
            dve.wait_ge(evac[0], n_evac(l, 0, OFF_IN) + IN_AV // 2 + 1)
            for t in range(4):
                ve.bn_stats(stat[:, t, :], av[:, t, :]).then_inc(s["spatial_dve"], 1)
            for t in range(4):
                dve.wait_ge(s["spatial_dve"], g0 + t + 1)
                dve.sem_inc(s["apart_dve"], 1)
                ve.bn_aggr(mv[:, t, :], stat[:, t, :]).then_inc(s["spatial_dve"], 1)
            dve.wait_ge(s["spatial_std"], l + 1)
            ve.reciprocal(sgt[:, :], sgt[:, :]).then_inc(s["spatial_dve"], 1)
            dve.wait_ge(s["spatial_dve"], g0 + 9)
            for t in range(4):
                ve.tensor_scalar(av[:, t, :], av[:, t, :], mv[:, t, 0:1], sgt[:, t:t + 1], ALU.subtract, ALU.mult).then_inc(s["spatial_dve"], 1)

        def norm_squares(act, tiles, n0, first=False, t0=0):
            for t, tile in enumerate(tiles):
                if not first:
                    act.wait_ge(s["head_ms"], n0 + t - 1)
                nc.scalar.activation(tmp[:, (t0 + t) % 2, :], tile, ACT.Square).then_inc(s["head_square"], 1)

        def norm_roots(act, tiles, n0, scale, eps, first=False, t0=0):
            for t in range(tiles):
                act.wait_ge(s["head_ms"], n0 + t + 1)
                if not first:
                    act.wait_ge(s["head_rstd"], n0 + t - 1)
                nc.scalar.activation(tmp[:, 2 + (t0 + t) % 2, :], ps[:, 6 + (t0 + t) % 2, :], ACT.Sqrt, scale=scale, bias=eps).then_inc(s["head_std"], 1)

        def heads_norm_act(act, tiles, n0, scale, eps):
            for t in range(len(tiles) + 1):
                if t < len(tiles):
                    norm_squares(act, tiles[t:t + 1], n0 + t, t0=t)
                if t:
                    norm_roots(act, 1, n0 + t - 1, scale, eps, t0=t - 1)

        def heads_norm_pe(pe, n_tiles, n0, first=False):
            for t in range(n_tiles):
                n = n0 + t
                pe.wait_ge(s["head_square"], n + 1)
                if not first:
                    pe.wait_ge(s["head_std"], n - 1)
                nc.tensor.matmul(ps[:, 6 + t % 2, :], C("head_mean"), tmp[:, t % 2, :], start=True, stop=True).then_inc(s["head_ms"], 1)

        def heads_norm_dve(dve, tiles, factors, n0, then=None, first=False):
            for t in range(len(tiles)):
                n = n0 + t
                dve.wait_ge(s["head_std"], n + 1)
                if not first:
                    dve.wait_ge(s["head_normed"], n - 1)
                nc.vector.reciprocal(tmp[:, 4 + t % 2, :], tmp[:, 2 + t % 2, :]).then_inc(s["head_rstd"], 1)
                dve.wait_ge(s["head_rstd"], n + 1)
                nc.vector.scalar_tensor_tensor(out=tiles[t], in0=tiles[t], scalar=factors[t], in1=tmp[:, 4 + t % 2, :],
                                               op0=ALU.mult, op1=ALU.mult).then_inc(s["head_normed"], 1)
                if then:
                    dve.wait_ge(s["head_normed"], n + 1)
                    then(t)

        def qk_tiles():
            return [qkv[:, t, :] for t in range(8)]

        def o_tiles():
            return [oT[:, pr, :] for pr in range(PAIRS)]

        def oA_tiles():
            return [oA[:, a, :] for a in range(2)]

        def mixer_pe(l, pe):
            te = nc.tensor
            hn = l * 14
            for p in range(2):
                pe.wait_ge(evac[p], n_evac(l, p, OFF_IN) + INP // 2)
            pe.wait_ge(s["gla_dve"], l * 16 + 6)
            for c in range(NCH):
                for h in range(4):
                    mm = te.matmul(ps[64 * (c % 2):64 * (c % 2) + 64, h, (c // 2) * CH:(c // 2 + 1) * CH],
                                   tmp[32 * h:32 * h + 32, 1, c * CH:(c + 1) * CH],
                                   cqk[32 * h:32 * h + 32, 0, c * CH:(c + 1) * CH], start=True, stop=True)
            mm.then_inc(s["gla_pe"], 1)
            pe.wait_ge(s["gla_dve"], l * 16 + 7)
            for t in range(4):
                mm = te.transpose(ps[:, 5, t * P:(t + 1) * P], cqk[:, 1, t * P:(t + 1) * P], C("ident"))
            mm.then_inc(s["gla_pe"], 1)
            pe.wait_ge(s["gla_keys"], l + 1)
            pe.wait_ge(s["spatial_dve"], l * 16 + 16)
            pe.sem_inc(s["apart_pe"], 1)
            for c in range(NCH):
                b, t = 64 * (c % 2), c // 2
                for h in range(4):
                    mm = te.matmul(ps[32 * h:32 * h + 32, 6 + c % 2, t * CH:(t + 1) * CH], kdA[b:b + 64, t, 32 * h:32 * h + 32],
                                   cv[b:b + 64, t, 64 * h:64 * h + 64], start=True, stop=True)
            mm.then_inc(s["gla_pe"], 1)
            pe.wait_ge(s["gla_dve"], l * 16 + 16)
            for c in range(NCH):
                b, t = 64 * (c % 2), c // 2
                for h in range(4):
                    dst = ps[64 * (h % 2):64 * (h % 2) + 64, 2 * (h // 2) + c % 2, t * CH:(t + 1) * CH]
                    te.matmul(dst, stA[32 * h:32 * h + 32, c, :], cqk[32 * h:32 * h + 32, 0, c * CH:(c + 1) * CH], start=True, stop=False)
                    mm = te.matmul(dst, cv[b:b + 64, t, 64 * h:64 * h + 64], pA[b:b + 64, h, t, :], start=False, stop=True)
            mm.then_inc(s["gla_pe"], 1)
            heads_norm_pe(pe, 2, hn + 8)

            pe.wait_ge(s["head_std"], l * 14 + 10)
            pe.sem_inc(s["apart_pe"], 1)
            for src, b0 in ((kT, 0), (vT, 4)):
                for pr in range(PAIRS):
                    for c in range(NCH):
                        for b in (0, 64):
                            mm = te.matmul(ps[b:b + 64, b0 + pr, c * CH:(c + 1) * CH], src[b:b + 64, pr, c * CH:(c + 1) * CH],
                                           C("eye64")[b:b + 64, :], start=True, stop=True)
                mm.then_inc(s["by_token_ps"], 1)
            pe.wait_ge(s["by_token_sb"], l * 2 + 2)
            pe.wait_ge(s["gate_dve"], l * 4 + 4)
            pe.wait_ge(s["gate_act"], l * 5 + 5)
            for base_, bank in ((32, 4), (0, 5)):
                for c in range(NCH):
                    for b in range(2):
                        mm = te.matmul(ps[64 * b:64 * b + 64, bank, c * PAIRS:(c + 1) * PAIRS], decay_sum[base_:base_ + 8, c * CH:(c + 1) * CH],
                                       seln[base_:base_ + 8, b, :], start=True, stop=True)
            mm.then_inc(s["columns_ps"], 1)
            for pr in range(PAIRS):
                b4 = 4 * (pr % 2)
                if pr == 1:
                    pe.wait_ge(s["columns_sb"], l * 2 + 2)
                if pr >= 2:
                    pe.wait_ge(s["pair_dve"], l * PAIR_DVE * PAIRS + (pr - 2) * PAIR_DVE + 12)
                te.matmul(ps[:, b4, :], sel[32:40, pr, :], decay_sum[32:40, :], start=True, stop=True)
                te.matmul(ps[:, b4 + 1, :], sel[0:8, pr, :], decay_sum[0:8, :], start=True, stop=True)
                for c in range(NCH):
                    for b in (0, 64):
                        te.matmul(ps[b:b + 64, b4 + 2, c * CH:(c + 1) * CH], kT[b:b + 64, pr, c * CH:(c + 1) * CH],
                                  kT[b:b + 64, pr, c * CH:(c + 1) * CH], start=True, stop=True)
                for c in range(NCH):
                    for b in (0, 64):
                        mm = te.matmul(ps[b:b + 64, b4 + 3, c * CH:(c + 1) * CH], kT[b:b + 64, pr, c * CH:(c + 1) * CH],
                                       qT[b:b + 64, pr, c * CH:(c + 1) * CH], start=True, stop=True)
                mm.then_inc(s["pair_ps"], 1)
            pe.wait_ge(s["pair_dve"], (l + 1) * PAIR_DVE * PAIRS)
            pe.sem_inc(s["apart_pe"], 1)

            def level(lev, last):
                for pr in range(PAIRS):
                    pe.wait_ge(s["level_l"], l * 20 + lev * 4 + pr + 1)
                    pe.wait_ge(s["level_t"], l * LV_DVE + lev * 8 + 2 * pr + 1)
                    pe.sem_inc(s["apart_pe"], 1)
                    for c in range(NCH):
                        for b in (0, 64):
                            mm = te.matmul(ps[b:b + 64, pr, c * CH:(c + 1) * CH], tmp[b:b + 64, pr, c * CH:(c + 1) * CH],
                                           Tm[b:b + 64, pr, c, :], start=True, stop=True)
                    mm.then_inc(s["level_x"], 1)
                for pr in range(PAIRS):
                    pe.wait_ge(s["level_x_sb"], l * 20 + lev * 4 + pr + 1)
                    pe.wait_ge(s["level_t"], l * LV_DVE + lev * 8 + (pr + 7 if last and pr >= 2 else 2 * pr + 6))
                    pe.sem_inc(s["apart_pe"], 1)
                    for a, (lt, rt) in enumerate(((TT, Xb), (Xb, TT))):
                        if a or not last:
                            for c in range(NCH):
                                for b in (0, 64):
                                    mm = te.matmul(ps[b:b + 64, 4 + 2 * (pr % 2) + a, c * CH:(c + 1) * CH], lt[b:b + 64, pr, c, :],
                                                   rt[b:b + 64, pr, c, :], start=True, stop=True)
                    mm.then_inc(s["level_tx"], 1)
            with pe.Fori(0, 4) as lev:
                level(lev, False)
            level(4, True)
            pe.wait_ge(s["level_t"], l * LV_DVE + 8 + LV_DVE)
            pe.wait_ge(s["factor_dve"], l * 6 + 6)
            pe.sem_inc(s["apart_pe"], 1)
            for pr in range(PAIRS):
                for c in range(NCH):
                    for b in (0, 64):
                        mm = te.matmul(ps[b:b + 64, pr, c * CH:(c + 1) * CH], bk[b:b + 64, pr, c, :], TT[b:b + 64, pr, c, :], start=True, stop=True)
            mm.then_inc(s["wu_ps"], 1)
            for pr in range(PAIRS):
                for c in range(NCH):
                    for b in (0, 64):
                        mm = te.matmul(ps[b:b + 64, 4 + pr, c * CH:(c + 1) * CH], TT[b:b + 64, pr, c, :], vN[b:b + 64, pr, c, :], start=True, stop=True)
            mm.then_inc(s["wu_ps"], 1)
            pe.wait_ge(s["wu_sb"], l * 2 + 2)
            pe.sem_inc(s["apart_pe"], 1)
            HEADS = [(pr, b) for pr in range(PAIRS) for b in (0, 64)]
            for c in range(NCH):
                st = state[:, c % 2]
                pe.wait_ge(s["rec_state"], l * 9 + c + 1)
                pe.sem_inc(s["apart_pe"], 1)
                for pr, b in HEADS:
                    mm = te.matmul(ps[b:b + 64, 0, pr * CH:(pr + 1) * CH], nwT[b:b + 64, pr, c, :], st[b:b + 64, pr, :], start=True, stop=True)
                mm.then_inc(s["rec_u"], 1)
                if c >= 2:
                    pe.wait_ge(s["rec_out_sb"], l * 8 + c - 1)
                    pe.sem_inc(s["apart_pe"], 1)
                out_at = [ps[b:b + 64, 1 + c % 2, pr * CH:(pr + 1) * CH] for pr, b in HEADS]
                for dst, (pr, b) in zip(out_at, HEADS):
                    te.matmul(dst, st[b:b + 64, pr, :], qT[b:b + 64, pr, c * CH:(c + 1) * CH], start=(pr == 0), stop=False)
                pe.wait_ge(s["rec_unew"], l * 8 + c + 1)
                pe.sem_inc(s["apart_pe"], 1)
                for pr, b in HEADS:
                    mm = te.matmul(ps[b:b + 64, 3, pr * CH:(pr + 1) * CH], kN[b:b + 64, pr, c, :], unew[b:b + 64, pr, :], start=True, stop=True)
                mm.then_inc(s["rec_increment"], 1)
                for dst, (pr, b) in zip(out_at, HEADS):
                    mm = te.matmul(dst, unew[b:b + 64, pr, :], pT[b:b + 64, pr, c, :], start=False, stop=(pr == PAIRS - 1))
                mm.then_inc(s["rec_out"], 1)
            heads_norm_pe(pe, 4, hn + 10)

        def mixer_act(l, act):
            ac = nc.scalar
            hn = l * 14
            act.wait_ge(s["gla_pe"], l * 4 + 2)
            ac.activation(kdA[:, :, :].rearrange("p a b -> p (a b)"), ps[:, 5, :], ACT.Copy).then_inc(s["gla_keys"], 1)
            act.wait_ge(s["gla_pe"], l * 4 + 4)
            for a in range(2):
                for b in range(2):
                    ac.activation(oA[:, a, :].rearrange("p (t b i) -> p b t i", b=2, i=CH)[:, b], ps[:, 2 * a + b, 0:256].rearrange("p (t i) -> p t i", i=CH),
                                  ACT.Copy).then_inc(s["gla_out"], 1)
            act.wait_ge(s["gla_out"], l * 4 + 4)
            heads_norm_act(act, oA_tiles(), hn + 8, 1.0, eps_col("eps2"))
            ac.activation(decay_sum[0:8, :], rows[0:8, :], ACT.Sigmoid).then_inc(s["gate_act"], 1)
            mix_hi(l, act, ((0, au[:, 0, :], "spatial_done", 1), (1, au[:, 1, :], "spatial_done", 2), (6, cr[:, 0, :], "gla_done", 1), (7, cr[:, 1, :], "gla_done", 2)))

            act.wait_ge(s["by_token_ps"], l * 2 + 1)
            ac.activation(kN[:, :, :, :], ps[:, 0:4, :].rearrange("p a (c t) -> p a c t", t=CH), ACT.Copy).then_inc(s["by_token_sb"], 1)
            for pr in range(PAIRS):
                b4, d0 = 4 * (pr % 2), l * PAIR_DVE * PAIRS + pr * PAIR_DVE
                act.wait_ge(s["pair_dve"], d0 + 2)
                ac.activation(tmp[:, 1, :], ps[:, b4, :], ACT.Exp).then_inc(s["pair_act"], 1)
                act.wait_ge(s["pair_dve"], d0 + 3)
                ac.activation(tmp[:, 2, :], tmp[:, 2, :], ACT.Exp).then_inc(s["pair_act"], 1)
                act.wait_ge(s["pair_dve"], d0 + 4)
                ac.activation(tmp[:, 0, :], tmp[:, 0, :], ACT.Exp, scale=-1.0).then_inc(s["pair_act"], 1)
            act.wait_ge(s["pair_dve"], (l + 1) * PAIR_DVE * PAIRS)
            ac.activation(gtot[:, :, :], glast[:, :, :], ACT.Exp).then_inc(s["factor_act"], 1)
            ac.activation(egN[:, :, :], gN[:, :, :], ACT.Exp).then_inc(s["factor_act"], 1)
            act.wait_ge(s["factor_dve"], l * 6 + 1)
            ac.activation(kdN[:, :, :], kdN[:, :, :], ACT.Exp).then_inc(s["factor_act"], 1)
            with act.Fori(0, 5) as lev:
                for pr in range(PAIRS):
                    act.wait_ge(s["level_x"], l * 20 + lev * 4 + pr + 5)
                    act.wait_ge(s["level_tx"], l * 20 + lev * 4 + pr + 1)
                    ac.activation(Xb[:, pr, :, :], chunks(ps[:, pr, :]), ACT.Copy).then_inc(s["level_x_sb"], 1)
            act.wait_ge(s["wu_ps"], l * 2 + 1)
            ac.activation(nwT[:, :, :, :], ps[:, 0:4, :].rearrange("p a (c t) -> p a c t", t=CH), ACT.Copy, scale=-1.0).then_inc(s["wu_sb"], 1)
            for c in range(NCH):
                act.wait_ge(s["rec_out"], l * 8 + c + 1)
                ac.activation(oT[:, :, c * CH:(c + 1) * CH], ps[:, 1 + c % 2, 0:256].rearrange("p (a t) -> p a t", t=CH), ACT.Copy).then_inc(s["rec_out_sb"], 1)
            act.wait_ge(s["rec_out_sb"], l * 8 + 8)
            act.wait_ge(s["rec_state"], l * 9 + 9)
            heads_norm_act(act, o_tiles(), hn + 10, 1.0, eps_col("eps2"))
            mix_hi(l, act, [(2 + pr, oT[:, pr, :], "delta_done", pr + 1) for pr in range(PAIRS)])

        def mix_hi(l, act, tiles):
            for k, src, name, n in tiles:
                act.wait_ge(s[name], l * {"spatial_done": 2, "delta_done": 4, "gla_done": 2}[name] + n)
                nc.scalar.activation(xh[:, k, :], src, ACT.Copy).then_inc(s["mixed_hi"], 1)

        def mix_rest(l, pool, tiles, n0):
            for m, (k, src) in enumerate(tiles):
                pool.wait_ge(s["mixed_hi"], l * 8 + n0 + m + 1)
                nc.gpsimd.tensor_tensor(xl[:, k, :], src, xh[:, k, :].bitcast(F32), ALU.subtract).then_inc(s["mixed_lo"], 1)

        def mixer_pool(l, pool):
            gp = nc.gpsimd
            for j in range(IN_CR + 1):
                rest(pool, c_no(l, OFF_IN) + j + 2, j % 2)
                if j == 2:
                    pool.wait_ge(s["spatial_params_in"], l * 16 + 16)
                    gp.tensor_tensor(sgw, sgw, C("upper128").unsqueeze(1).to_broadcast([P, 4, P]), ALU.mult).then_inc(s["spatial_pool"], 1)
            pool.wait_ge(s["spatial_dve"], l * 16 + 13)
            gp.tensor_tensor(av[:, :, :], av[:, :, :], sgp[:, SG_G:SG_G + 256].unsqueeze(1).to_broadcast([P, 4, 256]), ALU.mult).then_inc(s["spatial_pool"], 1)
            pool.wait_ge(s["spatial_pool"], l * 3 + 2)
            gp.tensor_tensor(av[:, :, :], av[:, :, :], sgp[:, SG_B:SG_B + 256].unsqueeze(1).to_broadcast([P, 4, 256]), ALU.add).then_inc(s["spatial_pool"], 1)
            for j in (IN_Z, IN_Z + 1):
                rest(pool, c_no(l, OFF_IN) + j + 2, j % 2)
            mix_rest(l, pool, ((0, au[:, 0, :]), (1, au[:, 1, :]), (6, cr[:, 0, :]), (7, cr[:, 1, :])), 0)
            for pr in range(PAIRS):
                d0 = l * PAIR_DVE * PAIRS + pr * PAIR_DVE
                pool.wait_ge(s["pair_dve"], d0 + 6)
                gp.tensor_tensor(pT[:, pr], pT[:, pr], bc(C("upper64")), ALU.mult).then_inc(s["pair_pool"], 1)
                pool.wait_ge(s["pair_dve"], d0 + 10)
                gp.tensor_tensor(TT[:, pr], bc(C("eye64")), chunks(tmp[:, 5, :]), ALU.subtract).then_inc(s["pair_pool"], 1)
                pool.wait_ge(s["pair_dve"], d0 + 13)
                gp.tensor_tensor(Tm[:, pr], bc(C("eye64")), chunks(tmp[:, 4, :]), ALU.subtract).then_inc(s["pair_pool"], 1)
            a0 = CONST_AT["upT2"][0]
            with pool.Fori(0, 5) as lev:
                for pr in range(PAIRS):
                    pool.wait_ge(s["level_x"], l * 20 + lev * 4 + pr + 1)
                    pool.sem_inc(s["apart_pool"], 1)
                    gp.tensor_tensor(chunks(tmp[:, pr, :]), LT[:, pr], bc(const[:, bass.ds(lev * 64 + a0, 64)]), ALU.mult).then_inc(s["level_l"], 1)
            mix_rest(l, pool, [(2 + pr, oT[:, pr, :]) for pr in range(PAIRS)], 4)

        def mixer_dve(l, dve):
            ve = nc.vector
            hn = l * 14
            a0 = l * 16
            for a in range(2):
                dve.wait_ge(s["spatial_pe"], l * 2 + a + 1)
                z4 = ps[:, 6 + a, :].rearrange("p (t i) -> p t i", i=P)
                bs = sgp[:, SG_BS + a * P:SG_BS + (a + 1) * P].unsqueeze(1).to_broadcast([P, 4, P])
                ve.tensor_tensor(z4, z4, bs, ALU.add).then_inc(s["spatial_dve"], 1)
                dve.wait_ge(s["spatial_dve"], a0 + 14 + a)
                ve.tensor_tensor(au[:, a, :], au[:, a, :], ps[:, 6 + a, :], ALU.mult).then_inc(s["spatial_done"], 1)
            dve.wait_ge(s["spatial_done"], l * 2 + 2)
            ve.memset(stA[:, 0, :], 0.0).then_inc(s["spatial_dve"], 1)
            dve.wait_ge(s["gla_pe"], l * 4 + 1)
            up4 = C("upper64").unsqueeze(1).to_broadcast([P, 16, CH])
            for h in range(4):
                ve.tensor_tensor(pA[:, h], ps[:, h, 0:256].rearrange("p (t i) -> p t i", i=CH), up4[:, 0:4, :], ALU.mult).then_inc(*((s["gla_dve"], 1) if h == 3 else (s["gla_scores"], 1)))
            dve.wait_ge(s["gla_pe"], l * 4 + 3)
            for c in range(NCH - 1):
                ve.scalar_tensor_tensor(out=stA[:, c + 1, :], in0=stA[:, c, :], scalar=gtA[:, c:c + 1], in1=ps[:, 6 + c % 2, (c // 2) * CH:(c // 2 + 1) * CH],
                                        op0=ALU.mult, op1=ALU.add).then_inc(s["gla_dve"], 1)
                dve.wait_ge(s["gla_dve"], a0 + 9 + c)
            ve.memset(state[:, 0], 0.0).then_inc(s["rec_state"], 1)
            ve.memset(exp_a[0:1, 1:2], 0.0).then_inc(s["gla_dve"], 1)

            def gate(a):
                ve.tensor_tensor(cr[:, a, :], cr[:, a, :], oA[:, a, :], ALU.mult).then_inc(s["gla_done"], 1)
            heads_norm_dve(dve, oA_tiles(), [params[:, PK_LAN:PK_LAN + 1]] * 2, hn + 8, gate)

            dve.wait_ge(s["by_token_ps"], l * 2 + 2)
            dve.wait_ge(s["gla_done"], l * 2 + 2)
            ve.tensor_copy(vN[:, :, :, :], ps[:, 4:8, :].rearrange("p a (c t) -> p a c t", t=CH)).then_inc(s["by_token_sb"], 1)
            dve.wait_ge(s["columns_ps"], l + 1)
            ve.tensor_copy(gN[:, :, :].rearrange("p a b -> p (a b)"), ps[:, 4, 0:32]).then_inc(s["columns_sb"], 1)
            ve.tensor_copy(bN[:, :, :].rearrange("p a b -> p (a b)"), ps[:, 5, 0:32]).then_inc(s["columns_sb"], 1)
            dve.wait_ge(s["columns_sb"], l * 2 + 2)
            for pr in range(PAIRS):
                b4, d0 = 4 * (pr % 2), l * PAIR_DVE * PAIRS + pr * PAIR_DVE
                a1 = l * 12 + pr * 3
                p0 = (l * PAIRS + pr) * 3
                R, bR, kk, qk = (chunks(ps[:, b4 + m, :]) for m in range(4))

                def done(n):
                    dve.wait_ge(s["pair_dve"], d0 + n)
                dve.wait_ge(s["pair_ps"], l * 4 + pr + 1)
                ve.tensor_tensor(chunks(tmp[:, 0, :]), R, col(gN[:, :, pr]), ALU.subtract).then_inc(s["pair_dve"], 1)
                ve.tensor_copy(glast[:, :, pr], R[:, :, 63]).then_inc(s["pair_dve"], 1)
                done(1)
                ve.tensor_scalar(tmp[:, 2, :], tmp[:, 0, :], 0.0, None, ALU.min).then_inc(s["pair_dve"], 1)
                done(3)
                ve.tensor_scalar(tmp[:, 0, :], tmp[:, 0, :], 0.0, None, ALU.max).then_inc(s["pair_dve"], 1)
                dve.wait_ge(s["pair_act"], a1 + 1)
                ve.tensor_tensor(qT[:, pr, :], qT[:, pr, :], tmp[:, 1, :], ALU.mult).then_inc(s["pair_dve"], 1)
                dve.wait_ge(s["pair_act"], a1 + 2)
                ve.tensor_tensor(pT[:, pr], qk, chunks(tmp[:, 2, :]), ALU.mult).then_inc(s["pair_dve"], 1)
                ve.tensor_tensor(chunks(tmp[:, 3, :]), chunks(tmp[:, 2, :]), bc(C("strict64")), ALU.mult).then_inc(s["pair_dve"], 1)
                done(7)
                ve.tensor_tensor(chunks(tmp[:, 3, :]), chunks(tmp[:, 3, :]), bR, ALU.mult).then_inc(s["pair_dve"], 1)
                done(8)
                if pr == 0:
                    dve.wait_ge(s["mixed_lo"], l * 8 + 4)
                ve.tensor_tensor(LT[:, pr], chunks(tmp[:, 3, :]), kk, ALU.mult).then_inc(s["pair_dve"], 1)
                done(9)
                if pr:
                    dve.wait_ge(s["pair_pool"], p0 - 1)
                ve.tensor_tensor(chunks(tmp[:, 5, :]), LT[:, pr], bc(C("upT1")), ALU.mult).then_inc(s["pair_dve"], 1)
                dve.wait_ge(s["pair_act"], a1 + 3)
                ve.tensor_tensor(chunks(tmp[:, 0, :]), chunks(tmp[:, 0, :]), col(bN[:, :, pr]), ALU.mult).then_inc(s["pair_dve"], 1)
                done(11)
                if pr:
                    dve.wait_ge(s["pair_pool"], p0)
                ve.tensor_tensor(chunks(tmp[:, 4, :]), chunks(tmp[:, 0, :]), kk, ALU.mult).then_inc(s["pair_dve"], 1)
                done(12)
                ve.tensor_tensor(chunks(tmp[:, 4, :]), chunks(tmp[:, 4, :]), bc(C("low1")), ALU.mult).then_inc(s["pair_dve"], 1)
            k0 = l * 6
            ve.tensor_tensor(kdN[:, :, :], glast[:, :, :], gN[:, :, :], ALU.subtract).then_inc(s["factor_dve"], 1)
            dve.wait_ge(s["factor_act"], l * 3 + 2)
            ve.tensor_tensor(bgN[:, :, :], bN[:, :, :], egN[:, :, :], ALU.mult).then_inc(s["factor_dve"], 1)

            def by_token(v):
                return v[:, :, :].rearrange("p c a -> p a c").unsqueeze(3).to_broadcast([P, PAIRS, NCH, CH])
            dve.wait_ge(s["factor_dve"], k0 + 2)
            ve.tensor_tensor(bk[:, :, :, :], kN[:, :, :, :], by_token(bgN), ALU.mult).then_inc(s["factor_dve"], 1)
            dve.wait_ge(s["factor_act"], l * 3 + 3)
            dve.wait_ge(s["factor_dve"], k0 + 3)
            ve.tensor_tensor(kN[:, :, :, :], kN[:, :, :, :], by_token(kdN), ALU.mult).then_inc(s["factor_dve"], 1)
            ve.tensor_tensor(vN[:, :, :, :], vN[:, :, :, :], by_token(bN), ALU.mult).then_inc(s["factor_dve"], 1)
            ve.memset(exp_a[0:1, 3:4], 0.0).then_inc(s["factor_dve"], 1)

            def level(lev, last):
                for pr in range(PAIRS):
                    dve.wait_ge(s["level_tx"], l * 20 + lev * 4 + pr + 5)
                    for a, M in enumerate((Tm, TT)):
                        if a or not last:
                            ve.tensor_tensor(M[:, pr], M[:, pr], chunks(ps[:, 4 + 2 * (pr % 2) + a, :]), ALU.subtract).then_inc(s["level_t"], 1)
            with dve.Fori(0, 4) as lev:
                level(lev, False)
            level(4, True)
            dve.wait_ge(s["wu_ps"], l * 2 + 2)
            ve.tensor_copy(u_own[:, :, :, :], ps[:, 4:8, :].rearrange("p a (c t) -> p a c t", t=CH)).then_inc(s["wu_sb"], 1)
            dve.wait_ge(s["wu_sb"], l * 2 + 2)
            for c in range(NCH):
                dve.wait_ge(s["rec_u"], l * 8 + c + 1)
                if c:
                    dve.wait_ge(s["rec_out"], l * 8 + c)
                ve.tensor_tensor(unew[:, :, :], u_own[:, :, c, :], ps[:, 0, 0:256].rearrange("p (a t) -> p a t", t=CH), ALU.add).then_inc(s["rec_unew"], 1)
                dve.wait_ge(s["rec_state"], l * 9 + c + 1)
                if c:
                    dve.wait_ge(s["rec_decayed"], l * 8 + c)
                ve.tensor_tensor(tmp[:, 0, 0:256].rearrange("p (a t) -> p a t", t=CH), state[:, c % 2], gtot[:, c, :].unsqueeze(2).to_broadcast([P, PAIRS, CH]),
                                 ALU.mult).then_inc(s["rec_decayed"], 1)
                dve.wait_ge(s["rec_decayed"], l * 8 + c + 1)
                dve.wait_ge(s["rec_increment"], l * 8 + c + 1)
                ve.tensor_tensor(state[:, (c + 1) % 2], tmp[:, 0, 0:256].rearrange("p (a t) -> p a t", t=CH), ps[:, 3, 0:256].rearrange("p (a t) -> p a t", t=CH),
                                 ALU.add).then_inc(s["rec_state"], 1)

            def gate_z(pr):
                ve.tensor_tensor(oT[:, pr, :], oT[:, pr, :], zs[:, pr, :], ALU.mult).then_inc(s["delta_done"], 1)
            dve.wait_ge(s["rec_out_sb"], l * 8 + 8)
            heads_norm_dve(dve, o_tiles(), [params[:, PK_GN:PK_GN + 1]] * 4, hn + 10, gate_z)


        def view(v, r):
            return v.rearrange("p (l r) -> p r l", r=r)

        def own(v, r):
            return v.rearrange("p (r l) -> p r l", r=r)

        def key_tiles(g, i):
            return [j for j in (i - 1, i, i + 1) if 0 <= j < 4] if WIDE[g] else [i]

        def bias_of(g, h, i):
            if not WIDE[g]:
                return (bias_near, bias_far)[g == 3][:, h, :]
            a = P if i == 0 else 0
            return bias_wide[:, h, a:a + P * len(key_tiles(g, i))]

        def rest(pool, n, p):
            pool.wait_ge(s["chunk_hi"], n + 1)
            pool.wait_ge(s["chunk_lo"], n)
            nc.gpsimd.tensor_tensor(wl[:, p, :], raw[:, p, :], wh[:, p, :].bitcast(F32), ALU.subtract).then_inc(s["chunk_lo"], 1)

        def block1_pool(pool):
            gp = nc.gpsimd
            pool.dma_start(rel_table[0:32, :], rel).then_inc(s["rel_in"], 16)
            pool.dma_start(params1[:, :], p1).then_inc(s["first_params_in"], 16)
            for k in range(KT):
                pool.wait_ge(s["h_tile_hi"], k + 1)
                gp.tensor_tensor(xl[:, k, :], h_new[:, k % 4, :], xh[:, k, :].bitcast(F32), ALU.subtract).then_inc(s["h_tile_lo"], 1)
            pool.wait_ge(s["bias_row"], 2)
            for g in range(4):
                src = bias_rows[8 * (g % 2):8 * (g % 2) + 8, g // 2, :].unsqueeze(1).to_broadcast([8, P, 512])
                pool.dma_start(bias_dram[g].rearrange("m h r -> h m r"), src).then_inc(s["bias_dram"], 16)
            for n in range(2):
                rest(pool, n + 2, n)
            pool.wait_ge(s["bias_dram"], 64)

            def toeplitz(g, dst, p0, n, m0, m, first):
                src = bass.AP(bias_dram_t, g * P * 8 * 512 + first, [[8 * 512 - 1, n], [512, 8], [1, m]])
                return pool.dma_start(dst[p0:p0 + n, :, m0:m0 + m], src)
            toeplitz(0, bias_wide, 0, P, 0, 384, 127).then_inc(s["bias_wide"], 16)
            toeplitz(2, bias_near, 0, P, 0, P, 127).then_inc(s["bias_near"], 16)
            toeplitz(3, bias_far, 0, P, 0, P, 127).then_inc(s["bias_far"], 16)
            n = 0
            for gi, g in enumerate(ORDER):
                for kind in KINDS[g]:
                    if n >= 2:
                        rest(pool, n + 2, n % 2)
                    n += 1
                if gi == 0:
                    pool.wait_ge(s["att_logits"], 32)
                    toeplitz(1, bias_wide, 0, P, 0, 384, 127).then_inc(s["bias_wide"], 16)
            for pr in range(PAIRS):
                pool.wait_ge(s["y_weighted"], 4 * pr + 4)
                gp.tensor_tensor(group_out[:, 1, pr, :], group_out[:, 1, pr, :], group_out[:, 2, pr, :], ALU.add).then_inc(s["y_sum"], 1)
                pool.wait_ge(s["y_sum"], 2 * pr + 1)
                gp.tensor_tensor(group_out[:, 1, pr, :], group_out[:, 1, pr, :], group_out[:, 3, pr, :], ALU.add).then_inc(s["y_sum"], 1)
                for b in range(2):
                    k = 2 * pr + b
                    pool.wait_ge(s["y_hi"], k + 1)
                    gp.tensor_tensor(yl[:, 4 * b + pr, :], group_out[:, b, pr, :], yh[:, 4 * b + pr, :].bitcast(F32), ALU.subtract).then_inc(s["y_lo"], 1)
            for f in range(4):
                pool.wait_ge(s["merge_hi"], f + 1)
                gp.tensor_tensor(merge_l[:, 2 * f:2 * f + 2, :], merge[:, 2, :, :], merge_h[:, 2 * f:2 * f + 2, :].bitcast(F32), ALU.subtract).then_inc(s["merge_lo"], 1)
            for k in range(KT):
                pool.wait_ge(s["x1_hi"], k + 1)
                gp.tensor_tensor(xl[:, k, :], x[:, k, :], xh[:, k, :].bitcast(F32), ALU.subtract).then_inc(xr[k % 2], 1)

        X_SLOT = (0, 1, 3, 5)

        def block1_act(act, round_chunk):
            ac = nc.scalar

            def first_chunk(p):
                act.wait_ge(landed[p], 16)
                ac.activation(wh[:, p, :], raw[:, p, :], ACT.Copy).then_inc(s["chunk_hi"], 1)
            act.wait_ge(s["x_in"], 16)
            for k in range(KT):
                if k >= 4:
                    act.wait_ge(s["ms_x"], k - 3)
                ac.activation(bsq[:, X_SLOT[k % 4], :], x[:, k, :], ACT.Square).then_inc(s["sq_x"], 1)
            first_chunk(0)
            act.wait_ge(s["ms_x"], KT)
            act.wait_ge(s["columns_set"], 4)
            ac.activation(bsq[:, 2, :], ps[:, 5, :], ACT.Sqrt, bias=eps_col("eps_l2")).then_inc(s["rms_x"], 1)
            first_chunk(1)
            for k in range(KT):
                act.wait_ge(s["h_tile"], k + 1)
                ac.activation(xh[:, k, :], h_new[:, k % 4, :], ACT.Copy).then_inc(s["h_tile_hi"], 1)
            n = tile = u = 0
            for g in ORDER:
                for kind in KINDS[g]:
                    p = n % 2
                    act.wait_ge(s["chunk_used"], n + 1)
                    if kind[0] != "v":
                        for t in range(2):
                            if tile + t >= 2:
                                act.wait_ge(s["qk_ms"], tile + t - 1)
                            ac.activation(bsq[:, (tile + t) % 2, :], ps[:, 2 * p + t, :], ACT.Square).then_inc(s["qk_square"], 1)
                    round_chunk(n + 2, p)
                    if kind[0] != "v":
                        for t in range(2):
                            m = tile + t
                            act.wait_ge(s["qk_ms"], m + 1)
                            if m >= 2:
                                act.wait_ge(s["qk_rstd"], m - 1)
                            ac.activation(bsq[:, 2 + m % 2, :], ps[:, 6 + m % 2, :], ACT.Sqrt, bias=eps_col("eps_l2")).then_inc(s["qk_std"], 1)
                        tile += 2
                    n += 1
                act.wait_ge(s["bias_dram"], 64)
                for h in range(8):
                    for i in range(4):
                        w = P * len(key_tiles(g, i))
                        c = i * 8 + h
                        act.wait_ge(s["att_logits"], u + 1)
                        if u >= 3:
                            act.wait_ge(s["att_probs_t"], u - 2)
                        ac.activation(probs[:, u % 3, 0:w], logits[:, u % 2, 0:w], ACT.Exp, scale=-1.0, bias=neg_max[:, g, c:c + 1],
                                      accum_out=prob_sum[:, g, c:c + 1]).then_inc(s["att_probs"], 1)
                        u += 1
                        if h >= 2 and h % 2 == 0 and i == 3:
                            out_pair(act, g, u - 4, h // 2 - 1)
                out_pair(act, g, u, 3)
            act.wait_ge(s["stat_ps"], 8)
            for g in range(4):
                ac.activation(view(stat_rows[0:8, g, :], VIEW[g]), own(ps[0:8, g, :], VIEW[g]), ACT.Copy).then_inc(s["stat_max"], 1)
            act.wait_ge(s["stat_sum"], 4 + 5)
            ac.activation(stat_rows[0:8, 9:12, :], stat_rows[0:8, 9:12, :], ACT.Exp).then_inc(s["stat_exp"], 1)
            ac.activation(stat_rows[0:8, 8, :], stat_rows[0:8, 8, :], ACT.Exp).then_inc(s["stat_exp"], 1)
            ac.activation(shared[0:8, 0, :], shared[0:8, 0, :], ACT.Exp, bias=params1[0:8, P1_SINK:P1_SINK + 1]).then_inc(s["stat_exp"], 1)
            for half in range(2):
                for b in range(2):
                    p = n % 2
                    act.wait_ge(s["chunk_used"], n + 1)
                    if half:
                        act.wait_ge(s["y_gated"], 4)
                    ac.activation(zg[:, 2 * b:2 * b + 2, :], ps[:, 2 * p:2 * p + 2, :], ACT.Silu).then_inc(evac[p], 1)
                    round_chunk(n + 2, p)
                    n += 1
                for pr in (2 * half, 2 * half + 1):
                    for b in range(2):
                        act.wait_ge(s["y_gated"], 2 * pr + b + 1)
                        ac.activation(yh[:, 4 * b + pr, :], group_out[:, b, pr, :], ACT.Copy).then_inc(s["y_hi"], 1)
            for f in range(4):
                for b in range(3):
                    p = n % 2
                    act.wait_ge(s["chunk_used"], n + 1)
                    if b < 2:
                        if f and b == 0:
                            act.wait_ge(s["merge_step"], 2 * f)
                        for t in range(2):
                            c = P1_BM + 8 * b + 2 * f + t
                            ac.activation(merge[:, b, t, :], ps[:, 2 * p + t, :], ACT.Sigmoid, bias=params1[:, c:c + 1]).then_inc(
                                *((s["merge_gate"], 1) if t == 0 else (evac[p], 1)))
                    round_chunk(n + 2, p)
                    n += 1
                act.wait_ge(s["merge_step"], 2 * f + 2)
                ac.activation(merge_h[:, 2 * f:2 * f + 2, :], merge[:, 2, :, :], ACT.Copy).then_inc(s["merge_hi"], 1)
            for j in range(4):
                p = n % 2
                act.wait_ge(evac[p], n // 2 + 1)
                for t in range(2):
                    k = 2 * j + t
                    ac.activation(xh[:, k, :], x[:, k, :], ACT.Copy).then_inc(s["x1_hi"], 1)
                round_chunk(n + 2, p)
                n += 1

        def out_pair(act, g, u, pr):
            act.wait_ge(s["att_values"], u)
            nc.scalar.activation(view(group_out[:, g, pr, :], VIEW[g]), own(ps[:, pr % 2, :], VIEW[g]), ACT.Copy).then_inc(s["att_out"], 1)

        def block1_dve(dve, rest_chunk):
            ve = nc.vector
            rest_chunk(0, 0)
            dve.wait_ge(s["first_params_in"], 16)
            ve.tensor_scalar(cols[:, 3:4], params1[:, P1_QN:P1_QN + 1], -0.125, None, ALU.mult).then_inc(s["columns_negated"], 1)
            ve.tensor_scalar(cols[:, 4:5], params1[:, P1_QN + 2:P1_QN + 3], -0.125, None, ALU.mult).then_inc(s["columns_negated"], 1)
            ve.tensor_scalar(cols[:, 5:6], params1[:, P1_SINK:P1_SINK + 1], -1.0, None, ALU.mult).then_inc(s["columns_negated"], 1)
            dve.wait_ge(s["rms_x"], 1)
            ve.reciprocal(bsq[:, 4, :], bsq[:, 2, :]).then_inc(s["rrms_x"], 1)
            dve.wait_ge(s["rrms_x"], 1)
            for k in range(KT):
                if k >= 4:
                    dve.wait_ge(s["h_tile_lo"], k - 3)
                ve.scalar_tensor_tensor(out=h_new[:, k % 4, :], in0=x[:, k, :], scalar=params1[:, k:k + 1], in1=bsq[:, 4, :], op0=ALU.mult, op1=ALU.mult).then_inc(s["h_tile"], 1)
            rest_chunk(1, 1)
            dve.wait_ge(s["bias_ps"], 1)
            for o in range(2):
                ve.scalar_tensor_tensor(out=bias_rows[0:16, o, :], in0=ps[0:16, 4 + 2 * o, :], scalar=-1.0, in1=bias_cst[0:16, 1024 + 512 * o:1536 + 512 * o],
                                        op0=ALU.mult, op1=ALU.add).then_inc(s["bias_row"], 1)
            n = tile = u = 0
            for gi, g in enumerate(ORDER):
                if gi:
                    dve.wait_ge(s["att_out"], 4 * gi)
                for kind in KINDS[g]:
                    p = n % 2
                    if kind[0] == "v":
                        dve.wait_ge(s["chunk_used"], n + 1)
                        w = VW[g]
                        v0 = w * int(kind[1])
                        src = ps[:, 2 * p:2 * p + 2, 0:2 * w].rearrange("p a (b c) -> p a b c", b=2)
                        dst = vg[:, :, v0:v0 + w].rearrange("p (a b) c -> p a b c", b=2)
                        ve.tensor_copy(dst, src).then_inc(evac[p], 1)
                    else:
                        for t in range(2):
                            m = tile + t
                            dve.wait_ge(s["qk_std"], m + 1)
                            ve.reciprocal(bsq[:, 4 + m % 2, :], bsq[:, 2 + m % 2, :]).then_inc(s["qk_rstd"], 1)
                            dve.wait_ge(s["qk_rstd"], m + 1)
                            dst = (qg if kind[0] == "q" else kg)[:, 2 * int(kind[1]) + t, :]
                            if kind[0] == "q":
                                f = cols[:, 3:4] if g == 0 else cols[:, 4:5]
                            else:
                                f = params1[:, P1_QN + 1:P1_QN + 2] if g == 0 else params1[:, P1_QN + 3:P1_QN + 4]
                            if t:
                                dve.wait_ge(s["qk_first"], m // 2 + 1)
                            ve.scalar_tensor_tensor(out=own(dst, VIEW[g]), in0=view(ps[:, 2 * p + t, :], VIEW[g]), scalar=f, in1=view(bsq[:, 4 + m % 2, :], VIEW[g]),
                                                    op0=ALU.mult, op1=ALU.mult).then_inc(evac[p] if t else s["qk_first"], 1)
                        dve.wait_ge(evac[p], n // 2 + 1)
                        tile += 2
                    n += 1
                if gi == 0:
                    dve.wait_ge(s["bias_wide"], 16)
                if gi == 1:
                    dve.wait_ge(s["bias_near"], 16)
                if gi == 2:
                    dve.wait_ge(s["bias_wide"], 32)
                if gi == 3:
                    dve.wait_ge(s["bias_far"], 16)
                base_u = u
                for m in range(32 + 2):
                    if m < 32:
                        h, i = m // 4, m % 4
                        w = P * len(key_tiles(g, i))
                        c = i * 8 + h
                        dve.wait_ge(s["att_scores"], u + 1)
                        if u >= 2:
                            dve.wait_ge(s["att_probs"], u - 1)
                        ve.tensor_tensor_reduce(out=logits[:, u % 2, 0:w], in0=ps[:, 4 + u % 2, 0:w], in1=bias_of(g, h, i), scale=1.0, scalar=3e38,
                                                op0=ALU.add, op1=ALU.min, accum_out=neg_max[:, g, c:c + 1]).then_inc(s["att_logits"], 1)
                        u += 1
                    if m >= 2:
                        v = base_u + m - 2
                        i = (m - 2) % 4
                        w = P * len(key_tiles(g, i))
                        dve.wait_ge(s["att_probs_t"], v + 1)
                        if v >= 2:
                            dve.wait_ge(s["att_values"], v - 1)
                        ve.tensor_copy(probs_t[:, v % 2, 0:w], ps[:, 6 + v % 2, 0:w]).then_inc(s["att_probs_sb"], 1)
            dve.wait_ge(s["stat_ps"], 8)
            for g in range(4):
                ve.tensor_copy(view(stat_rows[0:8, 4 + g, :], VIEW[g]), own(ps[0:8, 4 + g, :], VIEW[g])).then_inc(s["stat_sum"], 1)
            dve.wait_ge(s["stat_max"], 4)
            ve.tensor_scalar(shared[0:8, 0, :], stat_rows[0:8, 0, :], cols[0:8, 5:6], None, ALU.min).then_inc(s["stat_sum"], 1)
            ve.tensor_tensor(shared[0:8, 1, :], stat_rows[0:8, 1, :], stat_rows[0:8, 2, :], ALU.min).then_inc(s["stat_sum"], 1)
            dve.wait_ge(s["stat_sum"], 6)
            ve.tensor_tensor(shared[0:8, 1, :], shared[0:8, 1, :], stat_rows[0:8, 3, :], ALU.min).then_inc(s["stat_sum"], 1)
            ve.tensor_tensor(stat_rows[0:8, 8, :], shared[0:8, 0, :], stat_rows[0:8, 0, :], ALU.subtract).then_inc(s["stat_sum"], 1)
            dve.wait_ge(s["stat_sum"], 7)
            ve.tensor_tensor(stat_rows[0:8, 9:12, :], shared[0:8, 1, :].unsqueeze(1).to_broadcast([8, 3, TOK]), stat_rows[0:8, 1:4, :], ALU.subtract).then_inc(s["stat_sum"], 1)
            dve.wait_ge(s["stat_exp"], 3)
            ve.tensor_tensor(stat_rows[0:8, 4:8, :], stat_rows[0:8, 4:8, :], stat_rows[0:8, 8:12, :], ALU.mult).then_inc(s["stat_factor"], 1)
            dve.wait_ge(s["stat_factor"], 1)
            ve.tensor_tensor(shared[0:8, 0, :], shared[0:8, 0, :], stat_rows[0:8, 4, :], ALU.add).then_inc(s["stat_factor"], 1)
            ve.tensor_tensor(shared[0:8, 1, :], stat_rows[0:8, 5, :], stat_rows[0:8, 6, :], ALU.add).then_inc(s["stat_factor"], 1)
            dve.wait_ge(s["stat_factor"], 3)
            ve.tensor_tensor(shared[0:8, 1, :], shared[0:8, 1, :], stat_rows[0:8, 7, :], ALU.add).then_inc(s["stat_factor"], 1)
            dve.wait_ge(s["stat_factor"], 4)
            ve.reciprocal(shared[0:8, :, :], shared[0:8, :, :]).then_inc(s["stat_factor"], 1)
            dve.wait_ge(s["stat_factor"], 5)
            ve.tensor_tensor(stat_rows[0:8, 8, :], stat_rows[0:8, 8, :], shared[0:8, 0, :], ALU.mult).then_inc(s["stat_factor"], 1)
            ve.tensor_tensor(stat_rows[0:8, 9:12, :], stat_rows[0:8, 9:12, :], shared[0:8, 1, :].unsqueeze(1).to_broadcast([8, 3, TOK]), ALU.mult).then_inc(s["stat_factor"], 1)
            dve.wait_ge(s["chunk_lo"], n + 2)
            for half in range(2):
                rest_chunk(n + 2, 0)
                for pr in (2 * half, 2 * half + 1):
                    dve.wait_ge(s["y_factor"], pr + 1)
                    for g in range(4):
                        ve.tensor_tensor(group_out[:, g, pr, :], group_out[:, g, pr, :], ps[:, 4 + g, :], ALU.mult).then_inc(s["y_weighted"], 1)
                    if pr % 2 == 0:
                        rest_chunk(n + 3, 1)
                    for b in range(2):
                        dve.wait_ge(evac[b], (n + b) // 2 + 1)
                        dve.wait_ge(s["y_weighted"], 4 * pr + 4)
                        if b:
                            dve.wait_ge(s["y_sum"], 2 * pr + 2)
                        ve.tensor_tensor(group_out[:, b, pr, :], group_out[:, b, pr, :], zg[:, 2 * b + pr % 2, :], ALU.mult).then_inc(s["y_gated"], 1)
                n += 2
            for f in range(4):
                for b in range(3):
                    p = n % 2
                    if b == 2:
                        dve.wait_ge(s["chunk_used"], n + 1)
                        dve.wait_ge(evac[1 - p], (n - 1) // 2 + 1)
                        dve.wait_ge(evac[p], n // 2)
                        if f:
                            dve.wait_ge(s["merge_lo"], f)
                        ve.tensor_tensor(merge[:, 2, :, :], merge[:, 0, :, :], ps[:, 2 * p:2 * p + 2, :], ALU.mult).then_inc(evac[p], 1)
                        ve.tensor_tensor(merge[:, 1, :, :], merge[:, 1, :, :], ps[:, 4 + 2 * (f % 2):6 + 2 * (f % 2), :], ALU.mult).then_inc(s["merge_step"], 1)
                        dve.wait_ge(s["merge_step"], 2 * f + 1)
                        dve.wait_ge(evac[p], n // 2 + 1)
                        ve.tensor_tensor(merge[:, 2, :, :], merge[:, 2, :, :], merge[:, 1, :, :], ALU.add).then_inc(s["merge_step"], 1)
                        dve.wait_ge(s["merge_step"], 2 * f + 2)
                    rest_chunk(n + 2, p)
                    n += 1
            for j in range(4):
                p = n % 2
                dve.wait_ge(s["chunk_used"], n + 1)
                ve.tensor_tensor(x[:, 2 * j:2 * j + 2, :], x[:, 2 * j:2 * j + 2, :], ps[:, 2 * p:2 * p + 2, :], ALU.add).then_inc(evac[p], 1)
                rest_chunk(n + 2, p)
                n += 1

        def block1_pe(pe):
            te = nc.tensor
            pe.wait_ge(s["mean_matrix_set"], 1)
            for k in range(KT):
                pe.wait_ge(s["sq_x"], k + 1)
                te.matmul(ps[:, 5, :], mean_matrix[:, :], bsq[:, X_SLOT[k % 4], :], start=(k == 0), stop=(k == KT - 1)).then_inc(s["ms_x"], 1)
            pe.wait_ge(s["rel_in"], 16)
            pe.wait_ge(s["consts_in"], 16)
            pe.wait_ge(s["bias_consts_in"], 16)
            for o in range(2):
                mm = te.matmul(ps[0:16, 4 + 2 * o, :], rel_table[0:32, 16 * o:16 * o + 16], bias_cst[0:32, 512 * o:512 * o + 512], start=True, stop=True)
            mm.then_inc(s["bias_ps"], 1)
            n = tile = u = 0
            pending = []

            def head_means():
                for m in pending:
                    pe.wait_ge(s["qk_square"], m + 1)
                    if m >= 2:
                        pe.wait_ge(s["qk_std"], m - 1)
                    te.matmul(ps[:, 6 + m % 2, :], C("head_mean"), bsq[:, m % 2, :], start=True, stop=True).then_inc(s["qk_ms"], 1)
                pending.clear()

            def begin(n):
                pe.wait_ge(s["chunk_lo"], n + 1)
                if n >= 2:
                    pe.wait_ge(evac[n % 2], n // 2)

            def features(n, kk, rh, rl, dst, w0, width, block, between=None):
                p = n % 2
                steps = [(w, r, k) for k in range(kk) for w, r in ((wh, rh), (wh, rl), (wl, rh))]
                for m, (w, r, k) in enumerate(steps):
                    mm = te.matmul(dst, w[:, p, w0 + k * block:w0 + k * block + P], r(k), start=(m == 0), stop=(m == len(steps) - 1))
                    if m == 8 and between:
                        between()
                return mm

            def h_first():
                begin(0)
                for k in range(KT):
                    pe.wait_ge(s["h_tile_lo"], k + 1)
                    for t in range(2):
                        for a, (w, r) in enumerate(((wh, xh), (wh, xl), (wl, xh))):
                            mm = te.matmul(ps[:, t, :], w[:, 0, 256 * k + P * t:256 * k + P * t + P], r[:, k, :], start=(k == 0 and a == 0), stop=(k == KT - 1 and a == 2))
                mm.then_inc(s["chunk_used"], 1)
                pe.wait_ge(s["bias_row"], 2)

            def h_chunk(n):
                begin(n)
                for t in range(2):
                    mm = features(n, KT, lambda k: xh[:, k, :], lambda k: xl[:, k, :], ps[:, 2 * (n % 2) + t, :], t * P, P, 256,
                                  None if t else head_means)
                mm.then_inc(s["chunk_used"], 1)

            def tokens(v, r, t):
                if r == 1:
                    return v[:, t * P:(t + 1) * P]
                return view(v, r)[:, t, :]

            for gi, g in enumerate(ORDER):
                for kind in KINDS[g]:
                    if kind[0] != "v":
                        h_chunk(n) if n else h_first()
                        pending += [tile, tile + 1]
                        tile += 2
                    else:
                        begin(n)
                        w, p = VW[g], n % 2
                        for t in range(4):
                            dst = ps[:, 2 * p + t // 2, w * (t % 2):w * (t % 2) + w]
                            steps = [(a, b, k) for k in range(KT) for a, b in ((xh, wh), (xl, wh), (xh, wl))]
                            for m, (a, b, k) in enumerate(steps):
                                mm = te.matmul(dst, tokens(a[:, k, :], VIEW[g], t), b[:, p, k * w:(k + 1) * w], start=(m == 0), stop=(m == len(steps) - 1))
                            if t == 0:
                                head_means()
                        mm.then_inc(s["chunk_used"], 1)
                    n += 1
                pe.wait_ge(s["qk_first"], tile // 2)
                for p in range(2):
                    pe.wait_ge(evac[p], (n + 1 - p) // 2)
                base_u = u
                for m in range(32 + 3):
                    if m < 32:
                        h, i = m // 4, m % 4
                        js = key_tiles(g, i)
                        b = 64 * (h % 2)
                        kt_ = kg[b:b + 64, h // 4 if g == 0 else h // 2, js[0] * P:(js[-1] + 1) * P]
                        if u >= 2:
                            pe.wait_ge(s["att_logits"], u - 1)
                        te.matmul(ps[:, 4 + u % 2, 0:P * len(js)], qg[b:b + 64, h // 2, i * P:(i + 1) * P], kt_, start=True, stop=True).then_inc(s["att_scores"], 1)
                        u += 1
                    if 2 <= m < 34:
                        v = base_u + m - 2
                        i = (m - 2) % 4
                        pe.wait_ge(s["att_probs"], v + 1)
                        if v >= 2:
                            pe.wait_ge(s["att_probs_sb"], v - 1)
                        for a in range(len(key_tiles(g, i))):
                            mm = te.transpose(ps[:, 6 + v % 2, a * P:(a + 1) * P], probs[:, v % 3, a * P:(a + 1) * P], C("ident"))
                        mm.then_inc(s["att_probs_t"], 1)
                    if m >= 3:
                        v = base_u + m - 3
                        h, i = (m - 3) // 4, (m - 3) % 4
                        pe.wait_ge(s["att_probs_sb"], v + 1)
                        if h % 2 == 0 and i == 0 and h >= 4:
                            pe.wait_ge(s["att_out"], 4 * gi + h // 2 - 1)
                        js = key_tiles(g, i)
                        hv = h // 4 if g == 0 else h
                        b = 64 * (h % 2)
                        for a, j in enumerate(js):
                            mm = te.matmul(ps[b:b + 64, (h // 2) % 2, i * P:(i + 1) * P], vg[:, j, 64 * hv:64 * hv + 64], probs_t[:, v % 2, a * P:(a + 1) * P],
                                           start=(a == 0), stop=(a == len(js) - 1))
                        mm.then_inc(s["att_values"], 1)
                pe.wait_ge(s["att_out"], 4 * gi + 4)
            for kind, src in ((0, neg_max), (1, prob_sum)):
                for g in range(4):
                    for i in range(4):
                        mm = te.transpose(ps[0:8, 4 * kind + g, i * P:(i + 1) * P], src[:, g, 8 * i:8 * i + 8], C("ident"))
                    mm.then_inc(s["stat_ps"], 1)
            pe.wait_ge(s["stat_max"], 4)
            pe.wait_ge(s["stat_sum"], 4)
            for half in range(2):
                for b in range(2):
                    h_chunk(n)
                    n += 1
                pe.wait_ge(s["stat_factor"], 7)
                for pr in (2 * half, 2 * half + 1):
                    if pr:
                        pe.wait_ge(s["y_weighted"], 4 * pr)
                    for g in range(4):
                        mm = te.matmul(ps[:, 4 + g, :], sel[0:8, pr, :], stat_rows[0:8, 8 + g, :], start=True, stop=True)
                    mm.then_inc(s["y_factor"], 1)
            for f in range(4):
                h_chunk(n)
                h_chunk(n + 1)
                begin(n + 2)
                p = n % 2
                if f == 0:
                    pe.wait_ge(s["y_lo"], 8)
                if f >= 2:
                    pe.wait_ge(s["merge_step"], 2 * f - 2)
                for b in range(2):
                    for t in range(2):
                        dst = ps[:, (2 * p if b == 0 else 4 + 2 * (f % 2)) + t, :]
                        mm = features(n + 2, 4, lambda k: yh[:, 4 * b + k, :], lambda k: yl[:, 4 * b + k, :], dst, 1024 * b + t * P, P, 256)
                mm.then_inc(s["chunk_used"], 1)
                n += 3
            for j in range(4):
                begin(n)
                if j == 0:
                    for k in range(KT):
                        if k % 2 == 0:
                            pe.wait_ge(s["merge_lo"], k // 2 + 1)
                        for t in range(2):
                            c = 256 * k + P * t
                            for a, (w, r) in enumerate(((wh, merge_h), (wh, merge_l), (wl, merge_h))):
                                mm = te.matmul(ps[:, 2 * (n % 2) + t, :], w[:, n % 2, c:c + P], r[:, k, :], start=(k == 0 and a == 0), stop=(k == KT - 1 and a == 2))
                else:
                    for t in range(2):
                        mm = features(n, KT, lambda k: merge_h[:, k, :], lambda k: merge_l[:, k, :], ps[:, 2 * (n % 2) + t, :], t * P, P, 256)
                mm.then_inc(s["chunk_used"], 1)
                n += 1

        @block.sync
        def _(sp):
            sp.dma_start(x[:, :, :], x_in).then_inc(s["x_in"], 16)
            sp.dma_start(raw[:, 0, :], stream[0]).then_inc(landed[0], 16)
            sp.dma_start(const[:, :], consts).then_inc(s["consts_in"], 16)
            sp.dma_start(raw[:, 1, :], stream[1]).then_inc(landed[1], 16)
            sp.dma_start(bias_cst[:, :], bias_consts).then_inc(s["bias_consts_in"], 16)
            with sp.Fori(1, N_CHUNKS // 2) as i:
                for p in range(2):
                    sp.wait_ge(s["chunk_lo"], i * 2 + p - 1)
                    sp.dma_start(raw[:, p, :], stream[bass.ds(i * 2 + p, 1)].rearrange("a p n -> (a p) n")).then_inc(landed[p], 16)

            for m in range(4):
                k = 4 * (m % 2) + m // 2
                sp.wait_ge(s["ln_x"], 24 * LAYERS - KT + 2 * m + 2)
                sp.dma_start(out[:, k:k + 3:2, :], x[:, k:k + 3:2, :]).then_inc(s["stored"], 16)
            sp.wait_ge(s["stored"], 4 * 16)

        @block.gpsimd
        def _(pool):
            gp = nc.gpsimd

            def hidden_rest(l, w, i):
                n = l * 22 + w * 11 + i + 1
                pool.wait_ge(s["hidden_hi"], n)
                gp.tensor_tensor(hl[:, bass.ds(i * 2, 2), :], hidden[:, :, :], hh[:, bass.ds(i * 2, 2), :].bitcast(F32), ALU.subtract).then_inc(s["hidden_lo"], 1)

            def down_rests(l, off):
                with pool.Fori(0, KT) as f:
                    for p in range(2):
                        rest(pool, c_no(l, off) + f * 2 + p + 2, p)

            def norm_rest(l, w):
                for k in range(0, KT, 2):
                    pool.wait_ge(s["ln_hi"], l * 24 + w * 8 + k + 1)
                    pool.wait_ge(s["ln_x"], l * 24 + w * 8 + k // 2 + 1)
                    gp.tensor_tensor(xl[:, k, :], x[:, k, :], xh[:, k, :].bitcast(F32), ALU.subtract).then_inc(xr[0], 1)

            block1_pool(pool)
            pool.sem_inc(s["hidden_lo"], 1)
            with pool.Fori(0, LAYERS) as l:
                for r in range(2):
                    pool.wait_ge(xr[r], l * 12 + 4)
                pool.dma_start(params[:, :], pk[bass.ds(l, 1)].rearrange("a p n -> (a p) n")).then_inc(s["layer_params_in"], 16)
                with pool.Fori(0, UP // 2) as i:
                    hidden_rest(l, 0, i)
                down_rests(l, OFF_DN1)
                norm_rest(l, 0)
                pool.dma_start(sgp[:, :], sg[bass.ds(l, 1)].rearrange("a p n -> (a p) n")).then_inc(s["spatial_params_in"], 16)
                mixer_pool(l, pool)
                for j in range(OUTP):
                    rest(pool, c_no(l, OFF_OUT) + j + 2, j % 2)
                norm_rest(l, 1)
                with pool.Fori(0, UP // 2) as i:
                    hidden_rest(l, 1, i)
                down_rests(l, OFF_DN2)
                norm_rest(l, 2)
                pool.wait_ge(s["ln_x"], l * 24 + 24)

        @block.scalar
        def _(act):
            ac = nc.scalar

            def round_chunk(n, p):
                act.wait_ge(landed[p], (n - p) * 8 + 16)
                act.wait_ge(s["chunk_used"], n - 1)
                ac.activation(wh[:, p, :], raw[:, p, :], ACT.Copy).then_inc(s["chunk_hi"], 1)

            def up(l, w, i, off):
                n = c_no(l, off) + i * 2
                act.wait_ge(s["chunk_used"], n + 1)
                act.wait_ge(evac[1], n_evac(l, 1, off) + i)
                ac.activation(silu_t[:, :, :], ps[:, 0:2, :], ACT.Silu).then_inc(evac[0], 1)
                round_chunk(n + 2, 0)
                act.wait_ge(evac[1], n_evac(l, 1, off) + i + 1)
                ac.activation(hh[:, bass.ds(i * 2, 2), :], hidden[:, :, :], ACT.Copy).then_inc(s["hidden_hi"], 1)
                round_chunk(n + 3, 1)

            def norm(l, w):
                for k in range(KT):
                    act.wait_ge(s["ln_centred"], l * 24 + w * 8 + k + 1)
                    if k >= 4:
                        act.wait_ge(s["ln_var"], l * 24 + w * 8 + k - 3)
                    ac.activation(sq[:, k % 4, :], x[:, k, :], ACT.Square).then_inc(s["ln_square"], 1)
                act.wait_ge(s["ln_var"], l * 24 + w * 8 + 8)
                ac.activation(std[:, :], ps[:, 5, :], ACT.Sqrt, bias=eps_col("eps_ln")).then_inc(s["ln_std"], 1)
                c = PK_LN + 16 * w + 8
                for k in range(KT):
                    act.wait_ge(s["ln_scaled"], l * 24 + w * 8 + k + 1)
                    ac.activation(xh[:, k, :], zn[:, k, :], ACT.Identity, bias=params[:, c + k:c + k + 1]).then_inc(s["ln_hi"], 1)
                    if k % 2 == 0:
                        ac.activation(x[:, k, :], zn[:, k, :], ACT.Identity, bias=params[:, c + k:c + k + 1]).then_inc(s["ln_x"], 1)
                for k in range(1, KT, 2):
                    ac.activation(x[:, k, :], zn[:, k, :], ACT.Identity, bias=params[:, c + k:c + k + 1]).then_inc(s["ln_x"], 1)
                act.wait_ge(s["ln_x"], l * 24 + w * 8 + 8)

            act.wait_ge(s["consts_in"], 16)
            block1_act(act, round_chunk)
            with act.Fori(0, LAYERS) as l:
                act.wait_ge(s["layer_params_in"], l * 16 + 16)
                with act.Fori(0, UP // 2) as i:
                    up(l, 0, i, OFF_UP1)
                with act.Fori(0, KT) as f:
                    for p in range(2):
                        round_chunk(c_no(l, OFF_DN1) + f * 2 + p + 2, p)
                norm(l, 0)
                in_products_act(l, act, round_chunk)
                mixer_act(l, act)
                for j in range(OUTP):
                    round_chunk(c_no(l, OFF_OUT) + j + 2, j % 2)
                norm(l, 1)
                with act.Fori(0, UP // 2) as i:
                    up(l, 1, i, OFF_UP2)
                with act.Fori(0, KT) as f:
                    for p in range(2):
                        round_chunk(c_no(l, OFF_DN2) + f * 2 + p + 2, p)
                norm(l, 2)

        @block.vector
        def _(dve):
            ve = nc.vector

            def rest_chunk(n, p):
                dve.wait_ge(s["chunk_hi"], n + 1)
                ve.tensor_tensor(wl[:, p, :], raw[:, p, :], wh[:, p, :].bitcast(F32), ALU.subtract).then_inc(s["chunk_lo"], 1)

            def up(l, w, i, off):
                n = c_no(l, off) + i * 2
                rest_chunk(n + 2, 0)
                dve.wait_ge(s["chunk_used"], n + 2)
                dve.wait_ge(evac[0], n_evac(l, 0, off) + i + 1)
                dve.wait_ge(s["hidden_lo"], l * 22 + w * 11 + i + 1)
                ve.tensor_tensor(hidden[:, :, :], ps[:, 2:4, :], silu_t[:, :, :], ALU.mult).then_inc(evac[1], 1)
                rest_chunk(n + 3, 1)

            def down(l, w, i, off):
                for q in range(2):
                    f = i * 2 + q
                    n = c_no(l, off) + i * 4 + q * 2
                    dve.wait_ge(s["chunk_used"], n + 2)
                    xf = x[:, bass.ds(f, 1), :].rearrange("p a t -> p (a t)")
                    ve.scalar_tensor_tensor(out=xf, in0=ps[:, 2 * q, :], scalar=0.5 / ALPHA, in1=xf, op0=ALU.mult, op1=ALU.add).then_inc(evac[1], 1)
                    dve.wait_ge(evac[1], n_evac(l, 1, off) + f + 1)
                    dve.wait_ge(s["z_sum"], l * 27 + w * 9 + f + 1)
                    ve.tensor_tensor(zacc[:, :], zacc[:, :], xf, ALU.add).then_inc(s["z_sum"], 1)

            def norm(l, w):
                dve.wait_ge(s["ln_mean"], l * 3 + w + 1)
                for k in range(KT):
                    ve.tensor_tensor(x[:, k, :], x[:, k, :], ps[:, 4, :], ALU.subtract).then_inc(s["ln_centred"], 1)
                dve.wait_ge(s["ln_std"], l * 3 + w + 1)
                ve.reciprocal(rstd[:, :], std[:, :]).then_inc(s["ln_rstd"], 1)
                dve.wait_ge(s["ln_rstd"], l * 3 + w + 1)
                for k in range(KT + 3):
                    if k < KT:
                        c = PK_LN + 16 * w + k
                        ve.scalar_tensor_tensor(out=zn[:, k, :], in0=x[:, k, :], scalar=params[:, c:c + 1], in1=rstd[:, :], op0=ALU.mult, op1=ALU.mult).then_inc(s["ln_scaled"], 1)
                    j = k - 2
                    if j > 0 and j % 2:
                        dve.wait_ge(s["ln_hi"], l * 24 + w * 8 + j + 1)
                        dve.wait_ge(s["ln_scaled"], l * 24 + w * 8 + j + 1)
                        c = PK_LN + 16 * w + 8 + j
                        ve.scalar_tensor_tensor(out=xl[:, j, :], in0=zn[:, j, :], scalar=params[:, c:c + 1], in1=xh[:, j, :].bitcast(F32),
                                                op0=ALU.add, op1=ALU.subtract).then_inc(xr[1], 1)

            dve.memset(mean_matrix[:, :], 1.0 / D).then_inc(s["mean_matrix_set"], 1)
            dve.memset(cols[:, 0:1], EPS2 / ALPHA ** 2).then_inc(s["columns_set"], 1)
            dve.memset(cols[:, 1:2], EPS2).then_inc(s["columns_set"], 1)
            dve.memset(cols[:, 2:3], EPS_L2).then_inc(s["columns_set"], 1)
            dve.memset(exp_a[:, :], 0.0).then_inc(s["columns_set"], 1)
            dve.wait_ge(s["columns_set"], 4)
            dve.sem_inc(s["level_t"], 8)
            block1_dve(dve, rest_chunk)
            with dve.Fori(0, LAYERS) as l:
                dve.wait_ge(s["chunk_lo"], c_no(l, OFF_UP1) + 2)
                dve.sem_inc(s["apart_dve"], 1)
                with dve.Fori(0, UP // 2) as i:
                    up(l, 0, i, OFF_UP1)
                dve.wait_ge(evac[1], n_evac(l, 1, OFF_DN1))
                ve.memset(zacc[:, :], 0.0).then_inc(s["z_sum"], 1)
                with dve.Fori(0, KT // 2) as i:
                    down(l, 0, i, OFF_DN1)
                norm(l, 0)
                in_products_dve(l, dve, rest_chunk)
                mixer_dve(l, dve)
                dve.wait_ge(s["delta_done"], l * 4 + 4)
                ve.memset(zacc[:, :], 0.0).then_inc(s["z_sum"], 1)
                for j in range(OUTP):
                    n = c_no(l, OFF_OUT) + j
                    p = j % 2
                    dve.wait_ge(s["chunk_used"], n + 1)
                    ve.scalar_tensor_tensor(out=x[:, 2 * j:2 * j + 2, :], in0=ps[:, 2 * p:2 * p + 2, :], scalar=1.0 / ALPHA, in1=x[:, 2 * j:2 * j + 2, :], op0=ALU.mult, op1=ALU.add).then_inc(evac[p], 1)
                    dve.wait_ge(evac[p], n_evac(l, p, OFF_OUT) + j // 2 + 1)
                    for k in range(2):
                        dve.wait_ge(s["z_sum"], l * 27 + 9 + 2 * j + k + 1)
                        ve.tensor_tensor(zacc[:, :], zacc[:, :], x[:, 2 * j + k, :], ALU.add).then_inc(s["z_sum"], 1)
                norm(l, 1)
                dve.wait_ge(s["chunk_lo"], c_no(l, OFF_UP2) + 2)
                dve.sem_inc(s["apart_dve"], 1)
                with dve.Fori(0, UP // 2) as i:
                    up(l, 1, i, OFF_UP2)
                dve.wait_ge(evac[1], n_evac(l, 1, OFF_DN2))
                ve.memset(zacc[:, :], 0.0).then_inc(s["z_sum"], 1)
                with dve.Fori(0, KT // 2) as i:
                    down(l, 2, i, OFF_DN2)
                norm(l, 2)

        @block.tensor
        def _(pe):
            te = nc.tensor

            def accumulate(dst, ks, wslice, rh, rl, start, stop):
                steps = []
                for k in ks:
                    steps += [(wh, rh, k), (wh, rl, k), (wl, rh, k)]
                for m, (w, r, k) in enumerate(steps):
                    mm = te.matmul(dst, wslice(w, k), r(k), start=(start and m == 0), stop=(stop and m == len(steps) - 1))
                return mm

            def chunk_t(l, off, i, p, cols=256, order=range(KT), ready=None):
                n = c_no(l, off) + i
                pe.wait_ge(s["chunk_lo"], n + 1)
                if ready:
                    for m, k in enumerate(order):
                        ready(k)
                        for j in range(cols // P):
                            cs = slice(k * cols + j * P, k * cols + (j + 1) * P)
                            for a, (w, r) in enumerate(((wh, xh), (wh, xl), (wl, xh))):
                                mm = te.matmul(ps[:, 2 * p + j, :], w[:, p, cs], r[:, k, :], start=(m == 0 and a == 0), stop=(m == KT - 1 and a == 2))
                    mm.then_inc(s["chunk_used"], 1)
                    return
                for j in range(cols // P):
                    mm = accumulate(ps[:, 2 * p + j, :], range(KT),
                                    lambda w, k: w[:, p, k * cols + j * P:k * cols + (j + 1) * P],
                                    lambda k: xh[:, k, :], lambda k: xl[:, k, :], True, True)
                mm.then_inc(s["chunk_used"], 1)

            def chunk_n(l, off, i, p):
                n = c_no(l, off) + i
                pe.wait_ge(s["chunk_lo"], n + 1)
                for t in range(4):
                    steps = [(xx, w, k) for k in range(KT) for xx, w in ((xh, wh), (xl, wh), (xh, wl))]
                    dst = ps[:, 2 * p + t // 2, 256 * (t % 2):256 * (t % 2) + 256]
                    for m, (a, w, k) in enumerate(steps):
                        mm = te.matmul(dst, a[:, k, t * P:(t + 1) * P], w[:, p, k * 256:(k + 1) * 256],
                                       start=(m == 0), stop=(m == len(steps) - 1))
                mm.then_inc(s["chunk_used"], 1)

            def up(l, w, i, off, ready=None):
                for p in range(2):
                    pe.wait_ge(evac[p], n_evac(l, p, off) + i)
                    chunk_t(l, off, i * 2 + p, p, ready=None if p else ready)

            def normed(l, w):
                return lambda k: pe.wait_ge(xr[k % 2], l * 12 + w * 4 + k // 2 + 1)

            def down(l, w, i, off):
                for q in range(2):
                    pe.wait_ge(evac[1], n_evac(l, 1, off) + i * 2 + q - 1)
                    for p in range(2):
                        n = c_no(l, off) + i * 4 + q * 2 + p
                        pe.wait_ge(s["chunk_lo"], n + 1)
                        if p and q == 0:
                            pe.wait_ge(s["hidden_lo"], l * 22 + w * 11 + 12)
                        mm = accumulate(ps[:, 2 * q, :], range(11), lambda w_, k: w_[:, p, k * P:(k + 1) * P],
                                        lambda k: hh[:, 11 * p + k, :], lambda k: hl[:, 11 * p + k, :], p == 0, p == 1)
                        mm.then_inc(s["chunk_used"], 1)

            def norm(l, w):
                pe.wait_ge(s["z_sum"], l * 27 + w * 9 + 9)
                te.matmul(ps[:, 4, :], C("feat_mean"), zacc[:, :], start=True, stop=True).then_inc(s["ln_mean"], 1)
                for k in range(KT):
                    pe.wait_ge(s["ln_square"], l * 24 + w * 8 + k + 1)
                    te.matmul(ps[:, 5, :], C("feat_mean"), sq[:, k % 4, :], start=(k == 0), stop=(k == KT - 1)).then_inc(s["ln_var"], 1)

            pe.sem_inc(s["level_x"], 4)
            pe.sem_inc(s["level_tx"], 4)
            block1_pe(pe)
            with pe.Fori(0, LAYERS) as l:
                up(l, 0, 0, OFF_UP1, normed(l, 0))
                with pe.Fori(1, UP // 2) as i:
                    up(l, 0, i, OFF_UP1)
                pe.wait_ge(s["hidden_lo"], l * 22 + 7)
                pe.wait_ge(evac[0], n_evac(l, 0, OFF_DN1))
                pe.sem_inc(s["apart_pe"], 1)
                with pe.Fori(0, KT // 2) as i:
                    down(l, 0, i, OFF_DN1)
                norm(l, 0)
                in_products_pe(l, pe, chunk_t, chunk_n, normed(l, 1))
                mixer_pe(l, pe)
                for j in range(OUTP):
                    pe.wait_ge(evac[j % 2], n_evac(l, j % 2, OFF_OUT) + j // 2)
                    order = (0, 1, 6, 7, 2, 3, 4, 5)
                    chunk_t(l, OFF_OUT, j, j % 2, order=order,
                            ready=None if j else lambda k: pe.wait_ge(s["mixed_lo"], l * 8 + order.index(k) + 1))
                norm(l, 1)
                up(l, 1, 0, OFF_UP2, normed(l, 2))
                with pe.Fori(1, UP // 2) as i:
                    up(l, 1, i, OFF_UP2)
                pe.wait_ge(s["hidden_lo"], l * 22 + 11 + 7)
                pe.wait_ge(evac[0], n_evac(l, 0, OFF_DN2))
                pe.sem_inc(s["apart_pe"], 1)
                with pe.Fori(0, KT // 2) as i:
                    down(l, 1, i, OFF_DN2)
                norm(l, 2)


def blocks(w, cols):
    k, n = w.shape
    return w.reshape(k // P, P, n // cols, cols).transpose(2, 1, 0, 3).reshape(n // cols, P, k // P * cols)


def pad(c):
    out = np.zeros(c.shape[:2] + (2048,), c.dtype)
    out[:, :, :c.shape[2]] = c
    return out


def up_chunks(w1, w3):
    return np.stack([blocks(w1, 256), blocks(w3, 256)], 1).reshape(-1, P, 2048)


def down_chunks(w2):
    b = w2.reshape(2, FT // 2, P, KT, P).transpose(3, 0, 2, 1, 4).reshape(2 * KT, P, FT // 2 * P)
    return pad(b)


def layer_chunks(a, l):
    w = a["w_in_2"][l]
    small = np.zeros((D, P), w.dtype)
    small[:, 64:80] = w[:, 3344:3360]
    small[:, 32:40] = w[:, 2568:2576]
    small[:, 0:8] = w[:, 2560:2568]
    order = [blocks(w[:, c:c + 256], 256) for c in (512, 768, 1024, 1280, 1536, 1792)]
    order += [pad(blocks(small, P))] + [blocks(w[:, c:c + 256], 256) for c in (2576, 2832, 0, 256, 3088, 2048, 2304)]
    return [up_chunks(a["ffn1_w1_2"][l], a["ffn1_w3_2"][l]), down_chunks(a["ffn1_w2_2"][l])] + order + [
        blocks(a["w_out_2"][l], 256), up_chunks(a["ffn2_w1_2"][l], a["ffn2_w3_2"][l]), down_chunks(a["ffn2_w2_2"][l])]


def layer_params(a, l):
    pk = np.zeros((P, NPK), np.float32)
    for w, (g, b) in enumerate((("ln1_g_2", "ln1_b_2"), ("ln2_g_2", "ln2_b_2"), ("ln3_g_2", "ln3_b_2"))):
        pk[:, PK_LN + 16 * w:PK_LN + 16 * w + 8] = a[g][l].reshape(KT, P).T
        pk[:, PK_LN + 16 * w + 8:PK_LN + 16 * w + 16] = a[b][l].reshape(KT, P).T
    pk[:, PK_CONV:PK_CONV + 48] = a["gdn_conv_w_2"][l].reshape(4, 12, P).transpose(2, 1, 0).reshape(P, 48)
    pk[:, PK_GN] = np.concatenate([a["gdn_norm_g_2"][l]] * 2)
    pk[:, PK_LAN] = np.concatenate([a["gla_norm_g_2"][l]] * 2)
    pk[32:40, PK_ALOG] = a["gdn_a_log_2"][l]
    pk[32:40, PK_DT] = a["gdn_dt_bias_2"][l]
    pk[:, PK_GB] = a["gla_gate_b_2"][l]
    pk[64:80, PK_UP:PK_UP + P] = a["gla_gate_up_2"][l]
    sg = np.zeros((P, NSG), np.float32)
    sg[:, SG_G:SG_G + 256] = a["sgu_ln_g_2"][l][None, :]
    sg[:, SG_B:SG_B + 256] = a["sgu_ln_b_2"][l][None, :]
    sg[:, SG_BS:SG_BS + 256] = np.repeat(a["sgu_b_2"][l].reshape(2, 2, P).transpose(1, 0, 2).reshape(2, 256), 64, 0)
    sg[:, SG_W:SG_W + 512] = a["sgu_w_2"][l].transpose(2, 0, 1).reshape(P, 512)
    return pk, sg


def first_chunks(a):
    w = a["w_in"][0]
    qa, ka, va, qb, kb, vb, ga, gb, mg = (w[:, c:c + n] for c, n in (
        (0, 512), (512, 128), (640, 128), (768, 1536), (2304, 1536), (3840, 1536), (5376, 512), (5888, 512), (6400, 2048)))
    k2 = np.concatenate([ka[:, 64 * h:64 * h + 64] for h in (0, 0, 1, 1)], 1)
    out = []
    for g in ORDER:
        if g == 0:
            out += [blocks(qa, 256), blocks(k2, 256), pad(blocks(va, 128))]
        else:
            c = slice(512 * (g - 1), 512 * g)
            out += [blocks(qb[:, c], 256), blocks(kb[:, c], 256), blocks(vb[:, c], 256)]
    for h in range(2):
        c = slice(256 * h, 256 * h + 256)
        out += [blocks(ga[:, c], 256), blocks(gb[:, c], 256)]
    wa, wb = blocks(a["w_branch_a"][0], 256), blocks(a["w_branch_b"][0], 256)
    for f in range(4):
        c = 256 * f
        out += [blocks(mg[:, c:c + 256], 256), blocks(mg[:, D + c:D + c + 256], 256), np.concatenate([wa[f:f + 1], wb[f:f + 1]], 2)]
    return out + [blocks(a["w_out"][0], 256)]


def first_params(a):
    p = np.zeros((P, 32), np.float32)
    p[:, 0:8] = a["norm_gain"][0].reshape(KT, P).T
    for m, name in enumerate(("q_norm_a", "k_norm_a", "q_norm_b", "k_norm_b")):
        p[:, P1_QN + m] = np.concatenate([a[name][0]] * 2)
    p[0:8, P1_SINK] = a["sink_a"][0]
    p[:, P1_BM:P1_BM + 16] = a["b_merge"][0].reshape(16, P).T
    return p


def lay_out(a):
    parts = first_chunks(a)
    for l in range(LAYERS):
        parts += layer_chunks(a, l)
    parts.append(np.zeros((2, P, 2048), np.float32))
    small = [layer_params(a, l) for l in range(LAYERS)]
    return {
        "stream": np.concatenate(parts, 0),
        "pk": np.stack([p for p, _ in small]),
        "sg": np.stack([g for _, g in small]),
        "consts": CONSTS,
        "bias_consts": bias_constants(),
        "rel": np.ascontiguousarray(a["rel_bias"]),
        "p1": first_params(a),
        "x_in": np.ascontiguousarray(a["x"][0].reshape(TOK, KT, P).transpose(2, 1, 0)),
    }


def kernel(**inputs):
    import concourse.bacc as bacc
    from concourse.bass_utils import run_bass_kernel_spmd

    nc = bacc.Bacc("TRN2", target_bir_lowering=False, num_devices=1)
    arrays = lay_out({name: np.asarray(v) for name, v in inputs.items()})
    aps = {name: nc.dram_tensor(name, v.shape, F32, kind="ExternalInput").ap() for name, v in arrays.items()}
    out = nc.dram_tensor("out", (P, KT, TOK), F32, kind="ExternalOutput").ap()
    program(nc, out=out, **aps)
    r = run_bass_kernel_spmd(nc, [arrays], core_ids=[0])
    y = r.results[0]["out"]
    return np.ascontiguousarray(y.transpose(2, 1, 0)).reshape(1, TOK, D)
```
